# Optimizing a Trainium2 kernel written in Bass

```python
import jax, jax.numpy as jnp
from jax import lax
import numpy as np

D_MODEL = 2048
BATCH = 1
SEQ = 256
DEPTH = 1

ATT_HEADS = 16
ATT_KV_HEADS = 2
HEAD_DIM = 64
ATT_WIDTH = ATT_HEADS * HEAD_DIM
KV_WIDTH = ATT_KV_HEADS * HEAD_DIM
GROUP = ATT_HEADS // ATT_KV_HEADS
WINDOW = 128
BLOCK = 128
ROT_DIM = HEAD_DIM // 4
ROPE_THETA = 500000.0
HG_HEADS = 8
HG_EXPAND = 128
HG_HEAD_V = 128
HG_F_WIDTH = HG_HEADS * HG_EXPAND
HG_V_WIDTH = HG_HEADS * HG_HEAD_V
CHUNK = 64
N_LB = DEPTH + 1
FFN_HIDDEN = ((8 * D_MODEL // 3 + 255) // 256) * 256
N_MOD = 6
IN_COLS = ATT_WIDTH + 2 * KV_WIDTH + 2 * HG_F_WIDTH + 2 * HG_V_WIDTH + 2 * D_MODEL
EPS = 1e-6


def rmsnorm(t, gain):
    t32 = t.astype(jnp.float32)
    y = t32 * lax.rsqrt(jnp.mean(t32 * t32, axis=-1, keepdims=True) + EPS)
    return (y * gain.astype(jnp.float32)).astype(t.dtype)

def rope_partial(t, cos, sin):
    half = ROT_DIM // 2
    t1 = t[..., :half].astype(jnp.float32)
    t2 = t[..., half:ROT_DIM].astype(jnp.float32)
    rot = jnp.concatenate([t1 * cos - t2 * sin, t2 * cos + t1 * sin], axis=-1)
    return jnp.concatenate([rot.astype(t.dtype), t[..., ROT_DIM:]], axis=-1)

def sliding_window_attention(q, k, v, sinks):
    B, S = q.shape[0], q.shape[1]
    nb = S // BLOCK
    qb = q.reshape(B, nb, BLOCK, ATT_KV_HEADS, GROUP, HEAD_DIM).astype(jnp.float32)
    kb = k.reshape(B, nb, BLOCK, ATT_KV_HEADS, HEAD_DIM).astype(jnp.float32)
    vb = v.reshape(B, nb, BLOCK, ATT_KV_HEADS, HEAD_DIM).astype(jnp.float32)
    prev = lambda t: jnp.concatenate([jnp.zeros_like(t[:, :1]), t[:, :-1]], axis=1)
    kk = jnp.concatenate([prev(kb), kb], axis=2)
    vv = jnp.concatenate([prev(vb), vb], axis=2)
    logits = jnp.einsum('bnqhgd,bnkhd->bnhgqk', qb, kk) * (HEAD_DIM ** -0.5)
    qi = jnp.arange(BLOCK)[:, None]
    kj = jnp.arange(2 * BLOCK)[None, :]
    rel = BLOCK + qi - kj
    band = (rel >= 0) & (rel < WINDOW)
    has_prev = (jnp.arange(nb) > 0)[:, None, None] | (kj >= BLOCK)[None]
    mask = band[None] & has_prev
    logits = jnp.where(mask[None, :, None, None], logits, -jnp.inf)
    sink = sinks.astype(jnp.float32).reshape(ATT_KV_HEADS, GROUP)[None, None, :, :, None, None]
    m = jnp.maximum(jnp.max(logits, axis=-1, keepdims=True), sink)
    p = jnp.exp(logits - m)
    denom = jnp.sum(p, axis=-1, keepdims=True) + jnp.exp(sink - m)
    out = jnp.einsum('bnhgqk,bnkhd->bnqhgd', p / denom, vv)
    return out.reshape(B, S, ATT_WIDTH).astype(q.dtype)

def hgrn2_recurrence(q, f_raw, i, lb):
    B, S = q.shape[0], q.shape[1]
    nc = S // CHUNK
    f = lb + (1.0 - lb) * jax.nn.sigmoid(f_raw.astype(jnp.float32))
    key = 1.0 - f
    logf = jnp.log(f)

    def chunks(t, d):
        return t.astype(jnp.float32).reshape(B, nc, CHUNK, HG_HEADS, d).transpose(1, 0, 3, 2, 4)

    qc = chunks(jax.nn.silu(q.astype(jnp.float32)), HG_EXPAND)
    kc = chunks(key, HG_EXPAND)
    vc = chunks(i, HG_HEAD_V)
    bc = jnp.cumsum(chunks(logf, HG_EXPAND), axis=3)
    causal = jnp.tril(jnp.ones((CHUNK, CHUNK), dtype=bool))[:, :, None]

    def step(state, xs):
        qt, kt, vt, bt = xs
        o_inter = jnp.einsum('bhck,bhkv->bhcv', qt * jnp.exp(bt), state)
        diff = bt[:, :, :, None, :] - bt[:, :, None, :, :]
        decay = jnp.where(causal, jnp.exp(jnp.where(causal, diff, 0.0)), 0.0)
        scores = jnp.einsum('bhtk,bhtsk,bhsk->bhts', qt, decay, kt)
        o = o_inter + jnp.einsum('bhts,bhsv->bhtv', scores, vt)
        b_last = bt[:, :, -1:, :]
        new_state = (jnp.exp(b_last[:, :, 0, :])[..., None] * state
                     + jnp.einsum('bhsk,bhsv->bhkv', kt * jnp.exp(b_last - bt), vt))
        return new_state, o

    state0 = jnp.zeros((B, HG_HEADS, HG_EXPAND, HG_HEAD_V), jnp.float32)
    _, o = lax.scan(step, state0, (qc, kc, vc, bc))
    return o.transpose(1, 0, 3, 2, 4).reshape(B, S, HG_HEADS, HG_HEAD_V)

def first_inputs(seed: int = 0) -> dict:
    key = jax.random.key(seed)
    ks = jax.random.split(key, 20)
    f32 = jnp.float32
    nrm = lambda k, shape, scale: (jax.random.normal(k, shape, f32) * scale)
    gain = lambda k, shape: 1.0 + 0.05 * jax.random.normal(k, shape, f32)
    offsets = jax.random.randint(ks[2], (BATCH, 1), 0, 4096, dtype=jnp.int32)
    positions = (offsets + jnp.arange(SEQ, dtype=jnp.int32)[None, :]).astype(jnp.int32)
    return {
        "x": nrm(ks[0], (BATCH, SEQ, D_MODEL), 1.0),
        "c": nrm(ks[1], (BATCH, D_MODEL), 1.0),
        "positions": positions,
        "w_ada": nrm(ks[3], (DEPTH, D_MODEL, N_MOD * D_MODEL), 0.5 * D_MODEL ** -0.5),
        "b_ada": nrm(ks[4], (DEPTH, N_MOD * D_MODEL), 0.02),
        "g_pre_mix": gain(ks[5], (DEPTH, D_MODEL)),
        "g_post_mix": gain(ks[6], (DEPTH, D_MODEL)),
        "g_pre_ffn": gain(ks[7], (DEPTH, D_MODEL)),
        "g_post_ffn": gain(ks[8], (DEPTH, D_MODEL)),
        "w_in": nrm(ks[9], (DEPTH, D_MODEL, IN_COLS), D_MODEL ** -0.5),
        "attn_sinks": nrm(ks[10], (DEPTH, ATT_HEADS), 1.0),
        "w_attn_proj": nrm(ks[11], (DEPTH, ATT_WIDTH, D_MODEL), ATT_WIDTH ** -0.5),
        "hg_lower_bounds": nrm(ks[12], (N_LB, HG_F_WIDTH), 0.5),
        "hg_norm": gain(ks[13], (DEPTH, HG_HEAD_V)),
        "w_hgrn_proj": nrm(ks[14], (DEPTH, HG_V_WIDTH, D_MODEL), HG_V_WIDTH ** -0.5),
        "w_out": nrm(ks[15], (DEPTH, D_MODEL, D_MODEL), D_MODEL ** -0.5),
        "w_ffn_in": nrm(ks[16], (DEPTH, D_MODEL, 2 * FFN_HIDDEN), D_MODEL ** -0.5),
        "w_ffn_out": nrm(ks[17], (DEPTH, FFN_HIDDEN, D_MODEL), FFN_HIDDEN ** -0.5),
    }

def first_block(x, c, positions, w_ada, b_ada, g_pre_mix, g_post_mix, g_pre_ffn, g_post_ffn,
              w_in, attn_sinks, w_attn_proj, hg_lower_bounds, hg_norm, w_hgrn_proj, w_out,
              w_ffn_in, w_ffn_out):
    B, S = x.shape[0], x.shape[1]
    inv_freq = ROPE_THETA ** (-jnp.arange(0, ROT_DIM, 2, dtype=jnp.float32) / ROT_DIM)
    ang = positions.astype(jnp.float32)[..., None] * inv_freq
    cos, sin = jnp.cos(ang)[:, :, None, :], jnp.sin(ang)[:, :, None, :]
    lb_table = jnp.cumsum(jax.nn.softmax(hg_lower_bounds.astype(jnp.float32), axis=0), axis=0)
    splits = [ATT_WIDTH, ATT_WIDTH + KV_WIDTH, ATT_WIDTH + 2 * KV_WIDTH,
              ATT_WIDTH + 2 * KV_WIDTH + HG_F_WIDTH,
              ATT_WIDTH + 2 * KV_WIDTH + 2 * HG_F_WIDTH,
              ATT_WIDTH + 2 * KV_WIDTH + 2 * HG_F_WIDTH + HG_V_WIDTH,
              ATT_WIDTH + 2 * KV_WIDTH + 2 * HG_F_WIDTH + 2 * HG_V_WIDTH,
              ATT_WIDTH + 2 * KV_WIDTH + 2 * HG_F_WIDTH + 2 * HG_V_WIDTH + D_MODEL]
    for l in range(DEPTH):
        mod = (c @ w_ada[l] + b_ada[l])[:, None, :]
        shift1, scale1, gate1, shift2, scale2, gate2 = jnp.split(mod, N_MOD, axis=-1)

        h = rmsnorm(x, g_pre_mix[l]) * (1.0 + scale1) + shift1
        proj = h @ w_in[l]
        q_a, k_a, v_a, q_h, f_h, i_h, g_h, gate_a, gate_h = jnp.split(proj, splits, axis=-1)
        qa = rope_partial(q_a.reshape(B, S, ATT_HEADS, HEAD_DIM), cos, sin)
        ka = rope_partial(k_a.reshape(B, S, ATT_KV_HEADS, HEAD_DIM), cos, sin)
        va = v_a.reshape(B, S, ATT_KV_HEADS, HEAD_DIM)
        y_a = sliding_window_attention(qa, ka, va, attn_sinks[l]) @ w_attn_proj[l]
        o_h = hgrn2_recurrence(q_h, f_h, i_h, lb_table[l])
        o_h = rmsnorm(o_h, hg_norm[l]).reshape(B, S, HG_V_WIDTH).astype(x.dtype)
        y_h = (o_h * jax.nn.sigmoid(g_h)) @ w_hgrn_proj[l]
        merged = jax.nn.sigmoid(gate_a) * y_a + jax.nn.sigmoid(gate_h) * y_h
        y = merged @ w_out[l]
        x = x + gate1 * rmsnorm(y, g_post_mix[l])

        h = rmsnorm(x, g_pre_ffn[l]) * (1.0 + scale2) + shift2
        gu = h @ w_ffn_in[l]
        g_ffn, u_ffn = jnp.split(gu, 2, axis=-1)
        y = (jax.nn.silu(g_ffn) * u_ffn) @ w_ffn_out[l]
        x = x + gate2 * rmsnorm(y, g_post_ffn[l])
    return x


PLE_DIM = 256

ATT_HEAD_DIM = 64
ATT_WIDTH_2 = D_MODEL // 2
ATT_HEADS_2 = ATT_WIDTH_2 // ATT_HEAD_DIM
BAND_CHUNKS = 9
MAX_REL_DIST = 256

GLA_HEADS = 4
GLA_WIDTH = D_MODEL // 2
GLA_DV = GLA_WIDTH // GLA_HEADS
GLA_KEY_WIDTH = GLA_WIDTH // 2
GLA_DK = GLA_KEY_WIDTH // GLA_HEADS
GLA_GATE_RANK = 16
GLA_GATE_TAU = 16.0

MIX_WIDTH = ATT_WIDTH_2 + GLA_WIDTH
IN_SPLITS = (ATT_WIDTH_2, ATT_WIDTH_2, ATT_WIDTH_2,
             GLA_KEY_WIDTH, GLA_KEY_WIDTH,
             GLA_WIDTH, GLA_WIDTH,
             GLA_GATE_RANK)
IN_PROJ_WIDTH = sum(IN_SPLITS)

D_FF = 5632
CONV_WIDTH = 3


def rms_norm(x, w):
    xf = x.astype(jnp.float32)
    y = xf * lax.rsqrt(jnp.mean(xf * xf, axis=-1, keepdims=True) + EPS)
    return (y * w.astype(jnp.float32)).astype(x.dtype)

def split_cols(t, sizes):
    idx = [int(v) for v in np.cumsum(sizes)[:-1]]
    return jnp.split(t, idx, axis=-1)

def rel_pos_bias(table):
    q_idx = jnp.arange(CHUNK) + (BAND_CHUNKS - 1) * CHUNK
    k_idx = jnp.arange(BAND_CHUNKS * CHUNK)
    dist = jnp.clip(q_idx[:, None] - k_idx[None, :], -MAX_REL_DIST, MAX_REL_DIST) + MAX_REL_DIST
    return table[:, dist]

def chunked_band_attention(q, k, v, bias_table):
    B, T, H, hd = q.shape
    nc = T // CHUNK
    pad = (BAND_CHUNKS - 1) * CHUNK
    band = BAND_CHUNKS * CHUNK
    k_pad = jnp.pad(k, ((0, 0), (pad, 0), (0, 0), (0, 0)))
    v_pad = jnp.pad(v, ((0, 0), (pad, 0), (0, 0), (0, 0)))
    bias = rel_pos_bias(bias_table).astype(jnp.float32)[None]
    key_off = jnp.arange(band) - pad
    q_chunks = q.reshape(B, nc, CHUNK, H, hd).transpose(1, 0, 2, 3, 4)
    scale = hd ** -0.5
    neg = jnp.finfo(jnp.float32).min

    def one_chunk(args):
        c, qc = args
        start = c * CHUNK
        kb = lax.dynamic_slice_in_dim(k_pad, start, band, axis=1)
        vb = lax.dynamic_slice_in_dim(v_pad, start, band, axis=1)
        s = jnp.einsum('bqhd,bkhd->bhqk', qc, kb).astype(jnp.float32) * scale + bias
        valid = (start + key_off) >= 0
        s = jnp.where(valid[None, None, None, :], s, neg)
        pr = jax.nn.softmax(s, axis=-1).astype(vb.dtype)
        return jnp.einsum('bhqk,bkhd->bqhd', pr, vb)

    out = lax.map(one_chunk, (jnp.arange(nc), q_chunks))
    return out.transpose(1, 0, 2, 3, 4).reshape(B, T, H * hd)

def gated_linear_attention(q, k, v, log_a):
    B, T, H, dk = q.shape
    dv = v.shape[-1]
    nc = T // CHUNK

    def to_chunks(t):
        return t.reshape(B, nc, CHUNK, H, t.shape[-1]).transpose(0, 1, 3, 2, 4).astype(jnp.float32)

    qc = to_chunks(q) * (dk ** -0.5)
    kc = to_chunks(k)
    vc = to_chunks(v)
    b = jnp.cumsum(to_chunks(log_a), axis=3)
    b_last = b[:, :, :, -1:, :]
    q_dec = qc * jnp.exp(b)
    k_inv = kc * jnp.exp(-b)
    k_to_end = kc * jnp.exp(b_last - b)
    causal = jnp.tril(jnp.ones((CHUNK, CHUNK), dtype=bool))
    attn = jnp.where(causal, jnp.einsum('bnhid,bnhjd->bnhij', q_dec, k_inv), 0.0)
    o_intra = jnp.einsum('bnhij,bnhjv->bnhiv', attn, vc)

    chunk_update = jnp.einsum('bnhjd,bnhjv->bnhdv', k_to_end, vc)
    chunk_decay = jnp.exp(b_last[:, :, :, 0, :])

    def step(S, xs):
        upd, dec = xs
        return dec[..., None] * S + upd, S

    S0 = jnp.zeros((B, H, dk, dv), jnp.float32)
    _, S_prev = lax.scan(step, S0, (chunk_update.transpose(1, 0, 2, 3, 4),
                                    chunk_decay.transpose(1, 0, 2, 3)))
    S_prev = S_prev.transpose(1, 0, 2, 3, 4)
    o_inter = jnp.einsum('bnhid,bnhdv->bnhiv', q_dec, S_prev)
    o = o_intra + o_inter
    return o.transpose(0, 1, 3, 2, 4).reshape(B, T, H, dv)

def causal_depthwise_conv(u, w, bias):
    T = u.shape[1]
    up = jnp.pad(u, ((0, 0), (CONV_WIDTH - 1, 0), (0, 0)))
    y = bias
    for tap in range(CONV_WIDTH):
        y = y + up[:, tap:tap + T] * w[tap]
    return y

def second_inputs(seed: int = 0) -> dict:
    key = jax.random.key(seed)
    ks = jax.random.split(key, 20)
    f32 = jnp.float32

    def nrm(k, shape, scale):
        return jax.random.normal(k, shape, f32) * scale

    def gain(k, shape):
        return 1.0 + 0.05 * jax.random.normal(k, shape, f32)

    return {
        "x": nrm(ks[0], (BATCH, SEQ, D_MODEL), 1.0),
        "p": nrm(ks[1], (DEPTH, BATCH, SEQ, PLE_DIM), 1.0),
        "norm_mix_w": gain(ks[2], (DEPTH, D_MODEL)),
        "w_in": nrm(ks[3], (DEPTH, D_MODEL, IN_PROJ_WIDTH), D_MODEL ** -0.5),
        "att_rel_bias": nrm(ks[4], (DEPTH, ATT_HEADS_2, 2 * MAX_REL_DIST + 1), 0.3),
        "w_gla_gate_up": nrm(ks[5], (DEPTH, GLA_GATE_RANK, GLA_KEY_WIDTH), GLA_GATE_RANK ** -0.5),
        "b_gla_gate": nrm(ks[6], (DEPTH, GLA_KEY_WIDTH), 0.5),
        "gla_norm_w": gain(ks[7], (DEPTH, GLA_DV)),
        "w_out": nrm(ks[8], (DEPTH, MIX_WIDTH, D_MODEL), MIX_WIDTH ** -0.5),
        "norm_ffn_w": gain(ks[9], (DEPTH, D_MODEL)),
        "w_ffn_up": nrm(ks[10], (DEPTH, D_MODEL, 2 * D_FF), D_MODEL ** -0.5),
        "w_ffn_conv": nrm(ks[11], (DEPTH, CONV_WIDTH, 2 * D_FF), CONV_WIDTH ** -0.5),
        "b_ffn_conv": nrm(ks[12], (DEPTH, 2 * D_FF), 0.02),
        "w_ffn_down": nrm(ks[13], (DEPTH, D_FF, D_MODEL), D_FF ** -0.5),
        "norm_ple_w": gain(ks[14], (DEPTH, D_MODEL)),
        "w_ple_gate": nrm(ks[15], (DEPTH, D_MODEL, D_MODEL), D_MODEL ** -0.5),
        "w_ple_proj": nrm(ks[16], (DEPTH, PLE_DIM, D_MODEL), PLE_DIM ** -0.5),
        "final_norm_w": gain(ks[17], (D_MODEL,)),
    }

def second_block(x, p, norm_mix_w, w_in, att_rel_bias, w_gla_gate_up, b_gla_gate, gla_norm_w,
              w_out, norm_ffn_w, w_ffn_up, w_ffn_conv, b_ffn_conv, w_ffn_down,
              norm_ple_w, w_ple_gate, w_ple_proj, final_norm_w):
    B, T, _ = x.shape
    for i in range(DEPTH):
        h = rms_norm(x, norm_mix_w[i])
        proj = h @ w_in[i]
        q_a, k_a, v_a, q_g, k_g, v_g, r_g, gate_lr = split_cols(proj, IN_SPLITS)

        hs_a = (B, T, ATT_HEADS_2, ATT_HEAD_DIM)
        y_a = chunked_band_attention(q_a.reshape(hs_a), k_a.reshape(hs_a), v_a.reshape(hs_a),
                                     att_rel_bias[i])

        gate_logit = (gate_lr @ w_gla_gate_up[i] + b_gla_gate[i]).astype(jnp.float32)
        log_a = (jax.nn.log_sigmoid(gate_logit) / GLA_GATE_TAU).reshape(B, T, GLA_HEADS, GLA_DK)
        o_g = gated_linear_attention(q_g.reshape(B, T, GLA_HEADS, GLA_DK),
                                     k_g.reshape(B, T, GLA_HEADS, GLA_DK),
                                     v_g.reshape(B, T, GLA_HEADS, GLA_DV), log_a)
        o_g = rms_norm(o_g.astype(x.dtype), gla_norm_w[i]).reshape(B, T, GLA_WIDTH)
        y_g = o_g * jax.nn.silu(r_g)

        x = x + jnp.concatenate([y_a, y_g], axis=-1) @ w_out[i]

        h = rms_norm(x, norm_ffn_w[i])
        u = causal_depthwise_conv(h @ w_ffn_up[i], w_ffn_conv[i], b_ffn_conv[i])
        u_gate, u_val = jnp.split(u, 2, axis=-1)
        x = x + (jax.nn.gelu(u_gate) * u_val) @ w_ffn_down[i]

        h = rms_norm(x, norm_ple_w[i])
        g = jax.nn.sigmoid(h @ w_ple_gate[i])
        x = x + g * (p[i] @ w_ple_proj[i])
    return rms_norm(x, final_norm_w)


def setup_inputs(seed=0):
    out = dict(first_inputs(seed))
    for name, value in second_inputs(seed + 1).items():
        if name != "x":
            out[name + "_2"] = value
    return out


def reference(
    x, c, positions, w_ada, b_ada, g_pre_mix, g_post_mix, g_pre_ffn, g_post_ffn, w_in,
    attn_sinks, w_attn_proj, hg_lower_bounds, hg_norm, w_hgrn_proj, w_out, w_ffn_in, w_ffn_out,
    p_2, norm_mix_w_2, w_in_2, att_rel_bias_2, w_gla_gate_up_2, b_gla_gate_2, gla_norm_w_2,
    w_out_2, norm_ffn_w_2, w_ffn_up_2, w_ffn_conv_2, b_ffn_conv_2, w_ffn_down_2, norm_ple_w_2,
    w_ple_gate_2, w_ple_proj_2, final_norm_w_2,
):
    x = first_block(
        x, c, positions, w_ada, b_ada, g_pre_mix, g_post_mix, g_pre_ffn, g_post_ffn, w_in,
        attn_sinks, w_attn_proj, hg_lower_bounds, hg_norm, w_hgrn_proj, w_out, w_ffn_in,
        w_ffn_out,
    )
    return second_block(
        x, p_2, norm_mix_w_2, w_in_2, att_rel_bias_2, w_gla_gate_up_2, b_gla_gate_2,
        gla_norm_w_2, w_out_2, norm_ffn_w_2, w_ffn_up_2, w_ffn_conv_2, b_ffn_conv_2,
        w_ffn_down_2, norm_ple_w_2, w_ple_gate_2, w_ple_proj_2, final_norm_w_2,
    )


_drawn_inputs = setup_inputs


def setup_inputs(seed=0):
    import zlib

    import numpy as np

    out = dict(_drawn_inputs(seed))
    spreads = {}
    factors = {'attn_sinks': 2.68,
     'hg_lower_bounds': 3.502,
     'gla_norm_w_2': 3.563,
     'b_ffn_conv_2': 4.668,
     'norm_ple_w_2': 27.221,
     'att_rel_bias_2': 3.854}
    for name, (base, spread) in spreads.items():
        noise = np.random.default_rng([zlib.crc32(name.encode()), seed]).standard_normal(out[name].shape)
        drawn = base * np.exp(spread * noise) if base else spread * noise
        out[name] = __import__('jax').numpy.asarray(drawn.astype(out[name].dtype))
    for name, factor in factors.items():
        out[name] = (out[name] * factor).astype(out[name].dtype)
    return out
```

```python
from contextlib import ExitStack, contextmanager

import numpy as np

import concourse.bass as bass
from concourse import mybir
from concourse.alu_op_type import AluOpType as ALU

ACT = mybir.ActivationFunctionType
AX_X = mybir.AxisListType.X
F32 = mybir.dt.float32
F32R = mybir.dt.float32r
I32 = mybir.dt.int32

P = 128
TOK = 256
TT = TOK // P
D = 2048
KD = D // P
COLS = 512
KU = 4
EPS = 1e-6

ATT_H, KV_H, HD = 16, 2, 64
ATT_W, KV_W = ATT_H * HD, KV_H * HD
HG_H, HG_D = 8, 128
HG_W = HG_H * HG_D
CHUNK = 64
FFN = 5632
ROT_HALF = HD // 8
ROPE_THETA = 500000.0
Q0 = 0
KV0 = ATT_W
QH0 = KV0 + 2 * KV_W
FH0 = QH0 + HG_W
IH0 = FH0 + HG_W
GH0 = IH0 + HG_W
GA0 = GH0 + HG_W
GB0 = GA0 + D

A2 = D // 2
GLA_H, GLA_DV, GLA_DK = 4, 256, 128
RANK = 16
TAU = 16.0
PLE = 256
DIST = 256
QG0 = 3 * A2
KG0 = QG0 + GLA_H * GLA_DK
VG0 = KG0 + GLA_H * GLA_DK
RG0 = VG0 + A2
LR0 = RG0 + A2

NEG = -1.0e30
LOWEST = -3.0e38
LEVELS = [32, 16, 8, 4, 2, 1]

INV_FREQ = np.float32(ROPE_THETA) ** (-np.arange(0, 2 * ROT_HALF, 2, dtype=np.float32)
                                      / np.float32(2 * ROT_HALF))
ROUNDER = 12582912.0
TURN_PARTS = [6.28125, int((2 * np.pi - 6.28125) * 2 ** 21) / 2 ** 21]
TURN_PARTS.append(float(np.float32(2 * np.pi - sum(TURN_PARTS))))

FFN_PARTS = [(0, 6), (6, 5)]


class Phase:

    def __init__(self, plan, iters, groups):
        self.iters, self.groups = iters, groups
        self.halves, self.units, self.end = [], [], []
        for g, (kt, cols) in enumerate(groups):
            for k0 in range(0, kt, KU):
                j = len(self.units)
                self.units.append((g, k0, min(KU, kt - k0), cols))
                for h in range(0, min(KU, kt - k0), 2):
                    self.halves.append((g, j, h // 2, k0 + h))
            self.end.append(len(self.halves))
        self.turn = -(-len(self.units) // 4) * 4
        self.n0 = plan.n
        plan.n += iters * self.turn
        self.fill0, per = list(plan.fill), [0] * 4
        self.occ = []
        for j in range(len(self.units)):
            self.occ.append(per[j % 4])
            per[j % 4] += 1
        self.per = per
        plan.fill = [a + iters * b for a, b in zip(plan.fill, per)]
        self.q0, self.qper = list(plan.q), [0, 0]
        self.pair, self.use = [], []
        for g in range(len(groups)):
            self.pair.append(g % 2)
            self.use.append(self.qper[g % 2])
            self.qper[g % 2] += 1
        plan.q = [a + iters * b for a, b in zip(plan.q, self.qper)]

    def half(self, i, idx):
        if idx >= len(self.halves):
            i, idx = i + 1, idx - len(self.halves)
        g, j, h, _ = self.halves[idx]
        at = 2 * j + h
        after = 2 * self.turn if idx + 1 == len(self.halves) else (
            2 * self.halves[idx + 1][1] + self.halves[idx + 1][2])
        full = 16 * (self.fill0[j % 4] + i * self.per[j % 4] + self.occ[j] + 1)
        return 2 * (self.n0 + i * self.turn) + at, at % 4, after - at, j % 4, h, full, self.units[j][3]

    def unit_number(self, i, j):
        return self.n0 + i * self.turn + j

    def done(self, i, g):
        g_, j, h, _ = self.halves[self.end[g] - 1]
        return 4 + 2 * (self.n0 + i * self.turn) + 2 * j + h + 1

    def free(self, i, g):
        p = self.pair[g]
        return 1 + self.q0[p] + i * self.qper[p] + self.use[g]

    def freed(self, i, g):
        return self.free(i, g) + 1


class Plan:
    def __init__(self):
        self.n, self.fill, self.q = 0, [0] * 4, [0, 0]
        full = (KD, COLS)
        self.mix_in = Phase(self, 1, [full, full, (KD, 2 * KV_W)] + [full] * 8)
        self.mix_gate = Phase(self, D // COLS, [full, (ATT_W // P, COLS), full, (HG_W // P, COLS)])
        self.mix_out = Phase(self, D // COLS // 2, [full, full])
        self.up1, self.down1 = [], []
        for _, n in FFN_PARTS:
            self.up1.append(Phase(self, n, [full, full]))
            self.down1.append(Phase(self, 2, [(4 * n, COLS), (4 * n, COLS)]))
        self.mix_in2 = Phase(self, 1, [full] * 8 + [(KD, RANK)] + [full] * 4)
        self.mix_out2 = Phase(self, D // COLS // 2, [full, full])
        self.up2, self.down2 = [], []
        for _, n in FFN_PARTS:
            self.up2.append(Phase(self, n, [full, full]))
            self.down2.append(Phase(self, 2, [(4 * n, COLS), (4 * n, COLS)]))
        self.ple = Phase(self, D // COLS - 1, [full, (PLE // P, COLS)])
        self.ple_last = Phase(self, 1, [full, (PLE // P, COLS)])


BANK_USES = [
    ("cols", (1, 0, 0, 0)), ("conv", (1, 1, 1, 1)),
    ("norm0", (2, 2, 2, 2)), ("rope", (2, 1, 1, 1)),
] + [(f"attn0_{b}", (3, 2, 2, 2)) for b in range(4)] + [
    ("diag0", (1, 1, 1, 1))] + [(f"level{n}", (1, 1, 1, 1)) for n in range(len(LEVELS))] + [
    ("rec0_k", (1, 1, 1, 1)), ("rec0_u0", (1, 1, 0, 0)), ("rec0_u1", (0, 0, 1, 1)),
    ("rec0_u2", (1, 1, 0, 0)), ("rec0_o", (1, 1, 1, 1)),
    ("heads0", (2, 2, 2, 2)), ("merged", (2, 2, 2, 2)), ("norm1", (2, 2, 2, 2)),
    ("norm2", (2, 2, 2, 2)),
] + [(f"attn1_{b}", (3, 2, 2, 2)) for b in range(4)] + [
    ("low_rank", (1, 0, 0, 0)), ("gate", (1, 1, 0, 0)), ("gla", (1, 1, 0, 0)),
    ("rec1_k", (1, 1, 0, 0)), ("rec1_u0", (1, 1, 0, 0)), ("rec1_u1", (0, 0, 1, 1)),
    ("rec1_u2", (1, 1, 0, 0)), ("rec1_o", (1, 1, 1, 1)),
    ("heads1", (2, 2, 2, 2)), ("norm3", (2, 2, 2, 2)), ("ple", (1, 0, 0, 0)), ("norm4", (2, 2, 2, 2)),
]


def bank_bases():
    at, base = [0] * 4, {}
    for name, uses in BANK_USES:
        base[name] = tuple(at)
        at = [a + u for a, u in zip(at, uses)]
    return base


@contextmanager
def turns(eng, n):
    if n == 1:
        yield 0
    else:
        with eng.Fori(0, n) as i:
            yield i


def build_program(nc, a, out):
    plan = Plan()
    bank0 = bank_bases()

    with ExitStack() as ctx:
        def sb(name, shape, dt=F32):
            return ctx.enter_context(nc.sbuf_tensor(name, shape, dt))

        sems = {}

        def sem(name):
            if name not in sems:
                sems[name] = ctx.enter_context(nc.semaphore(name))
            return sems[name]

        x = sb("x", [P, TT, D])
        tokbuf = sb("tokbuf", [P, TT, D])
        h_hi = sb("h_hi", [P, KD, TOK], F32R)
        h_lo = sb("h_lo", [P, KD, TOK], F32R)
        raw = sb("raw", [P, 4, KU, COLS])
        w_hi = sb("w_hi", [P, 4, 2, COLS], F32R)
        w_lo = sb("w_lo", [P, 4, 2, COLS], F32R)
        gate_row = sb("gate_row", [P, D])
        tmp = sb("tmp", [P, 2, 2, TOK])
        ident = sb("ident", [P, P])
        ones = sb("ones", [P, P])
        cols = sb("cols", [P, P])
        mod_cols = sb("mod_cols", [P, 96])
        a_cols = sb("a_cols", [P, 2, KD])
        conv_cols = sb("conv_cols", [P, 4, 2 * FFN // P])
        band = sb("band", [P, 3 * P])
        chunked = sb("chunked", [P, 3 * P])
        level_mask = sb("level_mask", [P, len(LEVELS), P])
        causal = sb("causal", [P, P])
        scan_keep = sb("scan_keep", [P, COLS])
        stats = sb("stats", [P, 8, 4])
        minus_half = sb("minus_half", [P, 16])
        trig = sb("trig", [P, 2, TT, ROT_HALF])
        pos_i = sb("pos_i", [P, TT], I32)
        pos_f = sb("pos_f", [P, TT])
        invf = sb("invf", [P, ROT_HALF])
        sinks = sb("sinks", [P, ATT_H])
        hg_gain = sb("hg_gain", [P, HG_D])
        gla_gain = sb("gla_gain", [P, GLA_DV])
        lb = sb("lb", [P, 6, HG_H])
        mx = sb("mx", [P, 2, 4, TT, 4])
        nmx = sb("nmx", [P, 2, 4, TT, 4])
        rsum = sb("rsum", [P, 2, 4, TT, 4])
        esink = sb("esink", [P, 4, TT, 4])
        den = sb("den", [P, 2, 4, TT, 4])
        rden = sb("rden", [P, 2, 4, TT, 4])
        hstat = sb("hstat", [P, 2, 2, 16])
        ends = sb("ends", [P, 2, 8, TOK // CHUNK])
        lr_tok = sb("lr_tok", [P, TT, RANK])
        ARENA_KB = 66
        ARENA0 = nc.sbuf_usable_end // 32 * 32 - ARENA_KB * 1024
        assert nc.sbuf_base <= ARENA0, (nc.sbuf_base, ARENA0, nc.sbuf_usable_end)

        def place(name, kb, shape, dt=F32):
            size = 4
            for n in shape[1:]:
                size *= n
            assert kb * 1024 + size <= ARENA_KB * 1024, name
            return nc.alloc_sbuf_tensor_at(name, shape, dt, offset=ARENA0 + int(kb * 1024))

        ada_raw = place("ada_raw", 0, [P, 4, KU, COLS])
        ada_acc = place("ada_acc", 32, [P, 2, COLS])
        ada_b = place("ada_b", 36, [1, 2, COLS])
        gate2_row = place("gate2_row", 40, [P, D])
        conv_rows = place("conv_rows", 48, [2 * FFN // P, 4, P])
        rows = place("rows", 51, [P, P])
        rope = place("rope", 52, [P, 6, 2, TT * ROT_HALF])
        qs = place("qs", 0, [P, HG_H, TOK])
        key = place("key", 8, [P, HG_H, TOK])
        logf = place("logf", 16, [P, HG_H, TOK])
        vh = place("vh", 24, [P, TT, HG_W])
        q_t = place("q_t", 32, [P, ATT_H // 2, TOK])
        k_t = place("k_t", 40, [P, KV_H, TOK])
        sm = place("sm", 42, [P, 4, 3 * P])
        pt = place("pt", 48, [P, 4, 3 * P])
        qk_tok = place("qk_tok", 54, [P, TT, ATT_H + 2 * KV_H, HD])
        v_tok = place("v_tok", 64, [P, TT, KV_W])
        rope_tmp = place("rope_tmp", 8, [P, 4, ATT_H + 2 * KV_H, ROT_HALF])
        fac = [place("fac0", 42, [P, HG_H, TOK]), place("fac1", 58, [P, HG_H, TOK])]
        scores = place("scores", 50, [P, 16, P])
        kend_t = place("kend_t", 58, [P, 16, P])
        state = [place("state1", 16, [P, HG_W]), place("state2", 20, [P, HG_W]),
                 place("state3", 42, [P, HG_W])]
        a_hi = place("a_hi", 0, [P, KD, TOK], F32R)
        a_lo = place("a_lo", 16, [P, KD, TOK], F32R)
        sig_a = place("sig_a", 42, [P, TT, COLS])
        sig_b = place("sig_b", 46, [P, TT, COLS])
        part_a = place("part_a", 50, [P, TT, COLS])
        part_b = place("part_b", 54, [P, TT, COLS])
        junk = place("junk", 58, [P, D])
        hid_hi = place("hid_hi", 0, [P, 24, TOK], F32R)
        hid_lo = place("hid_lo", 24, [P, 24, TOK], F32R)
        act_g = place("act_g", 48, [P, 4, TOK])
        act_u = place("act_u", 52, [P, 4, TOK])
        hid = place("hid", 56, [P, 4, TOK])
        q2_t = place("q2_t", 0, [P, ATT_H // 2, TOK])
        k2_t = place("k2_t", 8, [P, ATT_H // 2, TOK])
        va = place("va", 16, [P, TT, A2])
        toep = place("toep", 24, [P, ATT_H, TOK])
        sm2 = place("sm2", 40, [P, 4, 3 * P])
        pt2 = place("pt2", 46, [P, 4, 3 * P])
        qg = place("qg", 52, [P, GLA_H, TOK])
        kg = place("kg", 56, [P, GLA_H, TOK])
        w_up_g = place("w_up_g", 60, [RANK, GLA_H * GLA_DK])
        gate_lr = place("gate_lr", 62, [RANK, TOK])
        mirror = place("mirror", 63, [P, P])
        vg = place("vg", 24, [P, TT, A2])
        lg = place("lg", 0, [P, GLA_H, TOK])
        ebuf = [place("ebuf0", 4, [P, GLA_H, TOK]), place("ebuf1", 8, [P, GLA_H, TOK])]
        k_end = place("k_end", 12, [P, GLA_H, TOK])
        scores2 = place("scores2", 16, [P, 8, P])
        kend2_t = place("kend2_t", 20, [P, 8, P])
        state_2 = [place("state1_2", 32, [P, A2]), place("state2_2", 36, [P, A2]),
                   place("state3_2", 40, [P, A2])]
        p_tok = place("p_tok", 0, [P, TT, PLE])
        p_hi = place("p_hi", 2, [P, PLE // P, TOK], F32R)
        p_lo = place("p_lo", 4, [P, PLE // P, TOK], F32R)
        sig_p = place("sig_p", 8, [P, TT, COLS])
        out_row = place("out_row", 16, [P, D])

        psum = [ctx.enter_context(nc.psum_tensor(f"psum{n}", [P, 2, COLS], F32)) for n in range(2)]
        bank = ctx.enter_context(nc.psum_tensor("bank", [P, 4, COLS], F32))

        gate2_dram = nc.dram_tensor("gate2_dram", (P, D), F32).ap()

        raw_full = [sem(f"raw_full{n}") for n in range(4)]
        split_hi, split_lo, w_used = sem("split_hi"), sem("split_lo"), sem("w_used")
        psum_free = [sem("psum_free0"), sem("psum_free1")]
        bank_full = [sem(f"bank_full{n}") for n in range(4)]
        bank_free = [sem(f"bank_free{n}") for n in range(4)]
        ada_full = [sem(f"ada_full{n}") for n in range(4)]
        ada_b_full = [sem(f"ada_b_full{n}") for n in range(2)]

        class Chain:

            def __init__(self, eng, name):
                self.eng, self.sem, self.n = eng, sem(name), 0

            def __call__(self, ins):
                ins.then_inc(self.sem, 1)
                self.n += 1
                self.eng.wait_ge(self.sem, self.n)

        def fill(name, b, k=0):
            return 1 + bank0[name][b] + k

        def filled(name, b, k=0):
            return bank0[name][b] + k + 1

        def emptied(name, b, k=0):
            return fill(name, b, k) + 1

        def load_phase(sp, ph, source):
            with turns(sp, ph.iters) as i:
                for j, (g, k0, nk, ncol) in enumerate(ph.units):
                    sp.wait_ge(split_lo, 2 * ph.unit_number(i, j) + 2)
                    if ph.iters > 1:
                        sp.sem_inc(sem("slot_seen"), 1)
                    sp.dma_start(raw[:, j % 4, 0:nk, 0:ncol], source(i, g, k0, nk, ncol)
                                 ).then_inc(raw_full[j % 4], 16)

        def split_w_hi(act, ph, i, first, last):
            for idx in range(first, last):
                m, slot, inc, rs, h, full, ncol = ph.half(i, idx)
                act.wait_ge(raw_full[rs], full)
                act.wait_ge(w_used, m + 1)
                nc.scalar.activation(w_hi[:, slot, :, 0:ncol], raw[:, rs, 2 * h:2 * h + 2, 0:ncol],
                                     ACT.Copy).then_inc(split_hi, inc)

        def split_w_lo(dve, ph, i, first, last):
            for idx in range(first, last):
                m, slot, inc, rs, h, full, ncol = ph.half(i, idx)
                dve.wait_ge(split_hi, m + 1)
                nc.vector.tensor_tensor(w_lo[:, slot, :, 0:ncol], raw[:, rs, 2 * h:2 * h + 2, 0:ncol],
                                        w_hi[:, slot, :, 0:ncol].bitcast(F32),
                                        ALU.subtract).then_inc(split_lo, inc)

        def span(ph, g, final=False):
            first = (ph.end[g - 1] if g else 0) + 4
            last = ph.end[g] + 4
            if final:
                first, last = min(first, len(ph.halves)), min(last, len(ph.halves))
            return first, last

        def products(pe, ph, i, g, hi, lo, k_first=0, transposed=False):
            ps = psum[ph.pair[g]]
            pe.wait_ge(psum_free[ph.pair[g]], ph.free(i, g))
            start, stop = (ph.end[g - 1] if g else 0), ph.end[g]
            for idx in range(start, stop):
                m, slot, inc, _, _, _, ncol = ph.half(i, idx)
                pe.wait_ge(split_lo, 8 + m + 1)
                for kk in range(2):
                    k = k_first + ph.halves[idx][3] + kk
                    first = idx == start and kk == 0
                    last = idx == stop - 1 and kk == 1
                    wh, wl = w_hi[:, slot, kk, :], w_lo[:, slot, kk, :]
                    if not transposed:
                        for t in range(TT):
                            o = ps[:, t, 0:ncol]
                            xh, xl = hi[:, k, t * P:(t + 1) * P], lo[:, k, t * P:(t + 1) * P]
                            pe.matmul(o, xh, wh[:, 0:ncol], start=first, stop=False,
                                      skip_group_check=True)
                            pe.matmul(o, xh, wl[:, 0:ncol], start=False, stop=False,
                                      skip_group_check=True)
                            mm = pe.matmul(o, xl, wh[:, 0:ncol], start=False, stop=last,
                                           skip_group_check=True)
                    else:
                        for f in range(-(-ncol // P)):
                            n = min(P, ncol - f * P)
                            o = ps[0:n, f // 2, (f % 2) * TOK:(f % 2 + 1) * TOK]
                            fh, fl = wh[:, f * P:f * P + n], wl[:, f * P:f * P + n]
                            pe.matmul(o, fh, hi[:, k, :], start=first and f % 2 == 0, stop=False,
                                      skip_group_check=True)
                            pe.matmul(o, fh, lo[:, k, :], start=False, stop=False,
                                      skip_group_check=True)
                            mm = pe.matmul(o, fl, hi[:, k, :], start=False, stop=last,
                                           skip_group_check=True)
                mm.then_inc(w_used, inc)

        def transpose_pe(pe, stage, src, tiles):
            for b in range(tiles // 2):
                pe.wait_ge(bank_free[b % 4], fill(stage, b % 4, b // 4))
                for k in range(2):
                    for t in range(TT):
                        mm = pe.transpose(bank[:, b % 4, (2 * k + t) * P:(2 * k + t + 1) * P],
                                          src[:, t, (2 * b + k) * P:(2 * b + k + 1) * P], ident[:])
                mm.then_inc(bank_full[b % 4], 1)

        def split_act(act, stage, hi, tiles, scaled):
            for b in range(tiles // 2):
                if scaled:
                    act.wait_ge(bank_free[b % 4], emptied(stage, b % 4, b // 4))
                    src = tmp[:, b % 2, :, :]
                else:
                    act.wait_ge(bank_full[b % 4], filled(stage, b % 4, b // 4))
                    src = bank[:, b % 4, :].rearrange("p (k t) -> p k t", k=2)
                nc.scalar.activation(hi[:, 2 * b:2 * b + 2, :], src, ACT.Copy
                                     ).then_inc(sem(f"{stage}_hi"), 1)

        def split_dve(dve, stage, hi, lo, tiles, gain=None, shift=None):
            def lower(b):
                dve.wait_ge(sem(f"{stage}_hi"), b + 1)
                src = (tmp[:, b % 2, :, :] if gain is not None
                       else bank[:, b % 4, :].rearrange("p (k t) -> p k t", k=2))
                ins = nc.vector.tensor_tensor(lo[:, 2 * b:2 * b + 2, :], src,
                                              hi[:, 2 * b:2 * b + 2, :].bitcast(F32), ALU.subtract)
                ins.then_inc(bank_free[b % 4] if gain is None else sem(f"{stage}_lo"), 1)

            for b in range(tiles // 2):
                if gain is not None:
                    dve.wait_ge(bank_full[b % 4], filled(stage, b % 4, b // 4))
                    if b >= 2:
                        dve.wait_ge(sem(f"{stage}_lo"), b - 1)
                    for k in range(2):
                        f = 2 * b + k
                        ins = nc.vector.tensor_scalar(
                            tmp[:, b % 2, k, :], bank[:, b % 4, k * TOK:(k + 1) * TOK],
                            gain[:, f:f + 1], shift[:, f:f + 1] if shift is not None else None,
                            ALU.mult, *([ALU.add] if shift is not None else []))
                    ins.then_inc(bank_free[b % 4], 1)
                    if b:
                        lower(b - 1)
                else:
                    lower(b)
            if gain is not None:
                lower(tiles // 2 - 1)

        def split_done(pe, stage, tiles, scaled):
            if scaled:
                pe.wait_ge(sem(f"{stage}_lo"), tiles // 2)
            else:
                for b in range(min(4, tiles // 2)):
                    pe.wait_ge(bank_free[b], emptied(stage, b, (tiles // 2 - 1 - b) // 4))

        def squares_act(act, r, src):
            for t in range(TT):
                if r or t:
                    act.wait_ge(sem("squares"), 2 * r + t)
                nc.scalar.activation(junk[:], src[:, t, :], ACT.Square,
                                     accum_out=stats[:, r, t:t + 1]).then_inc(sem("squares"), 1)

        def rms_pool(pool, chain, r):
            pool.wait_ge(sem("squares"), 2 * (r + 1))
            chain(nc.gpsimd.tensor_scalar(stats[:, r, 2:4], stats[:, r, 0:2], 1.0 / D, EPS,
                                          ALU.mult, ALU.add))
            nc.gpsimd.tensor_tensor(stats[:, r, 2:4], stats[:, r, 2:4], minus_half[:, 0:2],
                                    ALU.pow).then_inc(sem("rms"), 1)

        def normed_dve(dve, r):
            dve.wait_ge(sem("rms"), r + 1)
            for t in range(TT):
                nc.vector.tensor_scalar(tokbuf[:, t, :], x[:, t, :], stats[:, r, 2 + t:3 + t], None,
                                        ALU.mult).then_inc(sem("normed"), 1)

        def residual_dve(dve, chain, r):
            dve.wait_ge(sem("rms"), r + 1)
            for t in range(TT):
                chain(nc.vector.scalar_tensor_tensor(tokbuf[:, t, :], tokbuf[:, t, :],
                                                     stats[:, r, 2 + t:3 + t], gate_row[:],
                                                     ALU.mult, ALU.mult))
                ins = nc.vector.tensor_tensor(x[:, t, :], x[:, t, :], tokbuf[:, t, :], ALU.add)
                ins.then_inc(sem("x_ready"), 1)

        def scores_pe(pe, r, b, q, k, k_tile):
            for hh in range(4):
                h = 4 * b + hh
                o = bank[:, hh, :]
                rows_ = slice(HD * (h % 2), HD * (h % 2) + HD)
                kk = k[rows_, k_tile(h), :]
                pe.wait_ge(bank_free[hh], fill(f"attn{r}_{b}", hh, 0))
                mm = pe.matmul(o[:, 0:P], q[rows_, h // 2, 0:P], kk[:, 0:P], start=True,
                               stop=(r == 0), skip_group_check=True)
                mm = pe.matmul(o[:, P:3 * P], q[rows_, h // 2, P:2 * P], kk, start=False,
                               stop=(r == 0), skip_group_check=True)
                if r == 1:
                    pe.matmul(o[:, 0:P], toep[:, h, 0:P], mirror[:], start=False, stop=False,
                              skip_group_check=True)
                    pe.matmul(o[:, P:2 * P], toep[:, h, P:2 * P], mirror[:], start=False,
                              stop=False, skip_group_check=True)
                    mm = pe.matmul(o[:, 2 * P:3 * P], toep[:, h, 0:P], mirror[:], start=False,
                                   stop=True, skip_group_check=True)
                mm.then_inc(bank_full[hh], 1)

        def softmax_dve(dve, chain, r, b, s, mask):
            for hh in range(4):
                h = 4 * b + hh
                dve.wait_ge(bank_full[hh], filled(f"attn{r}_{b}", hh, 0))
                start = sinks[:, h:h + 1] if r == 0 else LOWEST
                for t, part in ((0, slice(0, P)), (1, slice(P, 3 * P))):
                    ins = nc.vector.tensor_tensor_reduce(s[:, hh, part], bank[:, hh, part],
                                                         mask[:, part], 1.0, start, ALU.add, ALU.max,
                                                         mx[:, r, b, t, hh:hh + 1])
                ins.then_inc(bank_free[hh], 1)
            dve.wait_ge(bank_free[3], emptied(f"attn{r}_{b}", 3, 0))
            if r == 0:
                for t in range(TT):
                    nc.vector.tensor_tensor(esink[:, b, t, :], sinks[:, 4 * b:4 * b + 4],
                                            mx[:, r, b, t, :], ALU.subtract)
            nc.vector.tensor_scalar(nmx[:, r, b], mx[:, r, b], -1.0, None, ALU.mult
                                    ).then_inc(sem(f"attn{r}_max"), 1)

        def softmax_act(act, r, b, s):
            act.wait_ge(sem(f"attn{r}_max"), b + 1)
            for hh in range(4):
                for t, part in ((0, slice(0, P)), (1, slice(P, 3 * P))):
                    nc.scalar.activation(s[:, hh, part], s[:, hh, part], ACT.Exp,
                                         bias=nmx[:, r, b, t, hh:hh + 1],
                                         accum_out=rsum[:, r, b, t, hh:hh + 1]
                                         ).then_inc(sem(f"attn{r}_exp"), 1)
            if r == 0:
                nc.scalar.activation(esink[:, b], esink[:, b], ACT.Exp).then_inc(sem(f"attn{r}_exp"), 1)

        EXPS = [9, 8]

        def turn_pe(pe, r, b, s):
            pe.wait_ge(sem(f"attn{r}_exp"), EXPS[r] * (b + 1))
            for hh in range(4):
                pe.wait_ge(bank_free[hh], fill(f"attn{r}_{b}", hh, 1))
                for n in range(3):
                    mm = pe.transpose(bank[:, hh, n * P:(n + 1) * P], s[:, hh, n * P:(n + 1) * P],
                                      ident[:])
                mm.then_inc(bank_full[hh], 1)

        def turn_act(act, r, b, p_):
            for hh in range(4):
                act.wait_ge(bank_full[hh], filled(f"attn{r}_{b}", hh, 1))
                nc.scalar.activation(p_[:, hh, :], bank[:, hh, 0:3 * P], ACT.Copy
                                     ).then_inc(bank_free[hh], 1)

        def values_pe(pe, r, b, p_, v):
            for hh in range(4):
                pe.wait_ge(bank_free[hh], emptied(f"attn{r}_{b}", hh, 1))
            for hh in range(4):
                c = (4 * b + hh) * HD if r == 1 else (4 * b + hh) // (ATT_H // KV_H) * HD
                lo_, hi_ = hh * HD, 4 * HD + hh * HD
                pe.matmul(bank[:, 0, lo_:lo_ + HD], p_[:, hh, 0:P], v[:, 0, c:c + HD],
                          start=(hh == 0), stop=False, skip_group_check=True)
                pe.matmul(bank[:, 0, hi_:hi_ + HD], p_[:, hh, P:2 * P], v[:, 0, c:c + HD],
                          start=False, stop=False, skip_group_check=True)
                mm = pe.matmul(bank[:, 0, hi_:hi_ + HD], p_[:, hh, 2 * P:3 * P], v[:, 1, c:c + HD],
                               start=False, stop=(hh == 3), skip_group_check=True)
            mm.then_inc(bank_full[0], 1)

        def values_dve(dve, chain, r, b):
            dve.wait_ge(sem(f"attn{r}_exp"), EXPS[r] * (b + 1))
            if r == 0:
                chain(nc.vector.tensor_tensor(den[:, r, b], rsum[:, r, b], esink[:, b], ALU.add))
            d = den if r == 0 else rsum
            chain(nc.vector.reciprocal(rden[:, r, b], d[:, r, b]))
            dve.wait_ge(bank_full[0], filled(f"attn{r}_{b}", 0, 2))
            for t in range(TT):
                ins = nc.vector.tensor_tensor(
                    tokbuf[:, t, 4 * b * HD:4 * (b + 1) * HD].rearrange("p (h d) -> p h d", h=4),
                    bank[:, 0, 4 * HD * t:4 * HD * (t + 1)].rearrange("p (h d) -> p h d", h=4),
                    rden[:, r, b, t, :].unsqueeze(2).to_broadcast([P, 4, HD]), ALU.mult)
            ins.then_inc(bank_free[0], 1)

        REC = [(HG_H, HG_D, qs, key, kend_t, scores, vh, state, fac[0]),
               (GLA_H, GLA_DV, qg, k_end, kend2_t, scores2, vg, state_2, ebuf[0])]

        def chunk_place(c):
            return c // 2, slice(CHUNK * (c % 2), CHUNK * (c % 2 + 1))

        def recurrence_pe(pe, r, ready):
            heads, dv, q, k, kt, sc, v, st, _ = REC[r]
            per_bank = COLS // dv
            pe.wait_ge(sem(f"rec{r}_k_ready"), ready)
            for b in range(2 * heads // 4):
                pe.wait_ge(bank_free[b], fill(f"rec{r}_k", b))
                for n in range(4):
                    z = 4 * b + n
                    mm = pe.transpose(bank[:, b, n * P:(n + 1) * P],
                                      k[:, z // 2, (z % 2) * P:(z % 2 + 1) * P], ident[:])
                mm.then_inc(bank_full[b], 1)
            for b in range(2 * heads // 4):
                pe.wait_ge(bank_free[b], emptied(f"rec{r}_k", b))
            for c in range(3):
                t, ps = chunk_place(c)
                for n in range(2):
                    b = 2 * (c % 2) + n
                    pe.wait_ge(bank_free[b], fill(f"rec{r}_u{c}", b))
                    for hh in range(per_bank):
                        h = n * per_bank + hh
                        mm = pe.matmul(bank[:, b, hh * dv:(hh + 1) * dv], kt[ps, 2 * h + t, :],
                                       v[ps, t, h * dv:(h + 1) * dv], start=(hh == 0),
                                       stop=(hh == per_bank - 1), skip_group_check=True)
                    mm.then_inc(bank_full[b], 1)
            for b in range(4):
                pe.wait_ge(bank_free[b], fill(f"rec{r}_o", b))
            for b in range(4):
                t, n = b // 2, b % 2
                for hh in range(per_bank):
                    h = n * per_bank + hh
                    part = slice(hh * dv, (hh + 1) * dv)
                    pe.matmul(bank[:, b, part], sc[:, 2 * h + t, :], v[:, t, h * dv:(h + 1) * dv],
                              start=(hh == 0), stop=False, skip_group_check=True)
                    for c in (2 * t, 2 * t + 1):
                        if c:
                            _, ps = chunk_place(c)
                            mm = pe.matmul(bank[ps, b, part], q[:, h, c * CHUNK:(c + 1) * CHUNK],
                                           st[c - 1][:, h * dv:(h + 1) * dv], start=False,
                                           stop=(hh == per_bank - 1), skip_group_check=True)
                mm.then_inc(bank_full[b], 1)

        def recurrence_act(act, r):
            heads, dv, _, _, kt, _, _, _, sq = REC[r]
            for b in range(2 * heads // 4):
                act.wait_ge(bank_full[b], filled(f"rec{r}_k", b))
                nc.scalar.activation(kt[:, 4 * b:4 * b + 4, :],
                                     bank[:, b, :].rearrange("p (z k) -> p z k", z=4), ACT.Copy
                                     ).then_inc(bank_free[b], 1)
            for b in range(4):
                act.wait_ge(bank_full[b], filled(f"rec{r}_o", b))
            nc.scalar.activation(junk[:], bank[:].rearrange("p b c -> p (b c)"), ACT.Square
                                 ).then_inc(sem(f"rec{r}_sq"), 1)

        def recurrence_dve(dve, r):
            heads, dv, _, _, _, _, _, st, _ = REC[r]
            per_bank = COLS // dv
            for c in range(3):
                for n in range(2):
                    b = 2 * (c % 2) + n
                    dve.wait_ge(bank_full[b], filled(f"rec{r}_u{c}", b))
                    part = slice(n * COLS, (n + 1) * COLS)
                    if c == 0:
                        ins = nc.vector.tensor_copy(st[0][:, part], bank[:, b, :])
                    else:
                        for hh in range(per_bank):
                            h = n * per_bank + hh
                            cols_ = slice(h * dv, (h + 1) * dv)
                            ins = nc.vector.scalar_tensor_tensor(
                                st[c][:, cols_], st[c - 1][:, cols_],
                                ends[:, r, h, c:c + 1],
                                bank[:, b, hh * dv:(hh + 1) * dv], ALU.mult, ALU.add)
                    ins.then_inc(bank_free[b], 1)
                    dve.wait_ge(bank_free[b], emptied(f"rec{r}_u{c}", b))
            dve.wait_ge(sem(f"rec{r}_sq"), 1)
            groups = TT * heads
            nc.vector.tensor_reduce(hstat[:, r, 0, 0:groups],
                                    junk[:].rearrange("p (g v) -> p g v", v=dv), AX_X, ALU.add
                                    ).then_inc(sem(f"rec{r}_sum"), 1)
            dve.wait_ge(sem(f"rec{r}_rms"), 1)
            for b in range(4):
                part = slice(b * COLS, (b + 1) * COLS)
                ins = nc.vector.tensor_tensor(
                    junk[:, part].rearrange("p (g v) -> p g v", v=dv),
                    bank[:, b, :].rearrange("p (g v) -> p g v", v=dv),
                    hstat[:, r, 1, b * per_bank:(b + 1) * per_bank].unsqueeze(2)
                    .to_broadcast([P, per_bank, dv]), ALU.mult)
                ins.then_inc(bank_free[b], 1)
            dve.wait_ge(bank_free[3], emptied(f"rec{r}_o", 3))
            nc.vector.tensor_tensor(tokbuf[:, :, D // 2:], junk[:].rearrange("p (t c) -> p t c", t=TT),
                                    tokbuf[:, :, D // 2:], ALU.mult).then_inc(sem(f"heads{r}_ready"), 1)

        def recurrence_pool(pool, chain, r, gain):
            heads, dv = REC[r][0], REC[r][1]
            for t in range(TT):
                g = tokbuf[:, t, D // 2:].rearrange("p (h v) -> p h v", v=dv)
                chain(nc.gpsimd.tensor_tensor(g, g, gain[:].unsqueeze(1).to_broadcast([P, heads, dv]),
                                              ALU.mult))
            pool.wait_ge(sem(f"rec{r}_sum"), 1)
            n = TT * heads
            chain(nc.gpsimd.tensor_scalar(hstat[:, r, 1, 0:n], hstat[:, r, 0, 0:n], 1.0 / dv, EPS,
                                          ALU.mult, ALU.add))
            nc.gpsimd.tensor_tensor(hstat[:, r, 1, 0:n], hstat[:, r, 1, 0:n], minus_half[:, 0:n],
                                    ALU.pow).then_inc(sem(f"rec{r}_rms"), 1)

        ADA = [(8, 0, False), (4, 8, True), (8, 12, False), (4, 20, True)]

        w_ada = a["w_ada"].rearrange("l (k p) c -> (l p) k c", p=P)

        def weights(name):
            return a[name].rearrange("l (k p) c -> (l p) k c", p=P)

        W_in, W_ap, W_hp, W_out = (weights(n) for n in ("w_in", "w_attn_proj", "w_hgrn_proj", "w_out"))
        W_fi, W_fo = weights("w_ffn_in"), weights("w_ffn_out")
        W_in2, W_out2, W_fu2, W_fd2 = (weights(n) for n in
                                       ("w_in_2", "w_out_2", "w_ffn_up_2", "w_ffn_down_2"))
        W_pg, W_pp = weights("w_ple_gate_2"), weights("w_ple_proj_2")

        def cut(w, k0, nk, c0, ncol):
            return w[:, k0:k0 + nk, bass.ds(c0, ncol)]

        PARAMS = []

        def param(dst, src):
            PARAMS.append((dst, src))

        tiles_of = lambda ap: ap.rearrange("l (k p) -> (l k) p", p=P)
        ROW = {}
        at = 0
        for name, n in (("c", KD), ("g_pre_mix", KD), ("g_pre_ffn", KD), ("norm_mix_w_2", KD),
                        ("norm_ffn_w_2", KD), ("norm_ple_w_2", KD), ("hg_lower_bounds", 2 * HG_H),
                        ("b_gla_gate_2", GLA_H)):
            ROW[name] = at
            param(rows[at:at + n, :], tiles_of(a[name]))
            at += n
        N_ROWS = at
        param(x[:, :, :], a["x"].rearrange("b (t p) d -> p (b t) d", p=P))
        N_FIRST = len(PARAMS)
        nconv = 2 * FFN // P
        param(conv_rows[:, 0:3, :], a["w_ffn_conv_2"].rearrange("l t (j p) -> j (l t) p", p=P))
        param(conv_rows[:, 3, :], tiles_of(a["b_ffn_conv_2"]))
        ctx.enter_context(nc.allow_non_contiguous_dma(reason="positions, one number a partition"))
        param(pos_i[:], a["positions"].rearrange("b (t p) -> p (b t)", p=P))
        param(sinks[:], a["attn_sinks"][0, :].partition_broadcast(P))
        param(hg_gain[:], a["hg_norm"][0, :].partition_broadcast(P))
        param(gla_gain[:], a["gla_norm_w_2"][0, :].partition_broadcast(P))
        param(gate_row[:], a["g_post_mix"][0, :].partition_broadcast(P))
        param(gate2_row[:], a["g_post_ffn"][0, :].partition_broadcast(P))
        N_ALL = len(PARAMS)
        bias_tab = a["att_rel_bias_2"]

        block = ctx.enter_context(nc.Block())

        @block.sync
        def _(sp):
            for i in range(N_FIRST):
                sp.dma_start(*PARAMS[i]).then_inc(sem("params_first"), 16)
            group = 0
            for n, g0, _ in ADA:
                with turns(sp, n // 2) as i:
                    for gg in range(2):
                        g = g0 + 2 * i + gg
                        sp.wait_ge(sem("ada_summed"), g + 1)
                        sp.sem_inc(sem("slot_seen"), 1)
                        sp.dma_start(ada_b[:, gg, :], a["b_ada"][:, bass.ds(g * COLS, COLS)]
                                     ).then_inc(ada_b_full[gg], 16)
                        for u in range(4):
                            sp.wait_ge(sem("ada_used"), 4 * g + u + 1)
                            sp.sem_inc(sem("slot_seen"), 1)
                            sp.dma_start(ada_raw[:, u], cut(w_ada, u * KU, KU, g * COLS, COLS)
                                         ).then_inc(ada_full[u], 16)
            sp.wait_ge(sem("ada_read"), 26)
            sp.dma_start(gate2_dram, gate2_row[:]).then_inc(sem("gate2_saved"), 16)

            def mix_in_source(i, g, k0, nk, ncol):
                c0 = [Q0, Q0 + COLS, KV0, QH0, QH0 + COLS, FH0, FH0 + COLS, IH0, IH0 + COLS, GH0,
                      GH0 + COLS][g]
                return cut(W_in, k0, nk, c0, ncol)
            load_phase(sp, plan.mix_in, mix_in_source)
            load_phase(sp, plan.mix_gate, lambda i, g, k0, nk, ncol: cut(
                (W_in, W_ap, W_in, W_hp)[g], k0, nk, i * COLS + (GA0, 0, GB0, 0)[g], ncol))
            load_phase(sp, plan.mix_out, lambda i, g, k0, nk, ncol: cut(
                W_out, k0, nk, i * 2 * COLS + g * COLS, ncol))
            for part, (g0, n) in enumerate(FFN_PARTS):
                load_phase(sp, plan.up1[part], lambda i, g, k0, nk, ncol: cut(
                    W_fi, k0, nk, (i + g0) * COLS + g * FFN, ncol))
                if part == 0:
                    sp.wait_ge(sem("x_ready"), 2)
                    sp.wait_ge(sem("gate2_saved"), 16)
                    sp.dma_start(gate_row[:], gate2_dram).then_inc(sem("gate2_back"), 16)
                load_phase(sp, plan.down1[part], lambda i, g, k0, nk, ncol: cut(
                    W_fo, 4 * g0 + k0, nk, i * 2 * COLS + g * COLS, ncol))

            def mix_in2_source(i, g, k0, nk, ncol):
                c0 = [0, COLS, A2, A2 + COLS, 2 * A2, 2 * A2 + COLS, QG0, KG0, LR0, RG0, RG0 + COLS,
                      VG0, VG0 + COLS][g]
                return cut(W_in2, k0, nk, c0, ncol)
            load_phase(sp, plan.mix_in2, mix_in2_source)
            load_phase(sp, plan.mix_out2, lambda i, g, k0, nk, ncol: cut(
                W_out2, k0, nk, i * 2 * COLS + g * COLS, ncol))
            for part, (g0, n) in enumerate(FFN_PARTS):
                load_phase(sp, plan.up2[part], lambda i, g, k0, nk, ncol: cut(
                    W_fu2, k0, nk, (i + g0) * COLS + g * FFN, ncol))
                load_phase(sp, plan.down2[part], lambda i, g, k0, nk, ncol: cut(
                    W_fd2, 4 * g0 + k0, nk, i * 2 * COLS + g * COLS, ncol))
            for ph, first in ((plan.ple, 0), (plan.ple_last, D // COLS - 1)):
                load_phase(sp, ph, lambda i, g, k0, nk, ncol: cut(
                    (W_pg, W_pp)[g], k0, nk, (i + first) * COLS, ncol))
            o = out.rearrange("b (t p) d -> p (b t) d", p=P)
            for t in range(TT):
                sp.wait_ge(sem("result"), t + 1)
                sp.dma_start(o[:, t, :], tokbuf[:, t, :]).then_inc(sem("stored"), 16)
            sp.wait_ge(sem("stored"), 16 * TT)

        @block.scalar
        def _(act):
            act.sem_inc(sem("hid_hi"), 1)
            act.sem_inc(sem("hid2_hi"), 1)
            for i in range(N_FIRST, N_ALL):
                act.dma_start(*PARAMS[i]).then_inc(sem("params"), 16)
            act.wait_ge(sem("angles"), 1)
            nc.scalar.activation(trig[:].rearrange("p s t f -> p s (t f)"), rope[:, 5],
                                 ACT.Sin).then_inc(sem("trig"), 1)
            act.wait_ge(sem("lb_shifted"), 2)
            nc.scalar.activation(lb[:, 3:5, :], lb[:, 1:3, :], ACT.Exp).then_inc(sem("lb_exp"), 1)
            act.wait_ge(sem("params_first"), 16 * N_FIRST)
            squares_act(act, 0, x)
            split_act(act, "norm0", h_hi, KD, True)
            ph = plan.mix_in
            split_w_hi(act, ph, 0, 0, 4)
            for g in range(len(ph.groups)):
                split_w_hi(act, ph, 0, *span(ph, g))
                act.wait_ge(w_used, ph.done(0, g))
                ps, free = psum[ph.pair[g]], psum_free[ph.pair[g]]
                if g < 2:
                    nc.scalar.activation(
                        qk_tok[:, :, 8 * g:8 * g + 8, :], ps[:].rearrange("p t (h d) -> p t h d", d=HD),
                        ACT.Copy, scale=HD ** -0.5).then_inc(free, 1)
                elif g == 2:
                    for t in range(TT):
                        for dup in range(2):
                            nc.scalar.activation(
                                qk_tok[:, t, ATT_H:, :].rearrange("p (k u) d -> p k u d", u=2)[:, :, dup, :],
                                ps[:, t, 0:KV_W].rearrange("p (k d) -> p k d", d=HD), ACT.Copy)
                    nc.scalar.activation(v_tok[:], ps[:, :, KV_W:2 * KV_W], ACT.Copy
                                         ).then_inc(free, 1)
                elif g < 5:
                    nc.scalar.activation(qs[:, 4 * (g - 3):4 * (g - 2), :].rearrange("p h t -> p (h t)"),
                                         ps[:].rearrange("p b c -> p (b c)"), ACT.Silu
                                         ).then_inc(free, 1)
                elif g < 7:
                    nc.scalar.activation(logf[:, 4 * (g - 5):4 * (g - 4), :].rearrange("p h t -> p (h t)"),
                                         ps[:].rearrange("p b c -> p (b c)"), ACT.Sigmoid
                                         ).then_inc(free, 1)
                elif g < 9:
                    nc.scalar.activation(vh[:, :, (g - 7) * COLS:(g - 6) * COLS], ps[:], ACT.Copy
                                         ).then_inc(free, 1)
                else:
                    nc.scalar.activation(tokbuf[:, :, D // 2 + (g - 9) * COLS:D // 2 + (g - 8) * COLS],
                                         ps[:], ACT.Sigmoid).then_inc(free, 1)
                if g == 3:
                    for b in range(5):
                        dst = q_t[:, 2 * b:2 * b + 2, :] if b < 4 else k_t[:]
                        act.wait_ge(bank_full[b % 4], filled("rope", b % 4, b // 4))
                        nc.scalar.activation(dst, bank[:, b % 4, :].rearrange("p (k t) -> p k t", k=2),
                                             ACT.Copy).then_inc(bank_free[b % 4], 1)
                if 5 <= g < 9:
                    turn_act(act, 0, g - 5, pt)
                if 4 <= g < 8:
                    softmax_act(act, 0, g - 4, sm)
            act.wait_ge(sem("f_ready"), 1)
            nc.scalar.activation(logf[:], logf[:], ACT.Ln).then_inc(sem("logf_ready"), 1)
            for n in range(len(LEVELS)):
                act.wait_ge(sem("level_diff"), 2 * (n + 1))
                nc.scalar.activation(fac[n % 2][:], fac[n % 2][:], ACT.Exp
                                     ).then_inc(sem("level_exp"), 1)
            for b in range(4):
                act.wait_ge(bank_free[b], emptied(f"level{len(LEVELS) - 1}", b))
            nc.scalar.activation(fac[0][:], logf[:], ACT.Exp).then_inc(sem("decay_exp"), 1)
            act.wait_ge(sem("decay_diff"), 1)
            nc.scalar.activation(fac[1][:], fac[1][:], ACT.Exp).then_inc(sem("decay_exp"), 1)
            recurrence_act(act, 0)
            split_act(act, "heads0", a_hi, KD, False)

            ph = plan.mix_gate
            with turns(act, ph.iters) as i:
                for g in range(4):
                    split_w_hi(act, ph, i, *span(ph, g))
                    if g % 2 == 0:
                        act.wait_ge(w_used, ph.done(i, g))
                        act.wait_ge(psum_free[1], ph.freed(i, g + 1) - 2)
                        nc.scalar.activation((sig_a, None, sig_b)[g][:], psum[0][:], ACT.Sigmoid
                                             ).then_inc(psum_free[0], 1)
            split_act(act, "merged", h_hi, KD, False)

            ph = plan.mix_out
            with turns(act, ph.iters) as i:
                for g in range(2):
                    split_w_hi(act, ph, i, *span(ph, g))
                    act.wait_ge(w_used, ph.done(i, g))
                    nc.scalar.activation(tokbuf[:, :, bass.ds(i * 2 * COLS + g * COLS, COLS)],
                                         psum[g][:], ACT.Copy).then_inc(psum_free[g], 1)
            act.wait_ge(psum_free[1], plan.mix_out.freed(1, 1))
            act.wait_ge(psum_free[0], plan.mix_out.freed(1, 0))
            squares_act(act, 1, tokbuf)
            act.wait_ge(sem("x_ready"), 2)
            squares_act(act, 2, x)
            split_act(act, "norm1", h_hi, KD, True)
            for part, (g0, n) in enumerate(FFN_PARTS):
                ph = plan.up1[part]
                n0 = g0
                with turns(act, ph.iters) as i:
                    split_w_hi(act, ph, i, *span(ph, 0))
                    act.wait_ge(w_used, ph.done(i, 0))
                    act.wait_ge(psum_free[1], ph.freed(i, 1) - 1)
                    nc.scalar.activation(act_g[:], psum[0][:].rearrange("p b (f t) -> p (b f) t", t=TOK),
                                         ACT.Silu).then_inc(psum_free[0], 1)
                    split_w_hi(act, ph, i, *span(ph, 1))
                    act.wait_ge(psum_free[1], ph.freed(i, 1))
                    nc.scalar.activation(hid_hi[:, bass.ds(i * 4, 4), :], hid[:], ACT.Copy
                                         ).then_inc(sem("hid_hi"), 1)
                ph = plan.down1[part]
                with turns(act, ph.iters) as i:
                    for g in range(2):
                        split_w_hi(act, ph, i, *span(ph, g))
                        if part == 0:
                            act.wait_ge(w_used, ph.done(i, g))
                            nc.scalar.activation(tokbuf[:, :, bass.ds(i * 2 * COLS + g * COLS, COLS)],
                                                 psum[g][:], ACT.Copy).then_inc(psum_free[g], 1)
            act.wait_ge(psum_free[1], plan.down1[1].freed(1, 1))
            squares_act(act, 3, tokbuf)
            act.wait_ge(sem("x_ready"), 4)
            act.dma_start(toep[:], bass.AP(tensor=bias_tab.tensor, offset=DIST - (P - 1),
                                           ap=[[1, P], [2 * DIST + 1, ATT_H], [1, TOK]])
                          ).then_inc(sem("toep_full"), 16)
            squares_act(act, 4, x)
            split_act(act, "norm2", h_hi, KD, True)
            act.wait_ge(sem("rms"), 5)
            act.dma_start(w_up_g[:], a["w_gla_gate_up_2"][0]).then_inc(sem("w_up_g_full"), 16)

            ph = plan.mix_in2
            for g in range(len(ph.groups)):
                split_w_hi(act, ph, 0, *span(ph, g))
                act.wait_ge(w_used, ph.done(0, g))
                ps, free = psum[ph.pair[g]], psum_free[ph.pair[g]]
                flat = ps[:].rearrange("p b (f t) -> p (b f) t", t=TOK)
                if g < 2:
                    nc.scalar.activation(q2_t[:, 4 * g:4 * g + 4, :], flat, ACT.Copy,
                                         scale=HD ** -0.5).then_inc(free, 1)
                elif g < 4:
                    nc.scalar.activation(k2_t[:, 4 * (g - 2):4 * (g - 1), :], flat, ACT.Copy
                                         ).then_inc(free, 1)
                elif g < 6:
                    nc.scalar.activation(va[:, :, (g - 4) * COLS:(g - 3) * COLS], ps[:], ACT.Copy
                                         ).then_inc(free, 1)
                elif g == 6:
                    nc.scalar.activation(qg[:], flat, ACT.Copy).then_inc(free, 1)
                elif g == 7:
                    nc.scalar.activation(kg[:], flat, ACT.Copy).then_inc(free, 1)
                elif g == 8:
                    nc.scalar.activation(lr_tok[:], ps[:, :, 0:RANK], ACT.Copy).then_inc(free, 1)
                elif g < 11:
                    nc.scalar.activation(tokbuf[:, :, D // 2 + (g - 9) * COLS:D // 2 + (g - 8) * COLS],
                                         ps[:], ACT.Silu).then_inc(free, 1)
                else:
                    act.wait_ge(bank_full[3], filled("attn1_3", 3, 0))
                    nc.scalar.activation(vg[:, :, (g - 11) * COLS:(g - 10) * COLS], ps[:], ACT.Copy
                                         ).then_inc(free, 1)
                if 7 <= g < 11:
                    turn_act(act, 1, g - 7, pt2)
                if 6 <= g < 10:
                    softmax_act(act, 1, g - 6, sm2)
            act.wait_ge(bank_full[0], filled("low_rank", 0))
            nc.scalar.activation(gate_lr[:], bank[0:RANK, 0, 0:TOK], ACT.Copy).then_inc(bank_free[0], 1)
            act.wait_ge(sem("gate_abs"), 1)
            nc.scalar.activation(ebuf[0][:], ebuf[0][:], ACT.Exp, scale=-1.0).then_inc(sem("gate_exp"), 1)
            act.wait_ge(sem("gate_exp"), 1)
            nc.scalar.activation(ebuf[0][:], ebuf[0][:], ACT.Ln, bias=1.0).then_inc(sem("gate_ln"), 1)
            act.wait_ge(sem("gla_sum"), 2)
            nc.scalar.activation(ebuf[0][:], lg[:], ACT.Exp).then_inc(sem("gla_exp"), 1)
            nc.scalar.activation(ebuf[1][:], lg[:], ACT.Exp, scale=-1.0).then_inc(sem("gla_exp"), 1)
            act.wait_ge(sem("gla_diff"), 1)
            nc.scalar.activation(k_end[:], k_end[:], ACT.Exp).then_inc(sem("gla_exp"), 1)
            recurrence_act(act, 1)
            split_act(act, "heads1", h_hi, KD, False)
            ph = plan.mix_out2
            with turns(act, ph.iters) as i:
                for g in range(2):
                    split_w_hi(act, ph, i, *span(ph, g))
            act.wait_ge(psum_free[1], ph.freed(1, 1))
            squares_act(act, 5, x)
            split_act(act, "norm3", h_hi, KD, True)
            for part, (g0, n) in enumerate(FFN_PARTS):
                ph = plan.up2[part]
                with turns(act, ph.iters) as i:
                    for g in range(2):
                        split_w_hi(act, ph, i, *span(ph, g))
                        act.wait_ge(w_used, ph.done(i, g))
                        if g == 0:
                            act.wait_ge(sem("hid_ready"), 1 + g0 + i)
                        dst = (act_g, act_u)[g]
                        for f in range(4):
                            c = bass.ds((i + g0) * 4 + g * (FFN // P) + f, 1)
                            nc.scalar.activation(dst[:, f, :], psum[g][:, f // 2, (f % 2) * TOK:(f % 2 + 1) * TOK],
                                                 ACT.Identity, scale=conv_cols[:, 2, c],
                                                 bias=conv_cols[:, 3, c]).then_inc(sem("conv_tap2"), 1)
                        if g == 0:
                            act.wait_ge(psum_free[0], ph.freed(i, 0))
                            nc.scalar.activation(act_g[:], act_g[:], ACT.Gelu_apprx_tanh
                                                 ).then_inc(sem("gelu"), 1)
                    act.wait_ge(sem("hid_ready"), 2 + g0 + i)
                    nc.scalar.activation(hid_hi[:, bass.ds(i * 4, 4), :], hid[:], ACT.Copy
                                         ).then_inc(sem("hid2_hi"), 1)
                ph = plan.down2[part]
                with turns(act, ph.iters) as i:
                    for g in range(2):
                        split_w_hi(act, ph, i, *span(ph, g))
            act.wait_ge(psum_free[1], plan.down2[1].freed(1, 1))
            act.dma_start(p_tok[:], a["p_2"].rearrange("l b (t p) c -> p (l b t) c", p=P)
                          ).then_inc(sem("p_full"), 16)
            act.dma_start(out_row[:], a["final_norm_w_2"].partition_broadcast(P)
                          ).then_inc(sem("out_row_full"), 16)
            squares_act(act, 6, x)
            split_act(act, "ple", p_hi, 2, False)
            split_act(act, "norm4", h_hi, KD, True)
            for ph, final in ((plan.ple, False), (plan.ple_last, True)):
                with turns(act, ph.iters) as i:
                    split_w_hi(act, ph, i, *span(ph, 0, final))
                    act.wait_ge(w_used, ph.done(i, 0))
                    act.wait_ge(sem("ple_added"), i + (4 if final else 1))
                    nc.scalar.activation(sig_p[:], psum[0][:], ACT.Sigmoid).then_inc(psum_free[0], 1)
                    split_w_hi(act, ph, i, *span(ph, 1, final))
            act.wait_ge(sem("ple_added"), 5)
            squares_act(act, 7, x)

        @block.vector
        def _(dve):
            chain = Chain(dve, "dve_order")
            dve.sem_inc(split_lo, 8)
            dve.sem_inc(psum_free[0], 1)
            dve.sem_inc(psum_free[1], 1)
            for b in range(4):
                dve.sem_inc(bank_free[b], 1)
            dve.sem_inc(sem("ada_used"), 4)
            dve.sem_inc(sem("ada_read"), 2)
            dve.sem_inc(sem("hid_ready"), 1)
            dve.sem_inc(sem("ple_added"), 1)
            dve.wait_ge(bank_full[0], filled("cols", 0))
            nc.vector.tensor_copy(cols[:, 0:N_ROWS], bank[:, 0, 0:N_ROWS]).then_inc(bank_free[0], 1)
            for b in range(4):
                dve.wait_ge(bank_full[b], filled("conv", b))
                nc.vector.tensor_copy(conv_cols[:, b, :], bank[:, b, 0:nconv]).then_inc(bank_free[b], 1)
            dve.wait_ge(bank_free[0], emptied("cols", 0))

            dve.wait_ge(sem("params"), 16 * (N_ALL - N_FIRST))
            chain(nc.vector.tensor_copy(pos_f[:], pos_i[:]))
            dve.wait_ge(sem("freqs"), 1)
            for t in range(TT):
                for s in range(2):
                    chain(nc.vector.tensor_scalar(rope[:, 0, s, t * ROT_HALF:(t + 1) * ROT_HALF],
                                                  invf[:], pos_f[:, t:t + 1], None, ALU.mult))
            for s in range(2):
                chain(nc.vector.tensor_scalar(rope[:, 1, s, :], rope[:, 0, s, :],
                                              float(1 / (2 * np.pi)), 0.25 * s, ALU.mult, ALU.add))
            chain(nc.vector.tensor_scalar(rope[:, 2], rope[:, 1], ROUNDER, None, ALU.add))
            chain(nc.vector.tensor_scalar(rope[:, 2], rope[:, 2], ROUNDER, None, ALU.subtract))
            src = 0
            for n, part in enumerate(TURN_PARTS):
                chain(nc.vector.scalar_tensor_tensor(rope[:, 3 + n % 2], rope[:, 2], -part,
                                                     rope[:, src], ALU.mult, ALU.add))
                src = 3 + n % 2
            chain(nc.vector.tensor_scalar(rope[:, src, 1, :], rope[:, src, 1, :], float(np.pi / 2),
                                          None, ALU.add))
            nc.vector.tensor_scalar(rope[:, 5], rope[:, src], 3.1415925, -3.1415925, ALU.min, ALU.max
                                    ).then_inc(sem("angles"), 1)
            l0 = ROW["hg_lower_bounds"]
            chain(nc.vector.tensor_tensor(lb[:, 0, :], cols[:, l0:l0 + HG_H],
                                          cols[:, l0 + HG_H:l0 + 2 * HG_H], ALU.max))
            for n in range(2):
                nc.vector.tensor_tensor(lb[:, 1 + n, :], cols[:, l0 + n * HG_H:l0 + (n + 1) * HG_H],
                                        lb[:, 0, :], ALU.subtract).then_inc(sem("lb_shifted"), 1)
            dve.wait_ge(sem("lb_exp"), 1)
            chain(nc.vector.tensor_tensor(lb[:, 0, :], lb[:, 3, :], lb[:, 4, :], ALU.add))
            chain(nc.vector.reciprocal(lb[:, 5, :], lb[:, 0, :]))
            chain(nc.vector.tensor_tensor(lb[:, 0, :], lb[:, 3, :], lb[:, 5, :], ALU.mult))
            chain(nc.vector.tensor_scalar(lb[:, 1, :], lb[:, 0, :], -1.0, 1.0, ALU.mult, ALU.add))

            for n, g0, as_rows in ADA:
                with turns(dve, n // 2) as i:
                    for gg in range(2):
                        g = g0 + 2 * i + gg
                        dve.wait_ge(sem("ada_summed"), g + 1)
                        for k in range(KD):
                            if k % KU == 0:
                                dve.wait_ge(ada_full[k // KU], 16 * (g + 1))
                            unit = ada_raw[:, k // KU, k % KU, :]
                            cc = cols[:, ROW["c"] + k:ROW["c"] + k + 1]
                            if k == 0:
                                ins = nc.vector.tensor_scalar(ada_acc[:, gg, :], unit, cc, None, ALU.mult)
                            else:
                                if k % KU == 0:
                                    dve.wait_ge(sem("ada_used"), 4 + 4 * g + k // KU)
                                else:
                                    dve.wait_ge(sem("ada_order"), 12 * g + 3 * (k // KU) + k % KU)
                                ins = nc.vector.scalar_tensor_tensor(ada_acc[:, gg, :], unit, cc,
                                                                     ada_acc[:, gg, :], ALU.mult, ALU.add)
                            ins.then_inc(sem("ada_used") if k % KU == KU - 1 else sem("ada_order"), 1)
                    for gg in range(2):
                        g = g0 + 2 * i + gg
                        dve.wait_ge(sem("ada_summed"), g + 3)
                        if as_rows:
                            dst = (gate_row if g0 == 8 else gate2_row)[:, bass.ds((2 * i + gg) * COLS, COLS)]
                            ins = nc.vector.tensor_tensor(dst, dst, bank[:, gg, :], ALU.mult)
                        else:
                            ins = nc.vector.tensor_copy(mod_cols[:, bass.ds(4 * g, 4)], bank[:, gg, 0:4])
                        ins.then_inc(sem("ada_read"), 1)
            dve.wait_ge(sem("ada_read"), 26)
            for n, name in enumerate(("g_pre_mix", "g_pre_ffn")):
                s0 = (3 * n + 1) * KD
                chain(nc.vector.scalar_tensor_tensor(a_cols[:, n, :], mod_cols[:, s0:s0 + KD], 1.0,
                                                     cols[:, ROW[name]:ROW[name] + KD],
                                                     ALU.add, ALU.mult))
            normed_dve(dve, 0)
            split_dve(dve, "norm0", h_hi, h_lo, KD, a_cols[:, 0, :], mod_cols[:, 0:KD])

            ph = plan.mix_in
            split_w_lo(dve, ph, 0, 0, 4)
            for g in range(len(ph.groups)):
                split_w_lo(dve, ph, 0, *span(ph, g))
                if 5 <= g < 9:
                    values_dve(dve, chain, 0, g - 5)
                if 4 <= g < 8:
                    softmax_dve(dve, chain, 0, g - 4, sm, band)

            for g in (5, 6):
                dve.wait_ge(psum_free[ph.pair[g]], ph.freed(0, g))
            for h in range(HG_H):
                ins = nc.vector.tensor_scalar(logf[:, h, :], logf[:, h, :], lb[:, 1, h:h + 1],
                                              lb[:, 0, h:h + 1], ALU.mult, ALU.add)
            chain(ins)
            nc.vector.tensor_scalar(key[:], logf[:], -1.0, 1.0, ALU.mult, ALU.add
                                    ).then_inc(sem("f_ready"), 1)
            dve.wait_ge(sem("f_ready"), 1)
            dve.wait_ge(sem("logf_ready"), 1)
            flat = logf[:].rearrange("p h t -> p (h t)")
            for n in range(4):
                seg = flat[:, n * COLS:(n + 1) * COLS]
                nc.vector.tensor_tensor_scan(seg, scan_keep[:], seg, 0.0, ALU.mult, ALU.add
                                             ).then_inc(sem("scanned"), 1)

            def pick(stage, sc, mask, nbanks):
                for b in range(nbanks):
                    dve.wait_ge(bank_full[b], filled(stage, b))
                    nc.vector.copy_predicated(
                        sc[:, 4 * b:4 * b + 4, :],
                        mask.bitcast(I32).unsqueeze(1).to_broadcast([P, 4, P]),
                        bank[:, b, :].rearrange("p (z t) -> p z t", z=4)).then_inc(bank_free[b], 1)

            def level_factors(n):
                half = LEVELS[n]
                dve.wait_ge(sem("level_exp"), n + 1)
                for part, other in ((slice(half, 2 * half), qs), (slice(0, half), key)):
                    v_ = fac[n % 2][:].rearrange("p h (b e) -> p (h b) e", e=2 * half)[:, :, part]
                    o_ = other[:].rearrange("p h (b e) -> p (h b) e", e=2 * half)[:, :, part]
                    nc.vector.tensor_tensor(v_, v_, o_, ALU.mult).then_inc(sem("level_fac"), 1)

            dve.wait_ge(sem("scores_zero"), 1)
            pick("diag0", scores, ident[:], 4)
            level_factors(0)
            for n in range(len(LEVELS)):
                if n + 1 < len(LEVELS):
                    level_factors(n + 1)
                dve.wait_ge(bank_free[3], fill(f"level{n}", 3))
                pick(f"level{n}", scores, level_mask[:, n, :], 4)
            dve.wait_ge(sem("decay_exp"), 1)
            nc.vector.tensor_copy(ends[:, 0], fac[0][:].rearrange("p h (c e) -> p h c e", e=CHUNK)
                                  [:, :, :, CHUNK - 1]).then_inc(sem("rec0_k_ready"), 1)
            nc.vector.tensor_tensor(qs[:], qs[:], fac[0][:], ALU.mult).then_inc(sem("rec0_k_ready"), 1)
            dve.wait_ge(sem("decay_exp"), 2)
            nc.vector.tensor_tensor(key[:], key[:], fac[1][:], ALU.mult).then_inc(sem("rec0_k_ready"), 1)
            dve.wait_ge(sem("rec0_k_ready"), 3)
            recurrence_dve(dve, 0)
            split_dve(dve, "heads0", a_hi, a_lo, KD)

            ph = plan.mix_gate
            with turns(dve, ph.iters) as i:
                for g in range(4):
                    split_w_lo(dve, ph, i, *span(ph, g))
                    if g % 2:
                        dve.wait_ge(psum_free[0], ph.freed(i, g - 1))
                        dve.wait_ge(w_used, ph.done(i, g))
                        dve.wait_ge(sem("merged_sum"), i + 1)
                        nc.vector.tensor_tensor((part_a, part_b)[g // 2][:], (sig_a, sig_b)[g // 2][:],
                                                psum[1][:], ALU.mult).then_inc(psum_free[1], 1)
            split_dve(dve, "merged", h_hi, h_lo, KD)
            ph = plan.mix_out
            with turns(dve, ph.iters) as i:
                for g in range(2):
                    split_w_lo(dve, ph, i, *span(ph, g))
            residual_dve(dve, chain, 1)
            normed_dve(dve, 2)
            split_dve(dve, "norm1", h_hi, h_lo, KD, a_cols[:, 1, :], mod_cols[:, 3 * KD:4 * KD])

            for part, (g0, n) in enumerate(FFN_PARTS):
                ph = plan.up1[part]
                with turns(dve, ph.iters) as i:
                    split_w_lo(dve, ph, i, *span(ph, 0))
                    split_w_lo(dve, ph, i, *span(ph, 1))
                    dve.wait_ge(psum_free[0], ph.freed(i, 0))
                    dve.wait_ge(w_used, ph.done(i, 1))
                    dve.wait_ge(sem("hid_hi"), g0 + i + 1)
                    nc.vector.tensor_tensor(hid[:], act_g[:],
                                            psum[1][:].rearrange("p b (f t) -> p (b f) t", t=TOK),
                                            ALU.mult).then_inc(psum_free[1], 1)
                    dve.wait_ge(sem("hid_hi"), g0 + i + 2)
                    nc.vector.tensor_tensor(hid_lo[:, bass.ds(4 * i, 4), :], hid[:],
                                            hid_hi[:, bass.ds(4 * i, 4), :].bitcast(F32), ALU.subtract
                                            ).then_inc(sem("hid_lo"), 1)
                ph = plan.down1[part]
                if part == 1:
                    for g in range(2):
                        dve.wait_ge(psum_free[g], plan.down1[0].freed(1, g))
                with turns(dve, ph.iters) as i:
                    for g in range(2):
                        split_w_lo(dve, ph, i, *span(ph, g))
                        if part == 1:
                            dve.wait_ge(w_used, ph.done(i, g))
                            y = tokbuf[:, :, bass.ds(i * 2 * COLS + g * COLS, COLS)]
                            nc.vector.tensor_tensor(y, y, psum[g][:], ALU.add).then_inc(psum_free[g], 1)
            dve.wait_ge(sem("gate2_back"), 16)
            residual_dve(dve, chain, 3)
            normed_dve(dve, 4)
            split_dve(dve, "norm2", h_hi, h_lo, KD, cols[:, ROW["norm_mix_w_2"]:ROW["norm_mix_w_2"] + KD])

            ph = plan.mix_in2
            for g in range(len(ph.groups)):
                split_w_lo(dve, ph, 0, *span(ph, g))
                if 7 <= g < 11:
                    values_dve(dve, chain, 1, g - 7)
                if 6 <= g < 10:
                    softmax_dve(dve, chain, 1, g - 6, sm2, chunked)

            for f in range(GLA_H):
                if f % 2 == 0:
                    dve.wait_ge(bank_full[f // 2], filled("gate", f // 2))
                bias = cols[:, ROW["b_gla_gate_2"] + f:ROW["b_gla_gate_2"] + f + 1]
                ins = nc.vector.tensor_scalar(k_end[:, f, :],
                                              bank[:, f // 2, (f % 2) * TOK:(f % 2 + 1) * TOK],
                                              bias, None, ALU.add)
                if f % 2:
                    ins.then_inc(bank_free[f // 2], 1)
            for b in range(2):
                dve.wait_ge(bank_free[b], emptied("gate", b))
            nc.vector.scalar_tensor_tensor(ebuf[0][:], k_end[:], -1.0, k_end[:], ALU.mult, ALU.max
                                           ).then_inc(sem("gate_abs"), 1)
            chain(nc.vector.tensor_scalar(k_end[:], k_end[:], 0.0, 1.0 / TAU, ALU.min, ALU.mult))
            dve.wait_ge(sem("gate_ln"), 1)
            chain(nc.vector.scalar_tensor_tensor(lg[:], ebuf[0][:], -1.0 / TAU, k_end[:],
                                                 ALU.mult, ALU.add))
            flat = lg[:].rearrange("p h t -> p (h t)")
            for n in range(2):
                seg = flat[:, n * COLS:(n + 1) * COLS]
                nc.vector.tensor_tensor_scan(seg, scan_keep[:], seg, 0.0, ALU.mult, ALU.add
                                             ).then_inc(sem("gla_sum"), 1)
            dve.wait_ge(sem("gla_sum"), 2)
            chunks = lg[:].rearrange("p h (c e) -> p (h c) e", e=CHUNK)
            nc.vector.tensor_tensor(
                k_end[:].rearrange("p h (c e) -> p (h c) e", e=CHUNK),
                chunks[:, :, CHUNK - 1:CHUNK].to_broadcast([P, GLA_H * TOK // CHUNK, CHUNK]), chunks,
                ALU.subtract).then_inc(sem("gla_diff"), 1)
            dve.wait_ge(sem("gla_exp"), 1)
            nc.vector.tensor_copy(ends[:, 1, 0:GLA_H], ebuf[0][:].rearrange(
                "p h (c e) -> p h c e", e=CHUNK)[:, :, :, CHUNK - 1]).then_inc(sem("gla_fac"), 1)
            nc.vector.scalar_tensor_tensor(qg[:], qg[:], GLA_DK ** -0.5, ebuf[0][:], ALU.mult, ALU.mult
                                           ).then_inc(sem("gla_fac"), 1)
            dve.wait_ge(sem("gla_exp"), 2)
            nc.vector.tensor_tensor(ebuf[1][:], ebuf[1][:], kg[:], ALU.mult).then_inc(sem("gla_fac"), 1)
            dve.wait_ge(sem("gla_exp"), 3)
            nc.vector.tensor_tensor(k_end[:], k_end[:], kg[:], ALU.mult).then_inc(sem("rec1_k_ready"), 1)
            dve.wait_ge(sem("scores2_zero"), 1)
            pick("gla", scores2, causal[:], 2)
            recurrence_dve(dve, 1)
            split_dve(dve, "heads1", h_hi, h_lo, KD)

            ph = plan.mix_out2
            with turns(dve, ph.iters) as i:
                for g in range(2):
                    split_w_lo(dve, ph, i, *span(ph, g))
                    dve.wait_ge(w_used, ph.done(i, g))
                    xs = x[:, :, bass.ds(i * 2 * COLS + g * COLS, COLS)]
                    nc.vector.tensor_tensor(xs, xs, psum[g][:], ALU.add).then_inc(psum_free[g], 1)
            normed_dve(dve, 5)
            split_dve(dve, "norm3", h_hi, h_lo, KD, cols[:, ROW["norm_ffn_w_2"]:ROW["norm_ffn_w_2"] + KD])

            for part, (g0, n) in enumerate(FFN_PARTS):
                ph = plan.up2[part]
                with turns(dve, ph.iters) as i:
                    for g in range(2):
                        split_w_lo(dve, ph, i, *span(ph, g))
                        dst = (act_g, act_u)[g]
                        dve.wait_ge(sem("conv_tap2"), 8 * (g0 + i) + 4 * g + 4)
                        for tap, back in ((1, 1), (0, 2)):
                            for f in range(4):
                                c = bass.ds((i + g0) * 4 + g * (FFN // P) + f, 1)
                                u = psum[g][:, f // 2, (f % 2) * TOK:(f % 2 + 1) * TOK - back]
                                ins = nc.vector.scalar_tensor_tensor(
                                    dst[:, f, back:], u, conv_cols[:, tap, c], dst[:, f, back:],
                                    ALU.mult, ALU.add)
                            if tap == 1:
                                ins.then_inc(sem("conv_tap1"), 1)
                                dve.wait_ge(sem("conv_tap1"), 2 * (g0 + i) + g + 1)
                        ins.then_inc(psum_free[g], 1)
                    dve.wait_ge(psum_free[1], ph.freed(i, 1))
                    dve.wait_ge(sem("gelu"), g0 + i + 1)
                    dve.wait_ge(sem("hid2_hi"), g0 + i + 1)
                    nc.vector.tensor_tensor(hid[:], act_g[:], act_u[:], ALU.mult
                                            ).then_inc(sem("hid_ready"), 1)
                    dve.wait_ge(sem("hid2_hi"), g0 + i + 2)
                    nc.vector.tensor_tensor(hid_lo[:, bass.ds(4 * i, 4), :], hid[:],
                                            hid_hi[:, bass.ds(4 * i, 4), :].bitcast(F32), ALU.subtract
                                            ).then_inc(sem("hid2_lo"), 1)
                ph = plan.down2[part]
                with turns(dve, ph.iters) as i:
                    for g in range(2):
                        split_w_lo(dve, ph, i, *span(ph, g))
                        dve.wait_ge(w_used, ph.done(i, g))
                        xs = x[:, :, bass.ds(i * 2 * COLS + g * COLS, COLS)]
                        nc.vector.tensor_tensor(xs, xs, psum[g][:], ALU.add).then_inc(psum_free[g], 1)
            split_dve(dve, "ple", p_hi, p_lo, 2)
            normed_dve(dve, 6)
            split_dve(dve, "norm4", h_hi, h_lo, KD, cols[:, ROW["norm_ple_w_2"]:ROW["norm_ple_w_2"] + KD])
            for ph, final, i0 in ((plan.ple, False, 0), (plan.ple_last, True, D // COLS - 1)):
                with turns(dve, ph.iters) as i:
                    split_w_lo(dve, ph, i, *span(ph, 0, final))
                    split_w_lo(dve, ph, i, *span(ph, 1, final))
                    dve.wait_ge(psum_free[0], ph.freed(i, 0))
                    dve.wait_ge(w_used, ph.done(i, 1))
                    nc.vector.tensor_tensor(sig_p[:], sig_p[:], psum[1][:], ALU.mult
                                            ).then_inc(psum_free[1], 1)
                    dve.wait_ge(psum_free[1], ph.freed(i, 1))
                    xs = x[:, :, bass.ds((i + i0) * COLS, COLS)]
                    nc.vector.tensor_tensor(xs, xs, sig_p[:], ALU.add).then_inc(sem("ple_added"), 1)
            dve.wait_ge(sem("out_row_full"), 16)
            dve.wait_ge(sem("rms"), 8)
            for t in range(TT):
                nc.vector.scalar_tensor_tensor(tokbuf[:, t, :], x[:, t, :], stats[:, 7, 2 + t:3 + t],
                                               out_row[:], ALU.mult, ALU.mult).then_inc(sem("result"), 1)

        @block.gpsimd
        def _(pool):
            chain = Chain(pool, "pool_order")
            pool.sem_inc(sem("merged_sum"), 1)

            def keep_where(view, base, channel, pattern, fill_value, op=ALU.is_ge):
                chain(nc.gpsimd.affine_select(out=view, in_=view, compare_op=op, fill=fill_value,
                                              base=base, pattern=pattern, channel_multiplier=channel))

            chain(nc.gpsimd.memset(ident[:], 0.0))
            nc.gpsimd.affine_select(out=ident[:], in_=ident[:], compare_op=ALU.not_equal, fill=1.0,
                                    base=0, pattern=[[-1, P]], channel_multiplier=1
                                    ).then_inc(sem("ident_ready"), 1)
            nc.gpsimd.memset(ones[:], 1.0).then_inc(sem("ones_ready"), 1)
            for f in range(ROT_HALF):
                ins = nc.gpsimd.memset(invf[:, f:f + 1], float(INV_FREQ[f]))
            ins.then_inc(sem("freqs"), 1)
            chain(nc.gpsimd.memset(minus_half[:], -0.5))
            rms_pool(pool, chain, 0)
            chain(nc.gpsimd.memset(band[:], 0.0))
            keep_where(band[:, 0:P], 0, 1, [[-1, P]], NEG)
            keep_where(band[:, P:2 * P], -1, -1, [[1, P]], NEG)
            keep_where(band[:, 2 * P:3 * P], 0, 1, [[-1, P]], NEG)
            chain(nc.gpsimd.memset(chunked[:], 0.0))
            keep_where(chunked[:, CHUNK:P], -CHUNK, 1, [[0, CHUNK]], NEG)
            keep_where(chunked[:, 2 * P + CHUNK:3 * P], -CHUNK, 1, [[0, CHUNK]], NEG)
            chain(nc.gpsimd.memset(level_mask[:], 0.0))
            for n, half in enumerate(LEVELS):
                blocks = P // (2 * half)
                view = level_mask[:, n, :].rearrange("p (b e) -> p b e", e=2 * half)[:, :, half:]
                chain(nc.gpsimd.memset(view, 1.0))
                keep_where(view, 0, 1, [[-2 * half, blocks], [0, half]], 0.0)
                keep_where(view, half - 1, -1, [[2 * half, blocks], [0, half]], 0.0)
            chain(nc.gpsimd.memset(causal[:], 1.0))
            view = causal[:].rearrange("p (b e) -> p b e", e=CHUNK)
            keep_where(view, 0, -1, [[CHUNK, 2], [1, CHUNK]], 0.0)
            keep_where(view, 0, 1, [[-CHUNK, 2], [0, CHUNK]], 0.0)
            chain(nc.gpsimd.memset(scan_keep[:], 1.0))
            chain(nc.gpsimd.memset(scan_keep[:].rearrange("p (c e) -> p c e", e=CHUNK)[:, :, 0:1], 0.0))
            pool.sem_inc(sem("masks_ready"), 1)

            pool.wait_ge(sem("trig"), 1)
            for g in range(3):
                pool.wait_ge(psum_free[plan.mix_in.pair[g]], plan.mix_in.freed(0, g))
            nh = ATT_H + 2 * KV_H
            for t in range(TT):
                one = qk_tok[:, t, :, 0:ROT_HALF]
                two = qk_tok[:, t, :, ROT_HALF:2 * ROT_HALF]
                sin = trig[:, 0, t, :].unsqueeze(1).to_broadcast([P, nh, ROT_HALF])
                cos = trig[:, 1, t, :].unsqueeze(1).to_broadcast([P, nh, ROT_HALF])
                for n, (v_, w_) in enumerate(((one, cos), (two, sin), (two, cos), (one, sin))):
                    chain(nc.gpsimd.tensor_tensor(rope_tmp[:, n], v_, w_, ALU.mult))
                nc.gpsimd.tensor_tensor(one, rope_tmp[:, 0], rope_tmp[:, 1], ALU.subtract
                                        ).then_inc(sem("roped"), 1)
                nc.gpsimd.tensor_tensor(two, rope_tmp[:, 2], rope_tmp[:, 3], ALU.add
                                        ).then_inc(sem("roped"), 1)
                pool.wait_ge(sem("roped"), 2 * t + 2)

            pool.wait_ge(bank_free[0], emptied("attn0_3", 0, 2))
            nc.gpsimd.memset(scores[:], 0.0).then_inc(sem("scores_zero"), 1)
            pool.wait_ge(sem("scanned"), 4)
            for n, half in enumerate(LEVELS):
                if n >= 2:
                    pool.wait_ge(bank_free[3], emptied(f"level{n - 2}", 3))
                nb = HG_H * TOK // (2 * half)
                b_ = logf[:].rearrange("p h (b e) -> p (h b) e", e=2 * half)
                f_ = fac[n % 2][:].rearrange("p h (b e) -> p (h b) e", e=2 * half)
                mid = b_[:, :, half - 1:half].to_broadcast([P, nb, half])
                nc.gpsimd.tensor_tensor(f_[:, :, half:], b_[:, :, half:], mid, ALU.subtract
                                        ).then_inc(sem("level_diff"), 1)
                nc.gpsimd.tensor_tensor(f_[:, :, 0:half], mid, b_[:, :, 0:half], ALU.subtract
                                        ).then_inc(sem("level_diff"), 1)
            for b in range(4):
                pool.wait_ge(bank_free[b], emptied(f"level{len(LEVELS) - 1}", b))
            chunks = logf[:].rearrange("p h (c e) -> p (h c) e", e=CHUNK)
            nc.gpsimd.tensor_tensor(
                fac[1][:].rearrange("p h (c e) -> p (h c) e", e=CHUNK),
                chunks[:, :, CHUNK - 1:CHUNK].to_broadcast([P, HG_H * TOK // CHUNK, CHUNK]), chunks,
                ALU.subtract).then_inc(sem("decay_diff"), 1)
            for g in (9, 10):
                pool.wait_ge(psum_free[plan.mix_in.pair[g]], plan.mix_in.freed(0, g))
            recurrence_pool(pool, chain, 0, hg_gain)

            ph = plan.mix_gate
            with turns(pool, ph.iters) as i:
                pool.wait_ge(psum_free[1], ph.freed(i, 3))
                nc.gpsimd.tensor_tensor(tokbuf[:, :, bass.ds(i * COLS, COLS)], part_a[:], part_b[:],
                                        ALU.add).then_inc(sem("merged_sum"), 1)
            for r in range(1, 5):
                rms_pool(pool, chain, r)
            chain(nc.gpsimd.memset(mirror[:], 0.0))
            nc.gpsimd.affine_select(out=mirror[:], in_=mirror[:], compare_op=ALU.not_equal, fill=1.0,
                                    base=-(P - 1), pattern=[[1, P]], channel_multiplier=1
                                    ).then_inc(sem("mirror_ready"), 1)
            pool.wait_ge(bank_free[0], emptied("attn1_3", 0, 2))
            nc.gpsimd.memset(scores2[:], 0.0).then_inc(sem("scores2_zero"), 1)
            for g in (9, 10):
                pool.wait_ge(psum_free[plan.mix_in2.pair[g]], plan.mix_in2.freed(0, g))
            recurrence_pool(pool, chain, 1, gla_gain)
            for r in range(5, 8):
                rms_pool(pool, chain, r)

        @block.tensor
        def _(pe):
            pe.sem_inc(w_used, 4)
            pe.sem_inc(sem("ada_summed"), 2)
            pe.wait_ge(sem("ident_ready"), 1)
            pe.wait_ge(sem("params_first"), 16 * N_FIRST)
            pe.wait_ge(bank_free[0], fill("cols", 0))
            pe.transpose(bank[:, 0, 0:N_ROWS], rows[0:N_ROWS, :], ident[0:N_ROWS, 0:N_ROWS]
                         ).then_inc(bank_full[0], 1)
            pe.wait_ge(sem("params"), 16 * (N_ALL - N_FIRST))
            for b in range(4):
                pe.wait_ge(bank_free[b], fill("conv", b))
                pe.transpose(bank[:, b, 0:nconv], conv_rows[:, b, :], ident[0:nconv, 0:nconv]
                             ).then_inc(bank_full[b], 1)

            pe.wait_ge(sem("ones_ready"), 1)
            for b in range(2):
                pe.wait_ge(bank_free[b], emptied("conv", b))
            for n, g0, as_rows in ADA:
                with turns(pe, n // 2) as i:
                    for gg in range(2):
                        g = g0 + 2 * i + gg
                        pe.wait_ge(ada_b_full[gg], 16 * (g0 // 2 + i + 1))
                        pe.wait_ge(sem("ada_used"), 4 + 4 * g + 4)
                        pe.wait_ge(sem("ada_read"), g + 1)
                        if as_rows:
                            pe.matmul(bank[:, gg, :], ones[:], ada_acc[:, gg, :], start=True, stop=False)
                            mm = pe.matmul(bank[:, gg, :], ones[0:1, :], ada_b[:, gg, :], start=False,
                                           stop=True)
                        else:
                            for f in range(4):
                                part = slice(f * P, (f + 1) * P)
                                pe.matmul(bank[:, gg, f:f + 1], ada_acc[:, gg, part], ones[:, 0:1],
                                          start=(f == 0), stop=False, skip_group_check=True)
                                mm = pe.matmul(bank[:, gg, f:f + 1], ada_b[:, gg, part], ones[0:1, 0:1],
                                               start=False, stop=(f == 3), skip_group_check=True)
                        mm.then_inc(sem("ada_summed"), 1)

            pe.wait_ge(sem("normed"), 2)
            transpose_pe(pe, "norm0", tokbuf, KD)
            split_done(pe, "norm0", KD, True)
            ph = plan.mix_in
            for g in range(len(ph.groups)):
                products(pe, ph, 0, g, h_hi, h_lo, transposed=3 <= g < 7)
                if g == 3:
                    pe.wait_ge(sem("roped"), 4)
                    for b in range(5):
                        pe.wait_ge(bank_free[b % 4], fill("rope", b % 4, b // 4))
                        for n in range(2):
                            for t in range(TT):
                                pair = 2 * b + n
                                mm = pe.transpose(
                                    bank[:, b % 4, (2 * n + t) * P:(2 * n + t + 1) * P],
                                    qk_tok[:, t, 2 * pair:2 * pair + 2, :].rearrange("p h d -> p (h d)"),
                                    ident[:])
                        mm.then_inc(bank_full[b % 4], 1)
                if 5 <= g < 9:
                    turn_pe(pe, 0, g - 5, sm)
                    values_pe(pe, 0, g - 5, pt, v_tok)
                if g == 4:
                    pe.wait_ge(bank_free[0], emptied("rope", 0, 1))
                    for b in range(1, 4):
                        pe.wait_ge(bank_free[b], emptied("rope", b, 0))
                    pe.wait_ge(sem("masks_ready"), 1)
                if 4 <= g < 8:
                    scores_pe(pe, 0, g - 4, q_t, k_t, lambda h: h // (ATT_H // KV_H))

            def gram(stage, stationary, moving, nbanks):
                for b in range(nbanks):
                    pe.wait_ge(bank_free[b], fill(stage, b))
                    for n in range(4):
                        z = 4 * b + n
                        part = slice((z % 2) * P, (z % 2 + 1) * P)
                        mm = pe.matmul(bank[:, b, n * P:(n + 1) * P], stationary[:, z // 2, part],
                                       moving[:, z // 2, part], start=(n == 0), stop=(n == 3),
                                       skip_group_check=True)
                    mm.then_inc(bank_full[b], 1)

            pe.wait_ge(sem("f_ready"), 1)
            for g in (3, 4):
                pe.wait_ge(psum_free[plan.mix_in.pair[g]], plan.mix_in.freed(0, g))
            gram("diag0", key, qs, 4)
            for n in range(len(LEVELS)):
                pe.wait_ge(sem("level_fac"), 2 * (n + 1))
                gram(f"level{n}", fac[n % 2], fac[n % 2], 4)
            for g in (7, 8):
                pe.wait_ge(psum_free[plan.mix_in.pair[g]], plan.mix_in.freed(0, g))
            recurrence_pe(pe, 0, 3)
            pe.wait_ge(sem("heads0_ready"), 1)
            transpose_pe(pe, "heads0", tokbuf, KD)
            split_done(pe, "heads0", KD, False)

            ph = plan.mix_gate
            with turns(pe, ph.iters) as i:
                products(pe, ph, i, 0, h_hi, h_lo)
                products(pe, ph, i, 1, a_hi, a_lo)
                products(pe, ph, i, 2, h_hi, h_lo)
                products(pe, ph, i, 3, a_hi, a_lo, k_first=ATT_W // P)
            pe.wait_ge(sem("merged_sum"), ph.iters + 1)
            transpose_pe(pe, "merged", tokbuf, KD)
            split_done(pe, "merged", KD, False)
            ph = plan.mix_out
            with turns(pe, ph.iters) as i:
                for g in range(2):
                    products(pe, ph, i, g, h_hi, h_lo)
            pe.wait_ge(sem("normed"), 4)
            transpose_pe(pe, "norm1", tokbuf, KD)
            split_done(pe, "norm1", KD, True)
            for part, (g0, n) in enumerate(FFN_PARTS):
                ph = plan.up1[part]
                with turns(pe, ph.iters) as i:
                    for g in range(2):
                        products(pe, ph, i, g, h_hi, h_lo, transposed=True)
                pe.wait_ge(sem("hid_lo"), g0 + n)
                ph = plan.down1[part]
                with turns(pe, ph.iters) as i:
                    for g in range(2):
                        products(pe, ph, i, g, hid_hi, hid_lo)
            pe.wait_ge(sem("normed"), 6)
            transpose_pe(pe, "norm2", tokbuf, KD)
            split_done(pe, "norm2", KD, True)

            ph = plan.mix_in2
            pe.wait_ge(sem("toep_full"), 16)
            pe.wait_ge(sem("mirror_ready"), 1)
            for g in range(len(ph.groups)):
                products(pe, ph, 0, g, h_hi, h_lo, transposed=g < 4 or g in (6, 7))
                if 7 <= g < 11:
                    turn_pe(pe, 1, g - 7, sm2)
                    values_pe(pe, 1, g - 7, pt2, va)
                if g == 6:
                    for n in range(6):
                        pe.wait_ge(psum_free[ph.pair[n]], ph.freed(0, n))
                if 6 <= g < 10:
                    scores_pe(pe, 1, g - 6, q2_t, k2_t, lambda h: h // 2)
            pe.wait_ge(psum_free[ph.pair[8]], ph.freed(0, 8))
            pe.wait_ge(bank_free[0], fill("low_rank", 0))
            for t in range(TT):
                mm = pe.matmul(bank[0:RANK, 0, t * P:(t + 1) * P], lr_tok[:, t, :], ident[:],
                               start=(t == 0), stop=(t == 1), skip_group_check=True)
            mm.then_inc(bank_full[0], 1)
            pe.wait_ge(bank_free[0], emptied("low_rank", 0))
            pe.wait_ge(sem("w_up_g_full"), 16)
            for f in range(GLA_H):
                if f % 2 == 0:
                    pe.wait_ge(bank_free[f // 2], fill("gate", f // 2))
                mm = pe.matmul(bank[:, f // 2, (f % 2) * TOK:(f % 2 + 1) * TOK],
                               w_up_g[:, f * P:(f + 1) * P], gate_lr[:], start=(f % 2 == 0),
                               stop=(f % 2 == 1), skip_group_check=True)
                if f % 2:
                    mm.then_inc(bank_full[f // 2], 1)
            pe.wait_ge(sem("gla_fac"), 3)
            gram("gla", ebuf[1], qg, 2)
            for g in (11, 12):
                pe.wait_ge(psum_free[ph.pair[g]], ph.freed(0, g))
            recurrence_pe(pe, 1, 1)
            pe.wait_ge(sem("heads1_ready"), 1)
            transpose_pe(pe, "heads1", tokbuf, KD)
            split_done(pe, "heads1", KD, False)
            ph = plan.mix_out2
            with turns(pe, ph.iters) as i:
                for g in range(2):
                    products(pe, ph, i, g, h_hi, h_lo)
            pe.wait_ge(sem("normed"), 8)
            transpose_pe(pe, "norm3", tokbuf, KD)
            split_done(pe, "norm3", KD, True)
            for part, (g0, n) in enumerate(FFN_PARTS):
                ph = plan.up2[part]
                with turns(pe, ph.iters) as i:
                    for g in range(2):
                        products(pe, ph, i, g, h_hi, h_lo, transposed=True)
                pe.wait_ge(sem("hid2_lo"), g0 + n)
                ph = plan.down2[part]
                with turns(pe, ph.iters) as i:
                    for g in range(2):
                        products(pe, ph, i, g, hid_hi, hid_lo)
            pe.wait_ge(sem("p_full"), 16)
            transpose_pe(pe, "ple", p_tok, 2)
            split_done(pe, "ple", 2, False)
            pe.wait_ge(sem("normed"), 10)
            transpose_pe(pe, "norm4", tokbuf, KD)
            split_done(pe, "norm4", KD, True)
            for ph in (plan.ple, plan.ple_last):
                with turns(pe, ph.iters) as i:
                    products(pe, ph, i, 0, h_hi, h_lo)
                    products(pe, ph, i, 1, p_hi, p_lo)


_INS = ["x", "c", "positions", "w_ada", "b_ada", "g_pre_mix", "g_post_mix", "g_pre_ffn",
        "g_post_ffn", "w_in", "attn_sinks", "w_attn_proj", "hg_lower_bounds", "hg_norm",
        "w_hgrn_proj", "w_out", "w_ffn_in", "w_ffn_out", "p_2", "norm_mix_w_2", "w_in_2",
        "att_rel_bias_2", "w_gla_gate_up_2", "b_gla_gate_2", "gla_norm_w_2", "w_out_2",
        "norm_ffn_w_2", "w_ffn_up_2", "w_ffn_conv_2", "b_ffn_conv_2", "w_ffn_down_2",
        "norm_ple_w_2", "w_ple_gate_2", "w_ple_proj_2", "final_norm_w_2"]


def kernel(**inputs):
    import numpy as _np
    import concourse.bacc as _bacc
    from concourse import mybir as _mybir
    from concourse.bass_utils import run_bass_kernel_spmd as _run

    nc = _bacc.Bacc("TRN2", target_bir_lowering=False, num_devices=1, dynamic_dma_scratch_size=1024)
    arrays, args = {}, {}
    for name in _INS:
        a = _np.ascontiguousarray(inputs[name])
        arrays[f"in_{name}_dram"] = a
        args[name] = nc.dram_tensor(f"in_{name}_dram", a.shape, _mybir.dt.from_np(a.dtype),
                                    kind="ExternalInput").ap()
    out = nc.dram_tensor("out_0_dram", (1, TOK, D), F32, kind="ExternalOutput").ap()
    build_program(nc, args, out)
    r = _run(nc, [arrays], core_ids=[0])
    return r.results[0]["out_0_dram"]
```

```python
from contextlib import ExitStack, contextmanager

import numpy as np

import concourse.bass as bass
from concourse import mybir
from concourse.alu_op_type import AluOpType as ALU

ACT = mybir.ActivationFunctionType
AX_X = mybir.AxisListType.X
F32 = mybir.dt.float32
F32R = mybir.dt.float32r
I32 = mybir.dt.int32

P = 128
TOK = 256
TT = TOK // P
D = 2048
KD = D // P
COLS = 512
KU = 4
EPS = 1e-6

ATT_H, KV_H, HD = 16, 2, 64
ATT_W, KV_W = ATT_H * HD, KV_H * HD
HG_H, HG_D = 8, 128
HG_W = HG_H * HG_D
CHUNK = 64
FFN = 5632
ROT_HALF = HD // 8
ROPE_THETA = 500000.0
Q0 = 0
KV0 = ATT_W
QH0 = KV0 + 2 * KV_W
FH0 = QH0 + HG_W
IH0 = FH0 + HG_W
GH0 = IH0 + HG_W
GA0 = GH0 + HG_W
GB0 = GA0 + D

A2 = D // 2
GLA_H, GLA_DV, GLA_DK = 4, 256, 128
RANK = 16
TAU = 16.0
PLE = 256
DIST = 256
QG0 = 3 * A2
KG0 = QG0 + GLA_H * GLA_DK
VG0 = KG0 + GLA_H * GLA_DK
RG0 = VG0 + A2
LR0 = RG0 + A2

NEG = -1.0e30
LOWEST = -3.0e38
LEVELS = [32, 16, 8, 4, 2, 1]

INV_FREQ = np.float32(ROPE_THETA) ** (-np.arange(0, 2 * ROT_HALF, 2, dtype=np.float32)
                                      / np.float32(2 * ROT_HALF))
ROUNDER = 12582912.0
TURN_PARTS = [6.28125, int((2 * np.pi - 6.28125) * 2 ** 21) / 2 ** 21]
TURN_PARTS.append(float(np.float32(2 * np.pi - sum(TURN_PARTS))))

FFN_PARTS = [(0, 6), (6, 5)]


class Phase:

    def __init__(self, plan, iters, groups, mod=None):
        self.iters, self.groups = iters, groups
        self.halves, self.units, self.end, self.items = [], [], [], []
        mod = mod or [0] * len(groups)
        self.mod_units = weight_units = 0
        self.split_at = []

        def mod_unit():
            self.items.append((2 * len(self.units), "mod", self.mod_units))
            self.units.append(("mod", self.mod_units, KU, COLS))
            self.split_at.append(None)
            self.mod_units += 1

        for g, (kt, cols) in enumerate(groups):
            left = mod[g]
            for k0 in range(0, kt, KU):
                j = len(self.units)
                self.units.append((g, k0, min(KU, kt - k0), cols))
                self.split_at.append(2 * weight_units)
                weight_units += 1
                for h in range(0, min(KU, kt - k0), 2):
                    self.items.append((2 * j + h // 2, "half", len(self.halves)))
                    self.halves.append((g, j, h // 2, k0 + h))
                if left and (g or k0 >= 2 * KU):
                    mod_unit()
                    left -= 1
            while left:
                mod_unit()
                left -= 1
            self.end.append(len(self.halves))
        self.mod_base = plan.mod_units
        plan.mod_units += iters * self.mod_units
        self.sums = [next(g for g in range(len(groups)) if sum(mod[:g + 1]) >= 4 * (n + 1))
                     for n in range(self.mod_units // 4)]
        self.buffers = 1 if iters > 1 and len(self.sums) == 1 else 2
        self.turn = -(-len(self.units) // 4) * 4
        self.n0 = plan.n
        plan.n += iters * self.turn
        self.split_turn = -(-weight_units // 2) * 4
        self.split0 = plan.split
        plan.split += iters * self.split_turn
        self.fill0, per = list(plan.fill), [0] * 4
        self.occ = []
        for j in range(len(self.units)):
            self.occ.append(per[j % 4])
            per[j % 4] += 1
        self.per = per
        plan.fill = [a + iters * b for a, b in zip(plan.fill, per)]
        self.q0, self.qper = list(plan.q), [0, 0]
        self.pair, self.use = [], []
        for g in range(len(groups)):
            self.pair.append(g % 2)
            self.use.append(self.qper[g % 2])
            self.qper[g % 2] += 1
        plan.q = [a + iters * b for a, b in zip(plan.q, self.qper)]

    def half(self, i, idx):
        if idx >= len(self.halves):
            i, idx = i + 1, idx - len(self.halves)
        g, j, h, _ = self.halves[idx]
        at = self.split_at[j] + h
        after = self.split_turn
        if idx + 1 < len(self.halves):
            after = self.split_at[self.halves[idx + 1][1]] + self.halves[idx + 1][2]
        full = 16 * (self.fill0[j % 4] + i * self.per[j % 4] + self.occ[j] + 1)
        return (self.split0 + i * self.split_turn + at, at % 4, after - at,
                2 * (self.n0 + i * self.turn + j) + h, j % 4, h, full, self.units[j][3])

    def vector_items(self, i, idx):
        if idx >= len(self.halves):
            i, idx = i + 1, idx - len(self.halves)
        at = next(n for n, x in enumerate(self.items) if x[1:] == ("half", idx))
        found = []
        while True:
            number, kind, n = self.items[at]
            after = self.items[at + 1][0] if at + 1 < len(self.items) else 2 * self.turn
            found.append((kind, i, n, number, after - number))
            at += 1
            if at == len(self.items) or self.items[at][1] == "half":
                return found

    def mod_done(self, i, n):
        number = next(x[0] for x in self.items if x[1:] == ("mod", 4 * n + 3))
        return 8 + 2 * (self.n0 + i * self.turn) + number + 1

    def mod_sum(self, i, n):
        return self.mod_base // 4 + i * len(self.sums) + n

    def unit_number(self, i, j):
        return self.n0 + i * self.turn + j

    def done(self, i, g):
        g_, j, h, _ = self.halves[self.end[g] - 1]
        return 4 + self.split0 + i * self.split_turn + self.split_at[j] + h + 1

    def free(self, i, g):
        p = self.pair[g]
        return 1 + self.q0[p] + i * self.qper[p] + self.use[g]

    def freed(self, i, g):
        return self.free(i, g) + 1


class Plan:
    def __init__(self):
        self.n, self.split, self.fill, self.q, self.mod_units = 0, 0, [0] * 4, [0, 0], 0
        full = (KD, COLS)
        self.mix_in = Phase(self, 1, [full, full, (KD, 2 * KV_W)] + [full] * 8,
                            mod=[4, 4, 2, 2, 4, 2, 2, 2, 2, 4, 4])
        self.mix_gate = Phase(self, D // COLS, [full, (ATT_W // P, COLS), full, (HG_W // P, COLS)])
        self.mix_out = Phase(self, D // COLS // 2, [full, full], mod=[4, 4])
        self.up1, self.down1 = [], []
        for _, n in FFN_PARTS:
            self.up1.append(Phase(self, n, [full, full]))
            self.down1.append(Phase(self, 2, [(4 * n, COLS), (4 * n, COLS)], mod=[0, 4]))
        self.mix_in2 = Phase(self, 1, [full] * 8 + [(KD, RANK)] + [full] * 4)
        self.mix_out2 = Phase(self, D // COLS // 2, [full, full])
        self.up2, self.down2 = [], []
        for _, n in FFN_PARTS:
            self.up2.append(Phase(self, n, [full, full]))
            self.down2.append(Phase(self, 2, [(4 * n, COLS), (4 * n, COLS)]))
        self.ple = Phase(self, 1, [full, (PLE // P, COLS)] * (D // COLS))


def bank_uses(plan):
    uses = [("cols", (1, 0, 0, 0)), ("conv", (1, 1, 1, 1)), ("norm0", (2, 2, 2, 2))]

    def hooks(r, phase, first):
        for g in range(len(phase.groups)):
            if r == 0 and g == first - 1:
                uses.append(("rope", (2, 1, 1, 1)))
            if first + 2 <= g < first + 6:
                uses.append((f"attn{r}_v{g - first - 2}", (1, 0, 0, 0)))
            if first + 1 <= g < first + 5:
                uses.append((f"attn{r}_t{g - first - 1}", (1, 1, 1, 1)))
            if first <= g < first + 4:
                uses.append((f"attn{r}_s{g - first}", (1, 1, 1, 1)))
            for n in range(phase.sums.count(g)):
                uses.append((f"mod_in{g}", (0, 0, 0, 1)))

    hooks(0, plan.mix_in, 4)
    uses += [("diag0", (1, 1, 1, 1))] + [(f"level{n}", (1, 1, 1, 1)) for n in range(len(LEVELS))] + [
        ("rec0_k", (1, 1, 1, 1)), ("rec0_u0", (1, 1, 0, 0)), ("rec0_u1", (0, 0, 1, 1)),
        ("rec0_u2", (1, 1, 0, 0)), ("rec0_o", (1, 1, 1, 1)),
        ("heads0", (2, 2, 2, 2)), ("merged", (2, 2, 2, 2)), ("mod_out", (0, 0, 0, 4)),
        ("norm1", (2, 2, 2, 2)), ("mod_down0", (0, 0, 0, 2)), ("mod_down1", (0, 0, 0, 2)),
        ("norm2", (2, 2, 2, 2))]
    hooks(1, plan.mix_in2, 6)
    return uses + [
        ("low_rank", (1, 0, 0, 0)), ("gate", (1, 1, 0, 0)), ("gla", (1, 1, 0, 0)),
        ("rec1_k", (1, 1, 0, 0)), ("rec1_u0", (1, 1, 0, 0)), ("rec1_u1", (0, 0, 1, 1)),
        ("rec1_u2", (1, 1, 0, 0)), ("rec1_o", (1, 1, 1, 1)),
        ("heads1", (2, 2, 2, 2)), ("norm3", (2, 2, 2, 2)), ("ple", (1, 0, 0, 0)),
        ("norm4", (2, 2, 2, 2))]


def bank_bases(plan):
    at, base = [0] * 4, {}
    for name, uses in bank_uses(plan):
        base[name] = tuple(at)
        at = [a + u for a, u in zip(at, uses)]
    return base


@contextmanager
def turns(eng, n):
    if n == 1:
        yield 0
    else:
        with eng.Fori(0, n) as i:
            yield i


def build_program(nc, a, out):
    plan = Plan()
    bank0 = bank_bases(plan)

    with ExitStack() as ctx:
        def sb(name, shape, dt=F32):
            return ctx.enter_context(nc.sbuf_tensor(name, shape, dt))

        sems = {}

        def sem(name):
            if name not in sems:
                sems[name] = ctx.enter_context(nc.semaphore(name))
            return sems[name]

        x = sb("x", [P, TT, D])
        tokbuf = sb("tokbuf", [P, TT, D])
        h_hi = sb("h_hi", [P, KD, TOK], F32R)
        h_lo = sb("h_lo", [P, KD, TOK], F32R)
        raw = sb("raw", [P, 4, KU, COLS])
        w_hi = sb("w_hi", [P, 4, 2, COLS], F32R)
        w_lo = sb("w_lo", [P, 4, 2, COLS], F32R)
        GATE0 = -(-nc.sbuf_base // 32) * 32
        gate_row = sb("gate_row", [P, D])
        tmp = sb("tmp", [P, 2, 2, TOK])
        ident = sb("ident", [P, P])
        ones = sb("ones", [P, P])
        cols = sb("cols", [P, P])
        mod_cols = sb("mod_cols", [P, 96])
        a_cols = sb("a_cols", [P, 2, KD])
        conv_cols = sb("conv_cols", [P, 4, 2 * FFN // P])
        band = sb("band", [P, 3 * P])
        chunked = sb("chunked", [P, 3 * P])
        level_mask = sb("level_mask", [P, len(LEVELS), P])
        causal = sb("causal", [P, P])
        scan_keep = sb("scan_keep", [P, COLS])
        stats = sb("stats", [P, 8, 4])
        minus_half = sb("minus_half", [P, 16])
        diag = sb("diag", [P, TT, P])
        trig = sb("trig", [P, 2, TT, ROT_HALF])
        sinks = sb("sinks", [P, ATT_H])
        hg_gain = sb("hg_gain", [P, HG_D])
        gla_gain = sb("gla_gain", [P, GLA_DV])
        lb = sb("lb", [P, 6, HG_H])
        mx = sb("mx", [P, 2, 4, TT, 4])
        nmx = sb("nmx", [P, 2, 4, TT, 4])
        rsum = sb("rsum", [P, 2, 4, TT, 4])
        esink = sb("esink", [P, 4, TT, 4])
        den = sb("den", [P, 2, 4, TT, 4])
        rden = sb("rden", [P, 2, 4, TT, 4])
        hstat = sb("hstat", [P, 2, 2, 16])
        ends = sb("ends", [P, 2, 8, TOK // CHUNK])
        ARENA_KB = 66
        ARENA0 = nc.sbuf_usable_end // 32 * 32 - ARENA_KB * 1024
        assert nc.sbuf_base <= ARENA0, (nc.sbuf_base, ARENA0, nc.sbuf_usable_end)

        def place(name, kb, shape, dt=F32):
            size = 4
            for n in shape[1:]:
                size *= n
            assert kb * 1024 + size <= ARENA_KB * 1024, name
            return nc.alloc_sbuf_tensor_at(name, shape, dt, offset=ARENA0 + int(kb * 1024))

        mod_acc = [nc.alloc_sbuf_tensor_at("mod_acc0", [P, 2, COLS], F32, offset=GATE0),
                   place("mod_acc1", 58, [P, 2, COLS])]
        mod_b = [nc.alloc_sbuf_tensor_at("mod_b0", [1, 2, COLS], F32, offset=GATE0 + 4096),
                 place("mod_b1", 62, [1, 2, COLS])]
        ada_raw = place("ada_raw", 0, [P, 4, KU, COLS])
        ada_acc = place("ada_acc", 32, [P, 2, COLS])
        ada_b = place("ada_b", 36, [1, 2, COLS])
        conv_rows = place("conv_rows", 48, [2 * FFN // P, 4, P])
        rows = place("rows", 51, [P, P])
        pos_i = place("pos_i", 53, [P, TT], I32)
        pos_f = place("pos_f", 53.25, [P, TT])
        invf = place("invf", 53.5, [P, ROT_HALF])
        rope = place("rope", 52, [P, 6, 2, TT * ROT_HALF])
        qs = place("qs", 0, [P, HG_H, TOK])
        key = place("key", 8, [P, HG_H, TOK])
        logf = place("logf", 16, [P, HG_H, TOK])
        vh = place("vh", 24, [P, TT, HG_W])
        q_t = place("q_t", 32, [P, ATT_H // 2, TOK])
        k_t = place("k_t", 40, [P, KV_H, TOK])
        sm = place("sm", 42, [P, 4, 3 * P])
        pt = place("pt", 48, [P, 4, 3 * P])
        qk_tok = place("qk_tok", 54, [P, TT, ATT_H + 2 * KV_H, HD])
        v_tok = place("v_tok", 64, [P, TT, KV_W])
        rope_tmp = place("rope_tmp", 8, [P, 4, ATT_H + 2 * KV_H, ROT_HALF])
        fac = [place("fac0", 42, [P, HG_H, TOK]), place("fac1", 58, [P, HG_H, TOK])]
        scores = place("scores", 50, [P, 16, P])
        kend_t = place("kend_t", 58, [P, 16, P])
        state = [place("state1", 16, [P, HG_W]), place("state2", 20, [P, HG_W]),
                 place("state3", 42, [P, HG_W])]
        a_hi = place("a_hi", 0, [P, KD, TOK], F32R)
        a_lo = place("a_lo", 16, [P, KD, TOK], F32R)
        sig_a = place("sig_a", 42, [P, TT, COLS])
        sig_b = place("sig_b", 46, [P, TT, COLS])
        part_a = place("part_a", 50, [P, TT, COLS])
        part_b = place("part_b", 54, [P, TT, COLS])
        junk = place("junk", 58, [P, D])
        hid_hi = place("hid_hi", 0, [P, 24, TOK], F32R)
        hid_lo = place("hid_lo", 24, [P, 24, TOK], F32R)
        act_g = place("act_g", 48, [P, 4, TOK])
        act_u = place("act_u", 52, [P, 4, TOK])
        hid = place("hid", 56, [P, 4, TOK])
        q2_t = place("q2_t", 0, [P, ATT_H // 2, TOK])
        k2_t = place("k2_t", 8, [P, ATT_H // 2, TOK])
        va = place("va", 16, [P, TT, A2])
        toep = place("toep", 24, [P, ATT_H, TOK])
        sm2 = place("sm2", 40, [P, 4, 3 * P])
        pt2 = place("pt2", 46, [P, 4, 3 * P])
        qg = place("qg", 52, [P, GLA_H, TOK])
        kg = place("kg", 56, [P, GLA_H, TOK])
        w_up_g = place("w_up_g", 60, [RANK, GLA_H * GLA_DK])
        gate_lr = place("gate_lr", 62, [RANK, TOK])
        mirror = place("mirror", 63, [P, P])
        lr_tok = place("lr_tok", 63.5, [P, TT, RANK])
        vg = place("vg", 24, [P, TT, A2])
        lg = place("lg", 0, [P, GLA_H, TOK])
        ebuf = [place("ebuf0", 4, [P, GLA_H, TOK]), place("ebuf1", 8, [P, GLA_H, TOK])]
        k_end = place("k_end", 12, [P, GLA_H, TOK])
        scores2 = place("scores2", 16, [P, 8, P])
        kend2_t = place("kend2_t", 20, [P, 8, P])
        state_2 = [place("state1_2", 32, [P, A2]), place("state2_2", 36, [P, A2]),
                   place("state3_2", 40, [P, A2])]
        p_tok = place("p_tok", 0, [P, TT, PLE])
        p_hi = place("p_hi", 2, [P, PLE // P, TOK], F32R)
        p_lo = place("p_lo", 4, [P, PLE // P, TOK], F32R)
        sig_p = place("sig_p", 8, [P, TT, COLS])
        out_row = place("out_row", 16, [P, D])

        psum = [ctx.enter_context(nc.psum_tensor(f"psum{n}", [P, 2, COLS], F32)) for n in range(2)]
        bank = ctx.enter_context(nc.psum_tensor("bank", [P, 4, COLS], F32))

        raw_full = [sem(f"raw_full{n}") for n in range(4)]
        split_hi, split_lo, w_used = sem("split_hi"), sem("split_lo"), sem("w_used")
        psum_free = [sem("psum_free0"), sem("psum_free1")]
        bank_full = [sem(f"bank_full{n}") for n in range(4)]
        bank_free = [sem(f"bank_free{n}") for n in range(4)]
        ada_full = [sem(f"ada_full{n}") for n in range(4)]
        ada_b_full = [sem(f"ada_b_full{n}") for n in range(2)]
        mod_b_full = [sem(f"mod_b_full{n}") for n in range(2)]
        MODS = [(plan.mix_in, 12, 0, "mod_in"), (plan.mix_out, 8, 1, "mod_out"),
                (plan.down1[0], 20, 1, "mod_down0"), (plan.down1[1], 22, 1, "mod_down1")]

        class Chain:

            def __init__(self, eng, name):
                self.eng, self.sem, self.n = eng, sem(name), 0

            def __call__(self, ins):
                ins.then_inc(self.sem, 1)
                self.n += 1
                self.eng.wait_ge(self.sem, self.n)

        def fill(name, b, k=0):
            return 1 + bank0[name][b] + k

        def filled(name, b, k=0):
            return bank0[name][b] + k + 1

        def emptied(name, b, k=0):
            return fill(name, b, k) + 1

        def mod_of(ph):
            return next(x[1:] for x in MODS if x[0] is ph)

        def mod_buffer(ph, n):
            return n % 2 if ph.buffers == 2 else 0

        def mod_bias_uses(ph, i, n):
            first, per = [0, 0], [0, 0]
            for other, *_ in MODS:
                now = [0, 0]
                for m in range(len(other.sums)):
                    now[mod_buffer(other, m)] += 1
                if other is ph:
                    per = now
                    break
                first = [f + other.iters * x for f, x in zip(first, now)]
            b = mod_buffer(ph, n)
            before = sum(mod_buffer(ph, m) == b for m in range(n))
            return first[b] + i * per[b] + before + 1

        def load_mod(sp, ph, i, j, q):
            g0, place_, _ = mod_of(ph)
            n = q // 4
            g = g0 + i * len(ph.sums) + n
            if q % 4 == 0:
                s_ = ph.mod_sum(i, n) + 1 - ph.buffers
                if ph.iters > 1 or s_ > 0:
                    sp.wait_ge(sem("mod_summed"), s_)
                if ph.iters > 1:
                    sp.sem_inc(sem("slot_seen"), 1)
                b = mod_buffer(ph, n)
                sp.dma_start(mod_b[place_][:, b, :], a["b_ada"][:, bass.ds(g * COLS, COLS)]
                             ).then_inc(mod_b_full[b], 16)
            sp.wait_ge(split_lo, 2 * ph.unit_number(i, j) + 2)
            if ph.iters > 1:
                sp.sem_inc(sem("slot_seen"), 1)
            sp.dma_start(raw[:, j % 4], cut(w_ada, (q % 4) * KU, KU, g * COLS, COLS)
                         ).then_inc(raw_full[j % 4], 16)

        def add_mod(dve, ph, i, q, number, inc):
            _, place_, _ = mod_of(ph)
            n = q // 4
            j = number // 2
            acc = mod_acc[place_][:, mod_buffer(ph, n), :]
            done = 3 * (ph.mod_base + i * ph.mod_units + q)
            dve.wait_ge(raw_full[j % 4], 16 * (ph.fill0[j % 4] + i * ph.per[j % 4] + ph.occ[j] + 1))
            if q % 4 == 0:
                s_ = ph.mod_sum(i, n) + 1 - ph.buffers
                if ph.iters > 1 or s_ > 0:
                    dve.wait_ge(sem("mod_summed"), s_)
            else:
                before = next(x[0] for x in ph.items if x[1:] == ("mod", q - 1))
                dve.wait_ge(split_lo, 8 + 2 * (ph.n0 + i * ph.turn) + before + 1)
            for k in range(KU):
                cc = cols[:, ROW["c"] + (q % 4) * KU + k:ROW["c"] + (q % 4) * KU + k + 1]
                if k:
                    dve.wait_ge(sem("mod_order"), done + k)
                if q % 4 == 0 and k == 0:
                    ins = nc.vector.tensor_scalar(acc, raw[:, j % 4, k, :], cc, None, ALU.mult)
                else:
                    ins = nc.vector.scalar_tensor_tensor(acc, raw[:, j % 4, k, :], cc, acc,
                                                         ALU.mult, ALU.add)
                if k < KU - 1:
                    ins.then_inc(sem("mod_order"), 1)
                else:
                    ins.then_inc(split_lo, inc)

        def sum_pe(pe, acc, bias, o, as_rows):
            if as_rows:
                pe.matmul(o, ones[:], acc, start=True, stop=False, skip_group_check=True)
                return pe.matmul(o, ones[0:1, :], bias, start=False, stop=True,
                                 skip_group_check=True)
            for f in range(4):
                part = slice(f * P, (f + 1) * P)
                pe.matmul(o[:, f:f + 1], acc[:, part], ones[:, 0:1], start=(f == 0), stop=False,
                          skip_group_check=True)
                mm = pe.matmul(o[:, f:f + 1], bias[:, part], ones[0:1, 0:1], start=False,
                               stop=(f == 3), skip_group_check=True)
            return mm

        def mod_bank(ph, i, n):
            name = mod_of(ph)[2]
            if name == "mod_in":
                return f"mod_in{ph.sums[n]}", 0
            return name, i * len(ph.sums) + n

        def mod_pe(pe, ph, i, g):
            g0, place_, _ = mod_of(ph)
            for n, due in enumerate(ph.sums):
                if due != g:
                    continue
                b = mod_buffer(ph, n)
                stage, k = mod_bank(ph, i, n)
                pe.wait_ge(split_lo, ph.mod_done(i, n))
                pe.wait_ge(mod_b_full[b], 16 * mod_bias_uses(ph, i, n))
                pe.wait_ge(bank_free[3], fill(stage, 3, k))
                o = bank[:, 3, :]
                sum_pe(pe, mod_acc[place_][:, b, :], mod_b[place_][:, b, :], o, g0 != 12
                       ).then_inc(bank_full[3], 1)
                pe.wait_ge(bank_full[3], filled(stage, 3, k))
                pe.sem_inc(sem("mod_summed"), 1)

        def mod_dve(dve, ph, i, g):
            g0, _, _ = mod_of(ph)
            for n, due in enumerate(ph.sums):
                if due != g:
                    continue
                stage, k = mod_bank(ph, i, n)
                dve.wait_ge(bank_full[3], filled(stage, 3, k))
                if g0 == 12:
                    ins = nc.vector.tensor_copy(mod_cols[:, 4 * (g0 + n):4 * (g0 + n + 1)],
                                                bank[:, 3, 0:4])
                else:
                    at = (g0 - 8) % 12 if g0 != 22 else 2
                    dst = gate_row[:, bass.ds((at + i * len(ph.sums) + n) * COLS, COLS)]
                    ins = nc.vector.tensor_tensor(dst, dst, bank[:, 3, :], ALU.mult)
                ins.then_inc(bank_free[3], 1)

        def load_phase(sp, ph, source):
            with turns(sp, ph.iters) as i:
                for j, (g, k0, nk, ncol) in enumerate(ph.units):
                    if g == "mod":
                        load_mod(sp, ph, i, j, k0)
                        continue
                    sp.wait_ge(split_lo, 2 * ph.unit_number(i, j) + 2)
                    if ph.iters > 1:
                        sp.sem_inc(sem("slot_seen"), 1)
                    sp.dma_start(raw[:, j % 4, 0:nk, 0:ncol], source(i, g, k0, nk, ncol)
                                 ).then_inc(raw_full[j % 4], 16)

        def split_w_hi(act, ph, i, first, last):
            for idx in range(first, last):
                m, slot, inc, _, rs, h, full, ncol = ph.half(i, idx)
                act.wait_ge(raw_full[rs], full)
                act.wait_ge(w_used, m + 1)
                nc.scalar.activation(w_hi[:, slot, :, 0:ncol], raw[:, rs, 2 * h:2 * h + 2, 0:ncol],
                                     ACT.Copy).then_inc(split_hi, inc)

        def split_w_lo(dve, ph, i, first, last):
            for idx in range(first, last):
                m, slot, _, _, rs, h, full, ncol = ph.half(i, idx)
                for kind, turn, n, number, inc in ph.vector_items(i, idx):
                    if kind == "mod":
                        add_mod(dve, ph, turn, n, number, inc)
                        continue
                    dve.wait_ge(split_hi, m + 1)
                    nc.vector.tensor_tensor(w_lo[:, slot, :, 0:ncol],
                                            raw[:, rs, 2 * h:2 * h + 2, 0:ncol],
                                            w_hi[:, slot, :, 0:ncol].bitcast(F32),
                                            ALU.subtract).then_inc(split_lo, inc)

        def span(ph, g, final=False):
            first = (ph.end[g - 1] if g else 0) + 4
            last = ph.end[g] + 4
            if final:
                first, last = min(first, len(ph.halves)), min(last, len(ph.halves))
            return first, last

        def products(pe, ph, i, g, hi, lo, k_first=0, transposed=False, ready=None):
            ps = psum[ph.pair[g]]
            pe.wait_ge(psum_free[ph.pair[g]], ph.free(i, g))
            start, stop = (ph.end[g - 1] if g else 0), ph.end[g]
            for idx in range(start, stop):
                _, slot, inc, m, _, _, _, ncol = ph.half(i, idx)
                pe.wait_ge(split_lo, 8 + m + 1)
                if ready:
                    tile_ready(pe, ready, (k_first + ph.halves[idx][3]) // 2)
                for kk in range(2):
                    k = k_first + ph.halves[idx][3] + kk
                    first = idx == start and kk == 0
                    last = idx == stop - 1 and kk == 1
                    wh, wl = w_hi[:, slot, kk, :], w_lo[:, slot, kk, :]
                    if not transposed:
                        for t in range(TT):
                            o = ps[:, t, 0:ncol]
                            xh, xl = hi[:, k, t * P:(t + 1) * P], lo[:, k, t * P:(t + 1) * P]
                            pe.matmul(o, xh, wh[:, 0:ncol], start=first, stop=False,
                                      skip_group_check=True)
                            pe.matmul(o, xh, wl[:, 0:ncol], start=False, stop=False,
                                      skip_group_check=True)
                            mm = pe.matmul(o, xl, wh[:, 0:ncol], start=False, stop=last,
                                           skip_group_check=True)
                    else:
                        for f in range(-(-ncol // P)):
                            n = min(P, ncol - f * P)
                            o = ps[0:n, f // 2, (f % 2) * TOK:(f % 2 + 1) * TOK]
                            fh, fl = wh[:, f * P:f * P + n], wl[:, f * P:f * P + n]
                            pe.matmul(o, fh, hi[:, k, :], start=first and f % 2 == 0, stop=False,
                                      skip_group_check=True)
                            pe.matmul(o, fh, lo[:, k, :], start=False, stop=False,
                                      skip_group_check=True)
                            mm = pe.matmul(o, fl, hi[:, k, :], start=False, stop=last,
                                           skip_group_check=True)
                mm.then_inc(w_used, inc)

        def transpose_pe(pe, stage, src, tiles, r=None):
            for b in range(tiles // 2):
                pe.wait_ge(bank_free[b % 4], fill(stage, b % 4, b // 4))
                for k in range(2):
                    for t in range(TT):
                        o = bank[:, b % 4, (2 * k + t) * P:(2 * k + t + 1) * P]
                        tile = src[:, t, (2 * b + k) * P:(2 * b + k + 1) * P]
                        if r is None:
                            mm = pe.transpose(o, tile, ident[:])
                        else:
                            mm = pe.matmul(o, tile, diag[:, t, :], start=(k == 0 and t == 0),
                                           stop=(k == 1 and t == 1), skip_group_check=True)
                mm.then_inc(bank_full[b % 4], 1)

        def split_act(act, stage, hi, tiles, gain=None, shift=None):
            for b in range(tiles // 2):
                if shift is not None:
                    act.wait_ge(sem(f"{stage}_scaled"), b + 1)
                    nc.scalar.activation(hi[:, 2 * b:2 * b + 2, :], tmp[:, b % 2, :, :], ACT.Copy
                                         ).then_inc(sem(f"{stage}_hi"), 1)
                    continue
                act.wait_ge(bank_full[b % 4], filled(stage, b % 4, b // 4))
                if gain is None:
                    nc.scalar.activation(hi[:, 2 * b:2 * b + 2, :],
                                         bank[:, b % 4, :].rearrange("p (k t) -> p k t", k=2),
                                         ACT.Copy).then_inc(sem(f"{stage}_hi"), 1)
                    continue
                for k in range(2):
                    f = 2 * b + k
                    nc.scalar.activation(hi[:, f, :], bank[:, b % 4, k * TOK:(k + 1) * TOK],
                                         ACT.Identity, scale=gain[:, f:f + 1]
                                         ).then_inc(sem(f"{stage}_hi"), 1)

        def split_dve(dve, stage, hi, lo, tiles, gain=None, shift=None):
            def lower(b):
                dve.wait_ge(sem(f"{stage}_hi"), b + 1)
                nc.vector.tensor_tensor(lo[:, 2 * b:2 * b + 2, :], tmp[:, b % 2, :, :],
                                        hi[:, 2 * b:2 * b + 2, :].bitcast(F32), ALU.subtract
                                        ).then_inc(bank_free[b % 4], 1)

            if shift is not None:
                for b in range(tiles // 2):
                    dve.wait_ge(bank_full[b % 4], filled(stage, b % 4, b // 4))
                    if b >= 2:
                        dve.wait_ge(bank_free[(b - 2) % 4], emptied(stage, (b - 2) % 4, (b - 2) // 4))
                    for k in range(2):
                        f = 2 * b + k
                        ins = nc.vector.tensor_scalar(
                            tmp[:, b % 2, k, :], bank[:, b % 4, k * TOK:(k + 1) * TOK],
                            gain[:, f:f + 1], shift[:, f:f + 1], ALU.mult, ALU.add)
                    ins.then_inc(sem(f"{stage}_scaled"), 1)
                    if b:
                        lower(b - 1)
                lower(tiles // 2 - 1)
                return
            for b in range(tiles // 2):
                if gain is None:
                    dve.wait_ge(sem(f"{stage}_hi"), b + 1)
                    nc.vector.tensor_tensor(lo[:, 2 * b:2 * b + 2, :],
                                            bank[:, b % 4, :].rearrange("p (k t) -> p k t", k=2),
                                            hi[:, 2 * b:2 * b + 2, :].bitcast(F32), ALU.subtract
                                            ).then_inc(bank_free[b % 4], 1)
                    continue
                dve.wait_ge(sem(f"{stage}_hi"), 2 * b + 2)
                for k in range(2):
                    f = 2 * b + k
                    ins = nc.vector.scalar_tensor_tensor(
                        lo[:, f, :], bank[:, b % 4, k * TOK:(k + 1) * TOK], gain[:, f:f + 1],
                        hi[:, f, :].bitcast(F32), ALU.mult, ALU.subtract)
                ins.then_inc(bank_free[b % 4], 1)

        def tile_ready(pe, stage, b):
            pe.wait_ge(bank_free[b % 4], emptied(stage, b % 4, b // 4))

        def squares_act(act, r, src):
            for t in range(TT):
                if r or t:
                    act.wait_ge(sem("squares"), 2 * r + t)
                nc.scalar.activation(junk[:], src[:, t, :], ACT.Square,
                                     accum_out=stats[:, r, t:t + 1]).then_inc(sem("squares"), 1)

        def rms_pool(pool, chain, r):
            pool.wait_ge(sem("squares"), 2 * (r + 1))
            chain(nc.gpsimd.tensor_scalar(stats[:, r, 2:4], stats[:, r, 0:2], 1.0 / D, EPS,
                                          ALU.mult, ALU.add))
            nc.gpsimd.tensor_tensor(stats[:, r, 2:4], stats[:, r, 2:4], minus_half[:, 0:2],
                                    ALU.pow).then_inc(sem("rms"), 1)

        def normed_dve(dve, r):
            dve.wait_ge(sem("rms"), r + 1)
            for t in range(TT):
                nc.vector.tensor_scalar(diag[:, t, :], ident[:], stats[:, r, 2 + t:3 + t], None,
                                        ALU.mult).then_inc(sem("normed"), 1)

        def residual_dve(dve, chain, r):
            dve.wait_ge(sem("rms"), r + 1)
            for t in range(TT):
                chain(nc.vector.scalar_tensor_tensor(tokbuf[:, t, :], tokbuf[:, t, :],
                                                     stats[:, r, 2 + t:3 + t], gate_row[:],
                                                     ALU.mult, ALU.mult))
                ins = nc.vector.tensor_tensor(x[:, t, :], x[:, t, :], tokbuf[:, t, :], ALU.add)
                ins.then_inc(sem("x_ready"), 1)

        def scores_pe(pe, r, b, q, k, k_tile):
            for hh in range(4):
                h = 4 * b + hh
                o = bank[:, hh, :]
                rows_ = slice(HD * (h % 2), HD * (h % 2) + HD)
                kk = k[rows_, k_tile(h), :]
                pe.wait_ge(bank_free[hh], fill(f"attn{r}_s{b}", hh))
                mm = pe.matmul(o[:, 0:P], q[rows_, h // 2, 0:P], kk[:, 0:P], start=True,
                               stop=(r == 0), skip_group_check=True)
                mm = pe.matmul(o[:, P:3 * P], q[rows_, h // 2, P:2 * P], kk, start=False,
                               stop=(r == 0), skip_group_check=True)
                if r == 1:
                    pe.matmul(o[:, 0:P], toep[:, h, 0:P], mirror[:], start=False, stop=False,
                              skip_group_check=True)
                    pe.matmul(o[:, P:2 * P], toep[:, h, P:2 * P], mirror[:], start=False,
                              stop=False, skip_group_check=True)
                    mm = pe.matmul(o[:, 2 * P:3 * P], toep[:, h, 0:P], mirror[:], start=False,
                                   stop=True, skip_group_check=True)
                mm.then_inc(bank_full[hh], 1)

        def softmax_dve(dve, chain, r, b, s, mask):
            for hh in range(4):
                h = 4 * b + hh
                dve.wait_ge(bank_full[hh], filled(f"attn{r}_s{b}", hh))
                start = sinks[:, h:h + 1] if r == 0 else LOWEST
                for t, part in ((0, slice(0, P)), (1, slice(P, 3 * P))):
                    ins = nc.vector.tensor_tensor_reduce(s[:, hh, part], bank[:, hh, part],
                                                         mask[:, part], 1.0, start, ALU.add, ALU.max,
                                                         mx[:, r, b, t, hh:hh + 1])
                ins.then_inc(bank_free[hh], 1)
            dve.wait_ge(bank_free[3], emptied(f"attn{r}_s{b}", 3))
            if r == 0:
                for t in range(TT):
                    nc.vector.tensor_tensor(esink[:, b, t, :], sinks[:, 4 * b:4 * b + 4],
                                            mx[:, r, b, t, :], ALU.subtract)
            nc.vector.tensor_scalar(nmx[:, r, b], mx[:, r, b], -1.0, None, ALU.mult
                                    ).then_inc(sem(f"attn{r}_max"), 1)

        def softmax_act(act, r, b, s):
            act.wait_ge(sem(f"attn{r}_max"), b + 1)
            for hh in range(4):
                for t, part in ((0, slice(0, P)), (1, slice(P, 3 * P))):
                    nc.scalar.activation(s[:, hh, part], s[:, hh, part], ACT.Exp,
                                         bias=nmx[:, r, b, t, hh:hh + 1],
                                         accum_out=rsum[:, r, b, t, hh:hh + 1]
                                         ).then_inc(sem(f"attn{r}_exp"), 1)
            if r == 0:
                nc.scalar.activation(esink[:, b], esink[:, b], ACT.Exp).then_inc(sem(f"attn{r}_exp"), 1)

        EXPS = [9, 8]

        def turn_pe(pe, r, b, s):
            pe.wait_ge(sem(f"attn{r}_exp"), EXPS[r] * (b + 1))
            for hh in range(4):
                pe.wait_ge(bank_free[hh], fill(f"attn{r}_t{b}", hh))
                for n in range(3):
                    mm = pe.transpose(bank[:, hh, n * P:(n + 1) * P], s[:, hh, n * P:(n + 1) * P],
                                      ident[:])
                mm.then_inc(bank_full[hh], 1)

        def turn_act(act, r, b, p_):
            if b:
                act.wait_ge(bank_full[0], filled(f"attn{r}_v{b - 1}", 0))
            for hh in range(4):
                act.wait_ge(bank_full[hh], filled(f"attn{r}_t{b}", hh))
                nc.scalar.activation(p_[:, hh, :], bank[:, hh, 0:3 * P], ACT.Copy
                                     ).then_inc(bank_free[hh], 1)

        def values_pe(pe, r, b, p_, v):
            for hh in range(4):
                pe.wait_ge(bank_free[hh], emptied(f"attn{r}_t{b}", hh))
            pe.wait_ge(bank_free[0], fill(f"attn{r}_v{b}", 0))
            for hh in range(4):
                c = (4 * b + hh) * HD if r == 1 else (4 * b + hh) // (ATT_H // KV_H) * HD
                lo_, hi_ = hh * HD, 4 * HD + hh * HD
                pe.matmul(bank[:, 0, lo_:lo_ + HD], p_[:, hh, 0:P], v[:, 0, c:c + HD],
                          start=(hh == 0), stop=False, skip_group_check=True)
                pe.matmul(bank[:, 0, hi_:hi_ + HD], p_[:, hh, P:2 * P], v[:, 0, c:c + HD],
                          start=False, stop=False, skip_group_check=True)
                mm = pe.matmul(bank[:, 0, hi_:hi_ + HD], p_[:, hh, 2 * P:3 * P], v[:, 1, c:c + HD],
                               start=False, stop=(hh == 3), skip_group_check=True)
            mm.then_inc(bank_full[0], 1)

        def values_dve(dve, chain, r, b):
            dve.wait_ge(sem(f"attn{r}_exp"), EXPS[r] * (b + 1))
            if r == 0:
                chain(nc.vector.tensor_tensor(den[:, r, b], rsum[:, r, b], esink[:, b], ALU.add))
            d = den if r == 0 else rsum
            chain(nc.vector.reciprocal(rden[:, r, b], d[:, r, b]))
            dve.wait_ge(bank_full[0], filled(f"attn{r}_v{b}", 0))
            for t in range(TT):
                ins = nc.vector.tensor_tensor(
                    tokbuf[:, t, 4 * b * HD:4 * (b + 1) * HD].rearrange("p (h d) -> p h d", h=4),
                    bank[:, 0, 4 * HD * t:4 * HD * (t + 1)].rearrange("p (h d) -> p h d", h=4),
                    rden[:, r, b, t, :].unsqueeze(2).to_broadcast([P, 4, HD]), ALU.mult)
            ins.then_inc(bank_free[0], 1)

        REC = [(HG_H, HG_D, qs, key, kend_t, scores, vh, state, fac[0]),
               (GLA_H, GLA_DV, qg, k_end, kend2_t, scores2, vg, state_2, ebuf[0])]

        def chunk_place(c):
            return c // 2, slice(CHUNK * (c % 2), CHUNK * (c % 2 + 1))

        def recurrence_pe(pe, r, ready):
            heads, dv, q, k, kt, sc, v, st, _ = REC[r]
            per_bank = COLS // dv
            pe.wait_ge(sem(f"rec{r}_k_ready"), ready)
            for b in range(2 * heads // 4):
                pe.wait_ge(bank_free[b], fill(f"rec{r}_k", b))
                for n in range(4):
                    z = 4 * b + n
                    mm = pe.transpose(bank[:, b, n * P:(n + 1) * P],
                                      k[:, z // 2, (z % 2) * P:(z % 2 + 1) * P], ident[:])
                mm.then_inc(bank_full[b], 1)
            for b in range(2 * heads // 4):
                pe.wait_ge(bank_free[b], emptied(f"rec{r}_k", b))
            for c in range(3):
                t, ps = chunk_place(c)
                for n in range(2):
                    b = 2 * (c % 2) + n
                    pe.wait_ge(bank_free[b], fill(f"rec{r}_u{c}", b))
                    for hh in range(per_bank):
                        h = n * per_bank + hh
                        mm = pe.matmul(bank[:, b, hh * dv:(hh + 1) * dv], kt[ps, 2 * h + t, :],
                                       v[ps, t, h * dv:(h + 1) * dv], start=(hh == 0),
                                       stop=(hh == per_bank - 1), skip_group_check=True)
                    mm.then_inc(bank_full[b], 1)
            for b in range(4):
                pe.wait_ge(bank_free[b], fill(f"rec{r}_o", b))
            for b in range(4):
                t, n = b // 2, b % 2
                for hh in range(per_bank):
                    h = n * per_bank + hh
                    part = slice(hh * dv, (hh + 1) * dv)
                    pe.matmul(bank[:, b, part], sc[:, 2 * h + t, :], v[:, t, h * dv:(h + 1) * dv],
                              start=(hh == 0), stop=False, skip_group_check=True)
                    for c in (2 * t, 2 * t + 1):
                        if c:
                            _, ps = chunk_place(c)
                            mm = pe.matmul(bank[ps, b, part], q[:, h, c * CHUNK:(c + 1) * CHUNK],
                                           st[c - 1][:, h * dv:(h + 1) * dv], start=False,
                                           stop=(hh == per_bank - 1), skip_group_check=True)
                mm.then_inc(bank_full[b], 1)

        def recurrence_act(act, r):
            heads, dv, _, _, kt, _, _, _, sq = REC[r]
            for b in range(2 * heads // 4):
                act.wait_ge(bank_full[b], filled(f"rec{r}_k", b))
                nc.scalar.activation(kt[:, 4 * b:4 * b + 4, :],
                                     bank[:, b, :].rearrange("p (z k) -> p z k", z=4), ACT.Copy
                                     ).then_inc(bank_free[b], 1)
            for b in range(4):
                act.wait_ge(bank_full[b], filled(f"rec{r}_o", b))
            nc.scalar.activation(junk[:], bank[:].rearrange("p b c -> p (b c)"), ACT.Square
                                 ).then_inc(sem(f"rec{r}_sq"), 1)

        def recurrence_dve(dve, r):
            heads, dv, _, _, _, _, _, st, _ = REC[r]
            per_bank = COLS // dv
            for c in range(3):
                for n in range(2):
                    b = 2 * (c % 2) + n
                    dve.wait_ge(bank_full[b], filled(f"rec{r}_u{c}", b))
                    part = slice(n * COLS, (n + 1) * COLS)
                    if c == 0:
                        ins = nc.vector.tensor_copy(st[0][:, part], bank[:, b, :])
                    else:
                        for hh in range(per_bank):
                            h = n * per_bank + hh
                            cols_ = slice(h * dv, (h + 1) * dv)
                            ins = nc.vector.scalar_tensor_tensor(
                                st[c][:, cols_], st[c - 1][:, cols_],
                                ends[:, r, h, c:c + 1],
                                bank[:, b, hh * dv:(hh + 1) * dv], ALU.mult, ALU.add)
                    ins.then_inc(bank_free[b], 1)
                    dve.wait_ge(bank_free[b], emptied(f"rec{r}_u{c}", b))
            dve.wait_ge(sem(f"rec{r}_sq"), 1)
            groups = TT * heads
            nc.vector.tensor_reduce(hstat[:, r, 0, 0:groups],
                                    junk[:].rearrange("p (g v) -> p g v", v=dv), AX_X, ALU.add
                                    ).then_inc(sem(f"rec{r}_sum"), 1)
            dve.wait_ge(sem(f"rec{r}_rms"), 1)
            for b in range(4):
                part = slice(b * COLS, (b + 1) * COLS)
                ins = nc.vector.tensor_tensor(
                    junk[:, part].rearrange("p (g v) -> p g v", v=dv),
                    bank[:, b, :].rearrange("p (g v) -> p g v", v=dv),
                    hstat[:, r, 1, b * per_bank:(b + 1) * per_bank].unsqueeze(2)
                    .to_broadcast([P, per_bank, dv]), ALU.mult)
                ins.then_inc(bank_free[b], 1)
            dve.wait_ge(bank_free[3], emptied(f"rec{r}_o", 3))
            nc.vector.tensor_tensor(tokbuf[:, :, D // 2:], junk[:].rearrange("p (t c) -> p t c", t=TT),
                                    tokbuf[:, :, D // 2:], ALU.mult).then_inc(sem(f"heads{r}_ready"), 1)

        def recurrence_pool(pool, chain, r, gain):
            heads, dv = REC[r][0], REC[r][1]
            for t in range(TT):
                g = tokbuf[:, t, D // 2:].rearrange("p (h v) -> p h v", v=dv)
                chain(nc.gpsimd.tensor_tensor(g, g, gain[:].unsqueeze(1).to_broadcast([P, heads, dv]),
                                              ALU.mult))
            pool.wait_ge(sem(f"rec{r}_sum"), 1)
            n = TT * heads
            chain(nc.gpsimd.tensor_scalar(hstat[:, r, 1, 0:n], hstat[:, r, 0, 0:n], 1.0 / dv, EPS,
                                          ALU.mult, ALU.add))
            nc.gpsimd.tensor_tensor(hstat[:, r, 1, 0:n], hstat[:, r, 1, 0:n], minus_half[:, 0:n],
                                    ALU.pow).then_inc(sem(f"rec{r}_rms"), 1)

        ADA = [(8, 0)]

        w_ada = a["w_ada"].rearrange("l (k p) c -> (l p) k c", p=P)

        def weights(name):
            return a[name].rearrange("l (k p) c -> (l p) k c", p=P)

        W_in, W_ap, W_hp, W_out = (weights(n) for n in ("w_in", "w_attn_proj", "w_hgrn_proj", "w_out"))
        W_fi, W_fo = weights("w_ffn_in"), weights("w_ffn_out")
        W_in2, W_out2, W_fu2, W_fd2 = (weights(n) for n in
                                       ("w_in_2", "w_out_2", "w_ffn_up_2", "w_ffn_down_2"))
        W_pg, W_pp = weights("w_ple_gate_2"), weights("w_ple_proj_2")

        def cut(w, k0, nk, c0, ncol):
            return w[:, k0:k0 + nk, bass.ds(c0, ncol)]

        PARAMS = []

        def param(dst, src):
            PARAMS.append((dst, src))

        tiles_of = lambda ap: ap.rearrange("l (k p) -> (l k) p", p=P)
        ROW = {}
        at = 0
        for name, n in (("c", KD), ("g_pre_mix", KD), ("g_pre_ffn", KD), ("norm_mix_w_2", KD),
                        ("norm_ffn_w_2", KD), ("norm_ple_w_2", KD), ("hg_lower_bounds", 2 * HG_H),
                        ("b_gla_gate_2", GLA_H)):
            ROW[name] = at
            param(rows[at:at + n, :], tiles_of(a[name]))
            at += n
        N_ROWS = at

        def gain_of(name):
            return cols[:, ROW[name]:ROW[name] + KD]

        param(x[:, :, :], a["x"].rearrange("b (t p) d -> p (b t) d", p=P))
        N_FIRST = len(PARAMS)
        nconv = 2 * FFN // P
        param(conv_rows[:, 0:3, :], a["w_ffn_conv_2"].rearrange("l t (j p) -> j (l t) p", p=P))
        param(conv_rows[:, 3, :], tiles_of(a["b_ffn_conv_2"]))
        ctx.enter_context(nc.allow_non_contiguous_dma(reason="positions, one number a partition"))
        param(pos_i[:], a["positions"].rearrange("b (t p) -> p (b t)", p=P))
        param(sinks[:], a["attn_sinks"][0, :].partition_broadcast(P))
        param(hg_gain[:], a["hg_norm"][0, :].partition_broadcast(P))
        param(gla_gain[:], a["gla_norm_w_2"][0, :].partition_broadcast(P))
        N_ALL = len(PARAMS)
        bias_tab = a["att_rel_bias_2"]

        block = ctx.enter_context(nc.Block())

        @block.sync
        def _(sp):
            for i in range(N_FIRST):
                sp.dma_start(*PARAMS[i]).then_inc(sem("params_first"), 16)
            group = 0
            for n, g0 in ADA:
                with turns(sp, n // 2) as i:
                    for gg in range(2):
                        g = g0 + 2 * i + gg
                        sp.wait_ge(sem("ada_summed"), g + 1)
                        sp.sem_inc(sem("slot_seen"), 1)
                        sp.dma_start(ada_b[:, gg, :], a["b_ada"][:, bass.ds(g * COLS, COLS)]
                                     ).then_inc(ada_b_full[gg], 16)
                        for u in range(4):
                            sp.wait_ge(sem("ada_used"), 4 * g + u + 1)
                            sp.sem_inc(sem("slot_seen"), 1)
                            sp.dma_start(ada_raw[:, u], cut(w_ada, u * KU, KU, g * COLS, COLS)
                                         ).then_inc(ada_full[u], 16)

            def mix_in_source(i, g, k0, nk, ncol):
                c0 = [Q0, Q0 + COLS, KV0, QH0, QH0 + COLS, FH0, FH0 + COLS, IH0, IH0 + COLS, GH0,
                      GH0 + COLS][g]
                return cut(W_in, k0, nk, c0, ncol)
            load_phase(sp, plan.mix_in, mix_in_source)
            load_phase(sp, plan.mix_gate, lambda i, g, k0, nk, ncol: cut(
                (W_in, W_ap, W_in, W_hp)[g], k0, nk, i * COLS + (GA0, 0, GB0, 0)[g], ncol))
            load_phase(sp, plan.mix_out, lambda i, g, k0, nk, ncol: cut(
                W_out, k0, nk, i * 2 * COLS + g * COLS, ncol))
            for part, (g0, n) in enumerate(FFN_PARTS):
                load_phase(sp, plan.up1[part], lambda i, g, k0, nk, ncol: cut(
                    W_fi, k0, nk, (i + g0) * COLS + g * FFN, ncol))
                if part == 0:
                    sp.wait_ge(sem("x_ready"), 2)
                    sp.dma_start(gate_row[:], a["g_post_ffn"][0, :].partition_broadcast(P)
                                 ).then_inc(sem("ffn_gain_full"), 16)
                load_phase(sp, plan.down1[part], lambda i, g, k0, nk, ncol: cut(
                    W_fo, 4 * g0 + k0, nk, i * 2 * COLS + g * COLS, ncol))

            def mix_in2_source(i, g, k0, nk, ncol):
                c0 = [0, COLS, A2, A2 + COLS, 2 * A2, 2 * A2 + COLS, QG0, KG0, LR0, RG0, RG0 + COLS,
                      VG0, VG0 + COLS][g]
                return cut(W_in2, k0, nk, c0, ncol)
            load_phase(sp, plan.mix_in2, mix_in2_source)
            load_phase(sp, plan.mix_out2, lambda i, g, k0, nk, ncol: cut(
                W_out2, k0, nk, i * 2 * COLS + g * COLS, ncol))
            for part, (g0, n) in enumerate(FFN_PARTS):
                load_phase(sp, plan.up2[part], lambda i, g, k0, nk, ncol: cut(
                    W_fu2, k0, nk, (i + g0) * COLS + g * FFN, ncol))
                load_phase(sp, plan.down2[part], lambda i, g, k0, nk, ncol: cut(
                    W_fd2, 4 * g0 + k0, nk, i * 2 * COLS + g * COLS, ncol))
            load_phase(sp, plan.ple, lambda i, g, k0, nk, ncol: cut(
                (W_pg, W_pp)[g % 2], k0, nk, g // 2 * COLS, ncol))
            o = out.rearrange("b (t p) d -> p (b t) d", p=P)
            for t in range(TT):
                sp.wait_ge(sem("result"), t + 1)
                sp.dma_start(o[:, t, :], tokbuf[:, t, :]).then_inc(sem("stored"), 16)
            sp.wait_ge(sem("stored"), 16 * TT)

        @block.scalar
        def _(act):
            for i in range(N_FIRST, N_ALL):
                act.dma_start(*PARAMS[i]).then_inc(sem("params"), 16)
            act.wait_ge(sem("angles"), 1)
            nc.scalar.activation(trig[:].rearrange("p s t f -> p s (t f)"), rope[:, 5],
                                 ACT.Sin).then_inc(sem("trig"), 1)
            act.wait_ge(sem("lb_shifted"), 2)
            nc.scalar.activation(lb[:, 3:5, :], lb[:, 1:3, :], ACT.Exp).then_inc(sem("lb_exp"), 1)
            act.wait_ge(sem("params_first"), 16 * N_FIRST)
            squares_act(act, 0, x)
            split_act(act, "norm0", h_hi, KD, a_cols[:, 0, :], mod_cols[:, 0:KD])
            ph = plan.mix_in
            split_w_hi(act, ph, 0, 0, 4)
            for g in range(len(ph.groups)):
                split_w_hi(act, ph, 0, *span(ph, g))
                act.wait_ge(w_used, ph.done(0, g))
                ps, free = psum[ph.pair[g]], psum_free[ph.pair[g]]
                if g < 2:
                    nc.scalar.activation(
                        qk_tok[:, :, 8 * g:8 * g + 8, :], ps[:].rearrange("p t (h d) -> p t h d", d=HD),
                        ACT.Copy, scale=HD ** -0.5).then_inc(free, 1)
                elif g == 2:
                    for t in range(TT):
                        for dup in range(2):
                            nc.scalar.activation(
                                qk_tok[:, t, ATT_H:, :].rearrange("p (k u) d -> p k u d", u=2)[:, :, dup, :],
                                ps[:, t, 0:KV_W].rearrange("p (k d) -> p k d", d=HD), ACT.Copy)
                    nc.scalar.activation(v_tok[:], ps[:, :, KV_W:2 * KV_W], ACT.Copy
                                         ).then_inc(free, 1)
                elif g < 5:
                    nc.scalar.activation(qs[:, 4 * (g - 3):4 * (g - 2), :].rearrange("p h t -> p (h t)"),
                                         ps[:].rearrange("p b c -> p (b c)"), ACT.Silu
                                         ).then_inc(free, 1)
                elif g < 7:
                    nc.scalar.activation(logf[:, 4 * (g - 5):4 * (g - 4), :].rearrange("p h t -> p (h t)"),
                                         ps[:].rearrange("p b c -> p (b c)"), ACT.Sigmoid
                                         ).then_inc(free, 1)
                elif g < 9:
                    nc.scalar.activation(vh[:, :, (g - 7) * COLS:(g - 6) * COLS], ps[:], ACT.Copy
                                         ).then_inc(free, 1)
                else:
                    nc.scalar.activation(tokbuf[:, :, D // 2 + (g - 9) * COLS:D // 2 + (g - 8) * COLS],
                                         ps[:], ACT.Sigmoid).then_inc(free, 1)
                if g == 3:
                    for b in range(5):
                        dst = q_t[:, 2 * b:2 * b + 2, :] if b < 4 else k_t[:]
                        act.wait_ge(bank_full[b % 4], filled("rope", b % 4, b // 4))
                        nc.scalar.activation(dst, bank[:, b % 4, :].rearrange("p (k t) -> p k t", k=2),
                                             ACT.Copy).then_inc(bank_free[b % 4], 1)
                if 5 <= g < 9:
                    turn_act(act, 0, g - 5, pt)
                if 4 <= g < 8:
                    softmax_act(act, 0, g - 4, sm)
            act.wait_ge(sem("f_ready"), 1)
            nc.scalar.activation(logf[:], logf[:], ACT.Ln).then_inc(sem("logf_ready"), 1)
            for n in range(len(LEVELS)):
                act.wait_ge(sem("level_diff"), 2 * (n + 1))
                nc.scalar.activation(fac[n % 2][:], fac[n % 2][:], ACT.Exp
                                     ).then_inc(sem("level_exp"), 1)
            for b in range(4):
                act.wait_ge(bank_free[b], emptied(f"level{len(LEVELS) - 1}", b))
            nc.scalar.activation(fac[0][:], logf[:], ACT.Exp).then_inc(sem("decay_exp"), 1)
            act.wait_ge(sem("decay_diff"), 1)
            nc.scalar.activation(fac[1][:], fac[1][:], ACT.Exp).then_inc(sem("decay_exp"), 1)
            recurrence_act(act, 0)
            act.wait_ge(sem("mod_summed"), len(plan.mix_in.sums))
            act.dma_start(gate_row[:], a["g_post_mix"][0, :].partition_broadcast(P)
                          ).then_inc(sem("mix_gain_full"), 16)
            split_act(act, "heads0", a_hi, KD)

            ph = plan.mix_gate
            with turns(act, ph.iters) as i:
                for g in range(4):
                    split_w_hi(act, ph, i, *span(ph, g))
                    if g % 2 == 0:
                        act.wait_ge(w_used, ph.done(i, g))
                        act.wait_ge(psum_free[1], ph.freed(i, g + 1) - 2)
                        nc.scalar.activation((sig_a, None, sig_b)[g][:], psum[0][:], ACT.Sigmoid
                                             ).then_inc(psum_free[0], 1)
            split_act(act, "merged", h_hi, KD)

            ph = plan.mix_out
            with turns(act, ph.iters) as i:
                for g in range(2):
                    split_w_hi(act, ph, i, *span(ph, g))
                    act.wait_ge(w_used, ph.done(i, g))
                    nc.scalar.activation(tokbuf[:, :, bass.ds(i * 2 * COLS + g * COLS, COLS)],
                                         psum[g][:], ACT.Copy).then_inc(psum_free[g], 1)
            act.wait_ge(psum_free[1], plan.mix_out.freed(1, 1))
            act.wait_ge(psum_free[0], plan.mix_out.freed(1, 0))
            act.wait_ge(sem("mod_summed"), 12)
            squares_act(act, 1, tokbuf)
            act.wait_ge(sem("x_ready"), 2)
            squares_act(act, 2, x)
            split_act(act, "norm1", h_hi, KD, a_cols[:, 1, :], mod_cols[:, 3 * KD:4 * KD])
            for part, (g0, n) in enumerate(FFN_PARTS):
                ph = plan.up1[part]
                n0 = g0
                with turns(act, ph.iters) as i:
                    split_w_hi(act, ph, i, *span(ph, 0))
                    act.wait_ge(w_used, ph.done(i, 0))
                    act.wait_ge(psum_free[1], ph.freed(i, 1) - 1)
                    nc.scalar.activation(act_g[:], psum[0][:].rearrange("p b (f t) -> p (b f) t", t=TOK),
                                         ACT.Silu).then_inc(psum_free[0], 1)
                    split_w_hi(act, ph, i, *span(ph, 1))
                    act.wait_ge(psum_free[1], ph.freed(i, 1))
                    nc.scalar.activation(hid_hi[:, bass.ds(i * 4, 4), :], hid[:], ACT.Copy
                                         ).then_inc(sem("hid_hi"), 1)
                ph = plan.down1[part]
                with turns(act, ph.iters) as i:
                    for g in range(2):
                        split_w_hi(act, ph, i, *span(ph, g))
                        if part == 0:
                            act.wait_ge(w_used, ph.done(i, g))
                            nc.scalar.activation(tokbuf[:, :, bass.ds(i * 2 * COLS + g * COLS, COLS)],
                                                 psum[g][:], ACT.Copy).then_inc(psum_free[g], 1)
            act.wait_ge(psum_free[1], plan.down1[1].freed(1, 1))
            act.wait_ge(sem("mod_summed"), 16)
            squares_act(act, 3, tokbuf)
            act.wait_ge(sem("x_ready"), 4)
            act.dma_start(toep[:], bass.AP(tensor=bias_tab.tensor, offset=DIST - (P - 1),
                                           ap=[[1, P], [2 * DIST + 1, ATT_H], [1, TOK]])
                          ).then_inc(sem("toep_full"), 16)
            squares_act(act, 4, x)
            split_act(act, "norm2", h_hi, KD, gain_of("norm_mix_w_2"))
            act.wait_ge(sem("rms"), 5)
            act.dma_start(w_up_g[:], a["w_gla_gate_up_2"][0]).then_inc(sem("w_up_g_full"), 16)

            ph = plan.mix_in2
            for g in range(len(ph.groups)):
                split_w_hi(act, ph, 0, *span(ph, g))
                act.wait_ge(w_used, ph.done(0, g))
                ps, free = psum[ph.pair[g]], psum_free[ph.pair[g]]
                flat = ps[:].rearrange("p b (f t) -> p (b f) t", t=TOK)
                if g < 2:
                    nc.scalar.activation(q2_t[:, 4 * g:4 * g + 4, :], flat, ACT.Copy,
                                         scale=HD ** -0.5).then_inc(free, 1)
                elif g < 4:
                    nc.scalar.activation(k2_t[:, 4 * (g - 2):4 * (g - 1), :], flat, ACT.Copy
                                         ).then_inc(free, 1)
                elif g < 6:
                    nc.scalar.activation(va[:, :, (g - 4) * COLS:(g - 3) * COLS], ps[:], ACT.Copy
                                         ).then_inc(free, 1)
                elif g == 6:
                    nc.scalar.activation(qg[:], flat, ACT.Copy).then_inc(free, 1)
                elif g == 7:
                    nc.scalar.activation(kg[:], flat, ACT.Copy).then_inc(free, 1)
                elif g == 8:
                    nc.scalar.activation(lr_tok[:], ps[:, :, 0:RANK], ACT.Copy).then_inc(free, 1)
                elif g < 11:
                    nc.scalar.activation(tokbuf[:, :, D // 2 + (g - 9) * COLS:D // 2 + (g - 8) * COLS],
                                         ps[:], ACT.Silu).then_inc(free, 1)
                else:
                    act.wait_ge(bank_full[3], filled("attn1_s3", 3))
                    nc.scalar.activation(vg[:, :, (g - 11) * COLS:(g - 10) * COLS], ps[:], ACT.Copy
                                         ).then_inc(free, 1)
                if 7 <= g < 11:
                    turn_act(act, 1, g - 7, pt2)
                if 6 <= g < 10:
                    softmax_act(act, 1, g - 6, sm2)
            act.wait_ge(bank_full[0], filled("low_rank", 0))
            nc.scalar.activation(gate_lr[:], bank[0:RANK, 0, 0:TOK], ACT.Copy).then_inc(bank_free[0], 1)
            act.wait_ge(sem("gate_abs"), 1)
            nc.scalar.activation(ebuf[0][:], ebuf[0][:], ACT.Exp, scale=-1.0).then_inc(sem("gate_exp"), 1)
            act.wait_ge(sem("gate_exp"), 1)
            nc.scalar.activation(ebuf[0][:], ebuf[0][:], ACT.Ln, bias=1.0).then_inc(sem("gate_ln"), 1)
            act.wait_ge(sem("gla_sum"), 2)
            nc.scalar.activation(ebuf[0][:], lg[:], ACT.Exp).then_inc(sem("gla_exp"), 1)
            nc.scalar.activation(ebuf[1][:], lg[:], ACT.Exp, scale=-1.0).then_inc(sem("gla_exp"), 1)
            act.wait_ge(sem("gla_diff"), 1)
            nc.scalar.activation(k_end[:], k_end[:], ACT.Exp).then_inc(sem("gla_exp"), 1)
            recurrence_act(act, 1)
            split_act(act, "heads1", h_hi, KD)
            ph = plan.mix_out2
            with turns(act, ph.iters) as i:
                for g in range(2):
                    split_w_hi(act, ph, i, *span(ph, g))
            act.wait_ge(psum_free[1], ph.freed(1, 1))
            squares_act(act, 5, x)
            split_act(act, "norm3", h_hi, KD, gain_of("norm_ffn_w_2"))
            for part, (g0, n) in enumerate(FFN_PARTS):
                ph = plan.up2[part]
                with turns(act, ph.iters) as i:
                    for g in range(2):
                        split_w_hi(act, ph, i, *span(ph, g))
                        act.wait_ge(w_used, ph.done(i, g))
                        if g == 0:
                            act.wait_ge(sem("hid_ready"), 1 + g0 + i)
                        dst = (act_g, act_u)[g]
                        for f in range(4):
                            c = bass.ds((i + g0) * 4 + g * (FFN // P) + f, 1)
                            nc.scalar.activation(dst[:, f, :], psum[g][:, f // 2, (f % 2) * TOK:(f % 2 + 1) * TOK],
                                                 ACT.Identity, scale=conv_cols[:, 2, c],
                                                 bias=conv_cols[:, 3, c]).then_inc(sem("conv_tap2"), 1)
                        if g == 0:
                            act.wait_ge(psum_free[0], ph.freed(i, 0))
                            nc.scalar.activation(act_g[:], act_g[:], ACT.Gelu_apprx_tanh
                                                 ).then_inc(sem("gelu"), 1)
                    act.wait_ge(sem("hid_ready"), 2 + g0 + i)
                    nc.scalar.activation(hid_hi[:, bass.ds(i * 4, 4), :], hid[:], ACT.Copy
                                         ).then_inc(sem("hid2_hi"), 1)
                ph = plan.down2[part]
                with turns(act, ph.iters) as i:
                    for g in range(2):
                        split_w_hi(act, ph, i, *span(ph, g))
            act.wait_ge(psum_free[1], plan.down2[1].freed(1, 1))
            act.dma_start(p_tok[:], a["p_2"].rearrange("l b (t p) c -> p (l b t) c", p=P)
                          ).then_inc(sem("p_full"), 16)
            act.dma_start(out_row[:], a["final_norm_w_2"].partition_broadcast(P)
                          ).then_inc(sem("out_row_full"), 16)
            squares_act(act, 6, x)
            split_act(act, "ple", p_hi, 2)
            split_act(act, "norm4", h_hi, KD, gain_of("norm_ple_w_2"))
            ph = plan.ple
            for g in range(len(ph.groups)):
                split_w_hi(act, ph, 0, *span(ph, g, True))
                if g % 2 == 0:
                    act.wait_ge(w_used, ph.done(0, g))
                    if g:
                        act.wait_ge(sem("ple_added"), g // 2)
                    nc.scalar.activation(sig_p[:], psum[0][:], ACT.Sigmoid).then_inc(psum_free[0], 1)
            act.wait_ge(sem("ple_added"), 4)
            squares_act(act, 7, x)

        @block.vector
        def _(dve):
            chain = Chain(dve, "dve_order")
            dve.sem_inc(split_lo, 8)
            dve.sem_inc(psum_free[0], 1)
            dve.sem_inc(psum_free[1], 1)
            for b in range(4):
                dve.sem_inc(bank_free[b], 1)
            dve.sem_inc(sem("ada_used"), 4)
            dve.sem_inc(sem("ada_read"), 2)
            dve.wait_ge(bank_full[0], filled("cols", 0))
            nc.vector.tensor_copy(cols[:, 0:N_ROWS], bank[:, 0, 0:N_ROWS]).then_inc(bank_free[0], 1)
            for b in range(4):
                dve.wait_ge(bank_full[b], filled("conv", b))
                nc.vector.tensor_copy(conv_cols[:, b, :], bank[:, b, 0:nconv]).then_inc(bank_free[b], 1)
            dve.wait_ge(bank_free[0], emptied("cols", 0))

            dve.wait_ge(sem("params"), 16 * (N_ALL - N_FIRST))
            chain(nc.vector.tensor_copy(pos_f[:], pos_i[:]))
            dve.wait_ge(sem("freqs"), 1)
            for t in range(TT):
                for s in range(2):
                    chain(nc.vector.tensor_scalar(rope[:, 0, s, t * ROT_HALF:(t + 1) * ROT_HALF],
                                                  invf[:], pos_f[:, t:t + 1], None, ALU.mult))
            for s in range(2):
                chain(nc.vector.tensor_scalar(rope[:, 1, s, :], rope[:, 0, s, :],
                                              float(1 / (2 * np.pi)), 0.25 * s, ALU.mult, ALU.add))
            chain(nc.vector.tensor_scalar(rope[:, 2], rope[:, 1], ROUNDER, None, ALU.add))
            chain(nc.vector.tensor_scalar(rope[:, 2], rope[:, 2], ROUNDER, None, ALU.subtract))
            src = 0
            for n, part in enumerate(TURN_PARTS):
                chain(nc.vector.scalar_tensor_tensor(rope[:, 3 + n % 2], rope[:, 2], -part,
                                                     rope[:, src], ALU.mult, ALU.add))
                src = 3 + n % 2
            chain(nc.vector.tensor_scalar(rope[:, src, 1, :], rope[:, src, 1, :], float(np.pi / 2),
                                          None, ALU.add))
            nc.vector.tensor_scalar(rope[:, 5], rope[:, src], 3.1415925, -3.1415925, ALU.min, ALU.max
                                    ).then_inc(sem("angles"), 1)
            l0 = ROW["hg_lower_bounds"]
            chain(nc.vector.tensor_tensor(lb[:, 0, :], cols[:, l0:l0 + HG_H],
                                          cols[:, l0 + HG_H:l0 + 2 * HG_H], ALU.max))
            for n in range(2):
                nc.vector.tensor_tensor(lb[:, 1 + n, :], cols[:, l0 + n * HG_H:l0 + (n + 1) * HG_H],
                                        lb[:, 0, :], ALU.subtract).then_inc(sem("lb_shifted"), 1)
            dve.wait_ge(sem("lb_exp"), 1)
            chain(nc.vector.tensor_tensor(lb[:, 0, :], lb[:, 3, :], lb[:, 4, :], ALU.add))
            chain(nc.vector.reciprocal(lb[:, 5, :], lb[:, 0, :]))
            chain(nc.vector.tensor_tensor(lb[:, 0, :], lb[:, 3, :], lb[:, 5, :], ALU.mult))
            chain(nc.vector.tensor_scalar(lb[:, 1, :], lb[:, 0, :], -1.0, 1.0, ALU.mult, ALU.add))

            for n, g0 in ADA:
                with turns(dve, n // 2) as i:
                    for gg in range(2):
                        g = g0 + 2 * i + gg
                        dve.wait_ge(sem("ada_summed"), g + 1)
                        for k in range(KD):
                            if k % KU == 0:
                                dve.wait_ge(ada_full[k // KU], 16 * (g + 1))
                            unit = ada_raw[:, k // KU, k % KU, :]
                            cc = cols[:, ROW["c"] + k:ROW["c"] + k + 1]
                            if k == 0:
                                ins = nc.vector.tensor_scalar(ada_acc[:, gg, :], unit, cc, None, ALU.mult)
                            else:
                                if k % KU == 0:
                                    dve.wait_ge(sem("ada_used"), 4 + 4 * g + k // KU)
                                else:
                                    dve.wait_ge(sem("ada_order"), 12 * g + 3 * (k // KU) + k % KU)
                                ins = nc.vector.scalar_tensor_tensor(ada_acc[:, gg, :], unit, cc,
                                                                     ada_acc[:, gg, :], ALU.mult, ALU.add)
                            ins.then_inc(sem("ada_used") if k % KU == KU - 1 else sem("ada_order"), 1)
                    for gg in range(2):
                        g = g0 + 2 * i + gg
                        dve.wait_ge(sem("ada_summed"), g + 3)
                        nc.vector.tensor_copy(mod_cols[:, bass.ds(4 * g, 4)], bank[:, gg, 0:4]
                                              ).then_inc(sem("ada_read"), 1)
            dve.wait_ge(sem("ada_read"), 10)

            def modulate_dve(n):
                s0 = (3 * n + 1) * KD
                at = ROW[("g_pre_mix", "g_pre_ffn")[n]]
                chain(nc.vector.scalar_tensor_tensor(a_cols[:, n, :], mod_cols[:, s0:s0 + KD], 1.0,
                                                     cols[:, at:at + KD], ALU.add, ALU.mult))

            modulate_dve(0)
            normed_dve(dve, 0)
            split_dve(dve, "norm0", h_hi, h_lo, KD, a_cols[:, 0, :], mod_cols[:, 0:KD])

            ph = plan.mix_in
            split_w_lo(dve, ph, 0, 0, 4)
            for g in range(len(ph.groups)):
                split_w_lo(dve, ph, 0, *span(ph, g))
                if 6 <= g < 10:
                    values_dve(dve, chain, 0, g - 6)
                if 4 <= g < 8:
                    softmax_dve(dve, chain, 0, g - 4, sm, band)
                mod_dve(dve, ph, 0, g)
            dve.wait_ge(bank_free[3], emptied(mod_bank(ph, 0, len(ph.sums) - 1)[0], 3))
            modulate_dve(1)

            for g in (5, 6):
                dve.wait_ge(psum_free[ph.pair[g]], ph.freed(0, g))
            for h in range(HG_H):
                ins = nc.vector.tensor_scalar(logf[:, h, :], logf[:, h, :], lb[:, 1, h:h + 1],
                                              lb[:, 0, h:h + 1], ALU.mult, ALU.add)
            chain(ins)
            nc.vector.tensor_scalar(key[:], logf[:], -1.0, 1.0, ALU.mult, ALU.add
                                    ).then_inc(sem("f_ready"), 1)
            dve.wait_ge(sem("f_ready"), 1)
            dve.wait_ge(sem("logf_ready"), 1)
            flat = logf[:].rearrange("p h t -> p (h t)")
            for n in range(4):
                seg = flat[:, n * COLS:(n + 1) * COLS]
                nc.vector.tensor_tensor_scan(seg, scan_keep[:], seg, 0.0, ALU.mult, ALU.add
                                             ).then_inc(sem("scanned"), 1)

            def pick(stage, sc, mask, nbanks):
                for b in range(nbanks):
                    dve.wait_ge(bank_full[b], filled(stage, b))
                    nc.vector.copy_predicated(
                        sc[:, 4 * b:4 * b + 4, :],
                        mask.bitcast(I32).unsqueeze(1).to_broadcast([P, 4, P]),
                        bank[:, b, :].rearrange("p (z t) -> p z t", z=4)).then_inc(bank_free[b], 1)

            def level_factors(n):
                half = LEVELS[n]
                dve.wait_ge(sem("level_exp"), n + 1)
                for part, other in ((slice(half, 2 * half), qs), (slice(0, half), key)):
                    v_ = fac[n % 2][:].rearrange("p h (b e) -> p (h b) e", e=2 * half)[:, :, part]
                    o_ = other[:].rearrange("p h (b e) -> p (h b) e", e=2 * half)[:, :, part]
                    nc.vector.tensor_tensor(v_, v_, o_, ALU.mult).then_inc(sem("level_fac"), 1)

            dve.wait_ge(sem("scores_zero"), 1)
            pick("diag0", scores, ident[:], 4)
            level_factors(0)
            for n in range(len(LEVELS)):
                if n + 1 < len(LEVELS):
                    level_factors(n + 1)
                dve.wait_ge(bank_free[3], fill(f"level{n}", 3))
                pick(f"level{n}", scores, level_mask[:, n, :], 4)
            dve.wait_ge(sem("decay_exp"), 1)
            nc.vector.tensor_copy(ends[:, 0], fac[0][:].rearrange("p h (c e) -> p h c e", e=CHUNK)
                                  [:, :, :, CHUNK - 1]).then_inc(sem("rec0_k_ready"), 1)
            nc.vector.tensor_tensor(qs[:], qs[:], fac[0][:], ALU.mult).then_inc(sem("rec0_k_ready"), 1)
            dve.wait_ge(sem("decay_exp"), 2)
            nc.vector.tensor_tensor(key[:], key[:], fac[1][:], ALU.mult).then_inc(sem("rec0_k_ready"), 1)
            dve.wait_ge(sem("rec0_k_ready"), 3)
            recurrence_dve(dve, 0)
            split_dve(dve, "heads0", a_hi, a_lo, KD)

            ph = plan.mix_gate
            with turns(dve, ph.iters) as i:
                for g in range(4):
                    split_w_lo(dve, ph, i, *span(ph, g))
                    if g % 2:
                        dve.wait_ge(psum_free[0], ph.freed(i, g - 1))
                        dve.wait_ge(w_used, ph.done(i, g))
                        dve.wait_ge(sem("merged_sum"), i + 1)
                        nc.vector.tensor_tensor((part_a, part_b)[g // 2][:], (sig_a, sig_b)[g // 2][:],
                                                psum[1][:], ALU.mult).then_inc(psum_free[1], 1)
            split_dve(dve, "merged", h_hi, h_lo, KD)
            ph = plan.mix_out
            with turns(dve, ph.iters) as i:
                for g in range(2):
                    split_w_lo(dve, ph, i, *span(ph, g))
                    if g == 0:
                        dve.wait_ge(sem("mix_gain_full"), 16)
                    mod_dve(dve, ph, i, g)
            dve.wait_ge(bank_free[3], emptied("mod_out", 3, 3))
            residual_dve(dve, chain, 1)
            normed_dve(dve, 2)
            split_dve(dve, "norm1", h_hi, h_lo, KD, a_cols[:, 1, :], mod_cols[:, 3 * KD:4 * KD])

            for part, (g0, n) in enumerate(FFN_PARTS):
                ph = plan.up1[part]
                with turns(dve, ph.iters) as i:
                    split_w_lo(dve, ph, i, *span(ph, 0))
                    split_w_lo(dve, ph, i, *span(ph, 1))
                    dve.wait_ge(psum_free[0], ph.freed(i, 0))
                    dve.wait_ge(w_used, ph.done(i, 1))
                    dve.wait_ge(sem("hid_lo"), g0 + i + 1)
                    nc.vector.tensor_tensor(hid[:], act_g[:],
                                            psum[1][:].rearrange("p b (f t) -> p (b f) t", t=TOK),
                                            ALU.mult).then_inc(psum_free[1], 1)
                ph = plan.down1[part]
                if part == 1:
                    for g in range(2):
                        dve.wait_ge(psum_free[g], plan.down1[0].freed(1, g))
                with turns(dve, ph.iters) as i:
                    for g in range(2):
                        split_w_lo(dve, ph, i, *span(ph, g))
                        if part == 1:
                            dve.wait_ge(w_used, ph.done(i, g))
                            y = tokbuf[:, :, bass.ds(i * 2 * COLS + g * COLS, COLS)]
                            nc.vector.tensor_tensor(y, y, psum[g][:], ALU.add).then_inc(psum_free[g], 1)
                        if g == 1:
                            dve.wait_ge(sem("ffn_gain_full"), 16)
                        mod_dve(dve, ph, i, g)
            dve.wait_ge(bank_free[3], emptied("mod_down1", 3, 1))
            residual_dve(dve, chain, 3)
            normed_dve(dve, 4)
            split_dve(dve, "norm2", h_hi, h_lo, KD, gain_of("norm_mix_w_2"))

            ph = plan.mix_in2
            for g in range(len(ph.groups)):
                split_w_lo(dve, ph, 0, *span(ph, g))
                if 8 <= g < 12:
                    values_dve(dve, chain, 1, g - 8)
                if 6 <= g < 10:
                    softmax_dve(dve, chain, 1, g - 6, sm2, chunked)

            for f in range(GLA_H):
                if f % 2 == 0:
                    dve.wait_ge(bank_full[f // 2], filled("gate", f // 2))
                bias = cols[:, ROW["b_gla_gate_2"] + f:ROW["b_gla_gate_2"] + f + 1]
                ins = nc.vector.tensor_scalar(k_end[:, f, :],
                                              bank[:, f // 2, (f % 2) * TOK:(f % 2 + 1) * TOK],
                                              bias, None, ALU.add)
                if f % 2:
                    ins.then_inc(bank_free[f // 2], 1)
            for b in range(2):
                dve.wait_ge(bank_free[b], emptied("gate", b))
            nc.vector.scalar_tensor_tensor(ebuf[0][:], k_end[:], -1.0, k_end[:], ALU.mult, ALU.max
                                           ).then_inc(sem("gate_abs"), 1)
            chain(nc.vector.tensor_scalar(k_end[:], k_end[:], 0.0, 1.0 / TAU, ALU.min, ALU.mult))
            dve.wait_ge(sem("gate_ln"), 1)
            chain(nc.vector.scalar_tensor_tensor(lg[:], ebuf[0][:], -1.0 / TAU, k_end[:],
                                                 ALU.mult, ALU.add))
            flat = lg[:].rearrange("p h t -> p (h t)")
            for n in range(2):
                seg = flat[:, n * COLS:(n + 1) * COLS]
                nc.vector.tensor_tensor_scan(seg, scan_keep[:], seg, 0.0, ALU.mult, ALU.add
                                             ).then_inc(sem("gla_sum"), 1)
            dve.wait_ge(sem("gla_sum"), 2)
            chunks = lg[:].rearrange("p h (c e) -> p (h c) e", e=CHUNK)
            nc.vector.tensor_tensor(
                k_end[:].rearrange("p h (c e) -> p (h c) e", e=CHUNK),
                chunks[:, :, CHUNK - 1:CHUNK].to_broadcast([P, GLA_H * TOK // CHUNK, CHUNK]), chunks,
                ALU.subtract).then_inc(sem("gla_diff"), 1)
            dve.wait_ge(sem("gla_exp"), 1)
            nc.vector.tensor_copy(ends[:, 1, 0:GLA_H], ebuf[0][:].rearrange(
                "p h (c e) -> p h c e", e=CHUNK)[:, :, :, CHUNK - 1]).then_inc(sem("gla_fac"), 1)
            nc.vector.scalar_tensor_tensor(qg[:], qg[:], GLA_DK ** -0.5, ebuf[0][:], ALU.mult, ALU.mult
                                           ).then_inc(sem("gla_fac"), 1)
            dve.wait_ge(sem("gla_exp"), 2)
            nc.vector.tensor_tensor(ebuf[1][:], ebuf[1][:], kg[:], ALU.mult).then_inc(sem("gla_fac"), 1)
            dve.wait_ge(sem("gla_exp"), 3)
            nc.vector.tensor_tensor(k_end[:], k_end[:], kg[:], ALU.mult).then_inc(sem("rec1_k_ready"), 1)
            dve.wait_ge(sem("scores2_zero"), 1)
            pick("gla", scores2, causal[:], 2)
            recurrence_dve(dve, 1)
            split_dve(dve, "heads1", h_hi, h_lo, KD)

            ph = plan.mix_out2
            with turns(dve, ph.iters) as i:
                for g in range(2):
                    split_w_lo(dve, ph, i, *span(ph, g))
                    dve.wait_ge(w_used, ph.done(i, g))
                    xs = x[:, :, bass.ds(i * 2 * COLS + g * COLS, COLS)]
                    nc.vector.tensor_tensor(xs, xs, psum[g][:], ALU.add).then_inc(psum_free[g], 1)
            normed_dve(dve, 5)
            split_dve(dve, "norm3", h_hi, h_lo, KD, gain_of("norm_ffn_w_2"))

            for part, (g0, n) in enumerate(FFN_PARTS):
                ph = plan.up2[part]
                with turns(dve, ph.iters) as i:
                    for g in range(2):
                        split_w_lo(dve, ph, i, *span(ph, g))
                        dst = (act_g, act_u)[g]
                        dve.wait_ge(sem("conv_tap2"), 8 * (g0 + i) + 4 * g + 4)
                        for tap, back in ((1, 1), (0, 2)):
                            for f in range(4):
                                c = bass.ds((i + g0) * 4 + g * (FFN // P) + f, 1)
                                u = psum[g][:, f // 2, (f % 2) * TOK:(f % 2 + 1) * TOK - back]
                                ins = nc.vector.scalar_tensor_tensor(
                                    dst[:, f, back:], u, conv_cols[:, tap, c], dst[:, f, back:],
                                    ALU.mult, ALU.add)
                            if tap == 1:
                                ins.then_inc(sem("conv_tap1"), 1)
                                dve.wait_ge(sem("conv_tap1"), 2 * (g0 + i) + g + 1)
                        ins.then_inc(psum_free[g], 1)
                ph = plan.down2[part]
                with turns(dve, ph.iters) as i:
                    for g in range(2):
                        split_w_lo(dve, ph, i, *span(ph, g))
                        dve.wait_ge(w_used, ph.done(i, g))
                        xs = x[:, :, bass.ds(i * 2 * COLS + g * COLS, COLS)]
                        nc.vector.tensor_tensor(xs, xs, psum[g][:], ALU.add).then_inc(psum_free[g], 1)
            split_dve(dve, "ple", p_hi, p_lo, 2)
            normed_dve(dve, 6)
            split_dve(dve, "norm4", h_hi, h_lo, KD, gain_of("norm_ple_w_2"))
            ph = plan.ple
            for g in range(len(ph.groups)):
                split_w_lo(dve, ph, 0, *span(ph, g, True))
                if g % 2:
                    dve.wait_ge(psum_free[0], ph.freed(0, g - 1))
                    dve.wait_ge(w_used, ph.done(0, g))
                    nc.vector.tensor_tensor(sig_p[:], sig_p[:], psum[1][:], ALU.mult
                                            ).then_inc(psum_free[1], 1)
                    dve.wait_ge(psum_free[1], ph.freed(0, g))
                    xs = x[:, :, g // 2 * COLS:(g // 2 + 1) * COLS]
                    nc.vector.tensor_tensor(xs, xs, sig_p[:], ALU.add).then_inc(sem("ple_added"), 1)
            dve.wait_ge(sem("out_row_full"), 16)
            dve.wait_ge(sem("rms"), 8)
            for t in range(TT):
                nc.vector.scalar_tensor_tensor(tokbuf[:, t, :], x[:, t, :], stats[:, 7, 2 + t:3 + t],
                                               out_row[:], ALU.mult, ALU.mult).then_inc(sem("result"), 1)

        @block.gpsimd
        def _(pool):
            chain = Chain(pool, "pool_order")
            pool.sem_inc(sem("merged_sum"), 1)
            pool.sem_inc(sem("hid_lo"), 1)
            pool.sem_inc(sem("hid2_lo"), 1)
            pool.sem_inc(sem("hid_ready"), 1)

            def hidden_lo(pool, i, g0, name):
                pool.wait_ge(sem(f"{name}_hi"), g0 + i + 1)
                nc.gpsimd.tensor_tensor(hid_lo[:, bass.ds(4 * i, 4), :], hid[:],
                                        hid_hi[:, bass.ds(4 * i, 4), :].bitcast(F32), ALU.subtract
                                        ).then_inc(sem(f"{name}_lo"), 1)


            def keep_where(view, base, channel, pattern, fill_value, op=ALU.is_ge):
                chain(nc.gpsimd.affine_select(out=view, in_=view, compare_op=op, fill=fill_value,
                                              base=base, pattern=pattern, channel_multiplier=channel))

            chain(nc.gpsimd.memset(ident[:], 0.0))
            nc.gpsimd.affine_select(out=ident[:], in_=ident[:], compare_op=ALU.not_equal, fill=1.0,
                                    base=0, pattern=[[-1, P]], channel_multiplier=1
                                    ).then_inc(sem("ident_ready"), 1)
            nc.gpsimd.memset(ones[:], 1.0).then_inc(sem("ones_ready"), 1)
            for f in range(ROT_HALF):
                ins = nc.gpsimd.memset(invf[:, f:f + 1], float(INV_FREQ[f]))
            ins.then_inc(sem("freqs"), 1)
            chain(nc.gpsimd.memset(minus_half[:], -0.5))
            rms_pool(pool, chain, 0)
            chain(nc.gpsimd.memset(band[:], 0.0))
            keep_where(band[:, 0:P], 0, 1, [[-1, P]], NEG)
            keep_where(band[:, P:2 * P], -1, -1, [[1, P]], NEG)
            keep_where(band[:, 2 * P:3 * P], 0, 1, [[-1, P]], NEG)
            chain(nc.gpsimd.memset(chunked[:], 0.0))
            keep_where(chunked[:, CHUNK:P], -CHUNK, 1, [[0, CHUNK]], NEG)
            keep_where(chunked[:, 2 * P + CHUNK:3 * P], -CHUNK, 1, [[0, CHUNK]], NEG)
            chain(nc.gpsimd.memset(level_mask[:], 0.0))
            for n, half in enumerate(LEVELS):
                blocks = P // (2 * half)
                view = level_mask[:, n, :].rearrange("p (b e) -> p b e", e=2 * half)[:, :, half:]
                chain(nc.gpsimd.memset(view, 1.0))
                keep_where(view, 0, 1, [[-2 * half, blocks], [0, half]], 0.0)
                keep_where(view, half - 1, -1, [[2 * half, blocks], [0, half]], 0.0)
            chain(nc.gpsimd.memset(causal[:], 1.0))
            view = causal[:].rearrange("p (b e) -> p b e", e=CHUNK)
            keep_where(view, 0, -1, [[CHUNK, 2], [1, CHUNK]], 0.0)
            keep_where(view, 0, 1, [[-CHUNK, 2], [0, CHUNK]], 0.0)
            chain(nc.gpsimd.memset(scan_keep[:], 1.0))
            chain(nc.gpsimd.memset(scan_keep[:].rearrange("p (c e) -> p c e", e=CHUNK)[:, :, 0:1], 0.0))
            pool.sem_inc(sem("masks_ready"), 1)

            pool.wait_ge(sem("trig"), 1)
            for g in range(3):
                pool.wait_ge(psum_free[plan.mix_in.pair[g]], plan.mix_in.freed(0, g))
            nh = ATT_H + 2 * KV_H
            for t in range(TT):
                one = qk_tok[:, t, :, 0:ROT_HALF]
                two = qk_tok[:, t, :, ROT_HALF:2 * ROT_HALF]
                sin = trig[:, 0, t, :].unsqueeze(1).to_broadcast([P, nh, ROT_HALF])
                cos = trig[:, 1, t, :].unsqueeze(1).to_broadcast([P, nh, ROT_HALF])
                for n, (v_, w_) in enumerate(((one, cos), (two, sin), (two, cos), (one, sin))):
                    chain(nc.gpsimd.tensor_tensor(rope_tmp[:, n], v_, w_, ALU.mult))
                nc.gpsimd.tensor_tensor(one, rope_tmp[:, 0], rope_tmp[:, 1], ALU.subtract
                                        ).then_inc(sem("roped"), 1)
                nc.gpsimd.tensor_tensor(two, rope_tmp[:, 2], rope_tmp[:, 3], ALU.add
                                        ).then_inc(sem("roped"), 1)
                pool.wait_ge(sem("roped"), 2 * t + 2)

            pool.wait_ge(bank_free[0], emptied("attn0_v3", 0))
            nc.gpsimd.memset(scores[:], 0.0).then_inc(sem("scores_zero"), 1)
            pool.wait_ge(sem("scanned"), 4)
            for n, half in enumerate(LEVELS):
                if n >= 2:
                    pool.wait_ge(bank_free[3], emptied(f"level{n - 2}", 3))
                nb = HG_H * TOK // (2 * half)
                b_ = logf[:].rearrange("p h (b e) -> p (h b) e", e=2 * half)
                f_ = fac[n % 2][:].rearrange("p h (b e) -> p (h b) e", e=2 * half)
                mid = b_[:, :, half - 1:half].to_broadcast([P, nb, half])
                nc.gpsimd.tensor_tensor(f_[:, :, half:], b_[:, :, half:], mid, ALU.subtract
                                        ).then_inc(sem("level_diff"), 1)
                nc.gpsimd.tensor_tensor(f_[:, :, 0:half], mid, b_[:, :, 0:half], ALU.subtract
                                        ).then_inc(sem("level_diff"), 1)
            for b in range(4):
                pool.wait_ge(bank_free[b], emptied(f"level{len(LEVELS) - 1}", b))
            chunks = logf[:].rearrange("p h (c e) -> p (h c) e", e=CHUNK)
            nc.gpsimd.tensor_tensor(
                fac[1][:].rearrange("p h (c e) -> p (h c) e", e=CHUNK),
                chunks[:, :, CHUNK - 1:CHUNK].to_broadcast([P, HG_H * TOK // CHUNK, CHUNK]), chunks,
                ALU.subtract).then_inc(sem("decay_diff"), 1)
            for g in (9, 10):
                pool.wait_ge(psum_free[plan.mix_in.pair[g]], plan.mix_in.freed(0, g))
            recurrence_pool(pool, chain, 0, hg_gain)

            ph = plan.mix_gate
            with turns(pool, ph.iters) as i:
                pool.wait_ge(psum_free[1], ph.freed(i, 3))
                nc.gpsimd.tensor_tensor(tokbuf[:, :, bass.ds(i * COLS, COLS)], part_a[:], part_b[:],
                                        ALU.add).then_inc(sem("merged_sum"), 1)
            rms_pool(pool, chain, 1)
            rms_pool(pool, chain, 2)
            for part, (g0, n) in enumerate(FFN_PARTS):
                with turns(pool, n) as i:
                    hidden_lo(pool, i, g0, "hid")
            rms_pool(pool, chain, 3)
            rms_pool(pool, chain, 4)
            chain(nc.gpsimd.memset(mirror[:], 0.0))
            nc.gpsimd.affine_select(out=mirror[:], in_=mirror[:], compare_op=ALU.not_equal, fill=1.0,
                                    base=-(P - 1), pattern=[[1, P]], channel_multiplier=1
                                    ).then_inc(sem("mirror_ready"), 1)
            pool.wait_ge(bank_free[0], emptied("attn1_v3", 0))
            nc.gpsimd.memset(scores2[:], 0.0).then_inc(sem("scores2_zero"), 1)
            for g in (9, 10):
                pool.wait_ge(psum_free[plan.mix_in2.pair[g]], plan.mix_in2.freed(0, g))
            recurrence_pool(pool, chain, 1, gla_gain)
            rms_pool(pool, chain, 5)
            for part, (g0, n) in enumerate(FFN_PARTS):
                ph = plan.up2[part]
                with turns(pool, n) as i:
                    pool.wait_ge(psum_free[1], ph.freed(i, 1))
                    pool.wait_ge(sem("gelu"), g0 + i + 1)
                    pool.wait_ge(sem("hid2_lo"), g0 + i + 1)
                    nc.gpsimd.tensor_tensor(hid[:], act_g[:], act_u[:], ALU.mult
                                            ).then_inc(sem("hid_ready"), 1)
                    hidden_lo(pool, i, g0, "hid2")
            rms_pool(pool, chain, 6)
            rms_pool(pool, chain, 7)

        @block.tensor
        def _(pe):
            pe.sem_inc(w_used, 4)
            pe.sem_inc(sem("ada_summed"), 2)
            pe.wait_ge(sem("ident_ready"), 1)
            pe.wait_ge(sem("params_first"), 16 * N_FIRST)
            pe.wait_ge(bank_free[0], fill("cols", 0))
            pe.transpose(bank[:, 0, 0:N_ROWS], rows[0:N_ROWS, :], ident[0:N_ROWS, 0:N_ROWS]
                         ).then_inc(bank_full[0], 1)
            pe.wait_ge(sem("params"), 16 * (N_ALL - N_FIRST))
            for b in range(4):
                pe.wait_ge(bank_free[b], fill("conv", b))
                pe.transpose(bank[:, b, 0:nconv], conv_rows[:, b, :], ident[0:nconv, 0:nconv]
                             ).then_inc(bank_full[b], 1)

            pe.wait_ge(sem("ones_ready"), 1)
            for b in range(2):
                pe.wait_ge(bank_free[b], emptied("conv", b))
            for n, g0 in ADA:
                with turns(pe, n // 2) as i:
                    for gg in range(2):
                        g = g0 + 2 * i + gg
                        pe.wait_ge(ada_b_full[gg], 16 * (g0 // 2 + i + 1))
                        pe.wait_ge(sem("ada_used"), 4 + 4 * g + 4)
                        pe.wait_ge(sem("ada_read"), g + 1)
                        sum_pe(pe, ada_acc[:, gg, :], ada_b[:, gg, :], bank[:, gg, :], False
                               ).then_inc(sem("ada_summed"), 1)

            pe.wait_ge(sem("normed"), 2)
            transpose_pe(pe, "norm0", x, KD, 0)
            ph = plan.mix_in
            for g in range(len(ph.groups)):
                products(pe, ph, 0, g, h_hi, h_lo, transposed=3 <= g < 7,
                         ready="norm0" if g == 0 else None)
                if g == 3:
                    pe.wait_ge(sem("roped"), 4)
                    for b in range(5):
                        pe.wait_ge(bank_free[b % 4], fill("rope", b % 4, b // 4))
                        for n in range(2):
                            for t in range(TT):
                                pair = 2 * b + n
                                mm = pe.transpose(
                                    bank[:, b % 4, (2 * n + t) * P:(2 * n + t + 1) * P],
                                    qk_tok[:, t, 2 * pair:2 * pair + 2, :].rearrange("p h d -> p (h d)"),
                                    ident[:])
                        mm.then_inc(bank_full[b % 4], 1)
                if 6 <= g < 10:
                    values_pe(pe, 0, g - 6, pt, v_tok)
                if 5 <= g < 9:
                    turn_pe(pe, 0, g - 5, sm)
                if g == 4:
                    pe.wait_ge(bank_free[0], emptied("rope", 0, 1))
                    for b in range(1, 4):
                        pe.wait_ge(bank_free[b], emptied("rope", b, 0))
                    pe.wait_ge(sem("masks_ready"), 1)
                if 4 <= g < 8:
                    scores_pe(pe, 0, g - 4, q_t, k_t, lambda h: h // (ATT_H // KV_H))
                mod_pe(pe, ph, 0, g)

            def gram(stage, stationary, moving, nbanks):
                for b in range(nbanks):
                    pe.wait_ge(bank_free[b], fill(stage, b))
                    for n in range(4):
                        z = 4 * b + n
                        part = slice((z % 2) * P, (z % 2 + 1) * P)
                        mm = pe.matmul(bank[:, b, n * P:(n + 1) * P], stationary[:, z // 2, part],
                                       moving[:, z // 2, part], start=(n == 0), stop=(n == 3),
                                       skip_group_check=True)
                    mm.then_inc(bank_full[b], 1)

            pe.wait_ge(sem("f_ready"), 1)
            for g in (3, 4):
                pe.wait_ge(psum_free[plan.mix_in.pair[g]], plan.mix_in.freed(0, g))
            gram("diag0", key, qs, 4)
            for n in range(len(LEVELS)):
                pe.wait_ge(sem("level_fac"), 2 * (n + 1))
                gram(f"level{n}", fac[n % 2], fac[n % 2], 4)
            for g in (7, 8):
                pe.wait_ge(psum_free[plan.mix_in.pair[g]], plan.mix_in.freed(0, g))
            recurrence_pe(pe, 0, 3)
            pe.wait_ge(sem("heads0_ready"), 1)
            transpose_pe(pe, "heads0", tokbuf, KD)

            ph = plan.mix_gate
            with turns(pe, ph.iters) as i:
                products(pe, ph, i, 0, h_hi, h_lo)
                products(pe, ph, i, 1, a_hi, a_lo, ready="heads0")
                products(pe, ph, i, 2, h_hi, h_lo)
                products(pe, ph, i, 3, a_hi, a_lo, k_first=ATT_W // P, ready="heads0")
            pe.wait_ge(sem("merged_sum"), ph.iters + 1)
            transpose_pe(pe, "merged", tokbuf, KD)
            ph = plan.mix_out
            with turns(pe, ph.iters) as i:
                for g in range(2):
                    products(pe, ph, i, g, h_hi, h_lo, ready="merged" if g == 0 else None)
                    mod_pe(pe, ph, i, g)
            pe.wait_ge(sem("normed"), 4)
            transpose_pe(pe, "norm1", x, KD, 2)
            for part, (g0, n) in enumerate(FFN_PARTS):
                ph = plan.up1[part]
                with turns(pe, ph.iters) as i:
                    for g in range(2):
                        products(pe, ph, i, g, h_hi, h_lo, transposed=True,
                                 ready="norm1" if g == 0 and part == 0 else None)
                pe.wait_ge(sem("hid_lo"), g0 + n + 1)
                ph = plan.down1[part]
                with turns(pe, ph.iters) as i:
                    for g in range(2):
                        products(pe, ph, i, g, hid_hi, hid_lo)
                        mod_pe(pe, ph, i, g)
            pe.wait_ge(sem("normed"), 6)
            transpose_pe(pe, "norm2", x, KD, 4)

            ph = plan.mix_in2
            pe.wait_ge(sem("toep_full"), 16)
            pe.wait_ge(sem("mirror_ready"), 1)
            for g in range(len(ph.groups)):
                products(pe, ph, 0, g, h_hi, h_lo, transposed=g < 4 or g in (6, 7),
                         ready="norm2" if g == 0 else None)
                if 8 <= g < 12:
                    values_pe(pe, 1, g - 8, pt2, va)
                if 7 <= g < 11:
                    turn_pe(pe, 1, g - 7, sm2)
                if g == 6:
                    for n in range(6):
                        pe.wait_ge(psum_free[ph.pair[n]], ph.freed(0, n))
                if 6 <= g < 10:
                    scores_pe(pe, 1, g - 6, q2_t, k2_t, lambda h: h // 2)
            pe.wait_ge(psum_free[ph.pair[8]], ph.freed(0, 8))
            pe.wait_ge(bank_free[0], fill("low_rank", 0))
            for t in range(TT):
                mm = pe.matmul(bank[0:RANK, 0, t * P:(t + 1) * P], lr_tok[:, t, :], ident[:],
                               start=(t == 0), stop=(t == 1), skip_group_check=True)
            mm.then_inc(bank_full[0], 1)
            pe.wait_ge(bank_free[0], emptied("low_rank", 0))
            pe.wait_ge(sem("w_up_g_full"), 16)
            for f in range(GLA_H):
                if f % 2 == 0:
                    pe.wait_ge(bank_free[f // 2], fill("gate", f // 2))
                mm = pe.matmul(bank[:, f // 2, (f % 2) * TOK:(f % 2 + 1) * TOK],
                               w_up_g[:, f * P:(f + 1) * P], gate_lr[:], start=(f % 2 == 0),
                               stop=(f % 2 == 1), skip_group_check=True)
                if f % 2:
                    mm.then_inc(bank_full[f // 2], 1)
            pe.wait_ge(sem("gla_fac"), 3)
            gram("gla", ebuf[1], qg, 2)
            for g in (11, 12):
                pe.wait_ge(psum_free[ph.pair[g]], ph.freed(0, g))
            recurrence_pe(pe, 1, 1)
            pe.wait_ge(sem("heads1_ready"), 1)
            transpose_pe(pe, "heads1", tokbuf, KD)
            ph = plan.mix_out2
            with turns(pe, ph.iters) as i:
                for g in range(2):
                    products(pe, ph, i, g, h_hi, h_lo, ready="heads1" if g == 0 else None)
            pe.wait_ge(sem("normed"), 8)
            transpose_pe(pe, "norm3", x, KD, 5)
            for part, (g0, n) in enumerate(FFN_PARTS):
                ph = plan.up2[part]
                with turns(pe, ph.iters) as i:
                    for g in range(2):
                        products(pe, ph, i, g, h_hi, h_lo, transposed=True,
                                 ready="norm3" if g == 0 and part == 0 else None)
                pe.wait_ge(sem("hid2_lo"), g0 + n + 1)
                ph = plan.down2[part]
                with turns(pe, ph.iters) as i:
                    for g in range(2):
                        products(pe, ph, i, g, hid_hi, hid_lo)
            pe.wait_ge(sem("p_full"), 16)
            transpose_pe(pe, "ple", p_tok, 2)
            tile_ready(pe, "ple", 0)
            pe.wait_ge(sem("normed"), 10)
            transpose_pe(pe, "norm4", x, KD, 6)
            for g in range(0, len(plan.ple.groups), 2):
                products(pe, plan.ple, 0, g, h_hi, h_lo, ready="norm4" if g == 0 else None)
                products(pe, plan.ple, 0, g + 1, p_hi, p_lo)


_INS = ["x", "c", "positions", "w_ada", "b_ada", "g_pre_mix", "g_post_mix", "g_pre_ffn",
        "g_post_ffn", "w_in", "attn_sinks", "w_attn_proj", "hg_lower_bounds", "hg_norm",
        "w_hgrn_proj", "w_out", "w_ffn_in", "w_ffn_out", "p_2", "norm_mix_w_2", "w_in_2",
        "att_rel_bias_2", "w_gla_gate_up_2", "b_gla_gate_2", "gla_norm_w_2", "w_out_2",
        "norm_ffn_w_2", "w_ffn_up_2", "w_ffn_conv_2", "b_ffn_conv_2", "w_ffn_down_2",
        "norm_ple_w_2", "w_ple_gate_2", "w_ple_proj_2", "final_norm_w_2"]


def kernel(**inputs):
    import numpy as _np
    import concourse.bacc as _bacc
    from concourse import mybir as _mybir
    from concourse.bass_utils import run_bass_kernel_spmd as _run

    nc = _bacc.Bacc("TRN2", target_bir_lowering=False, num_devices=1, dynamic_dma_scratch_size=1024)
    arrays, args = {}, {}
    for name in _INS:
        a = _np.ascontiguousarray(inputs[name])
        arrays[f"in_{name}_dram"] = a
        args[name] = nc.dram_tensor(f"in_{name}_dram", a.shape, _mybir.dt.from_np(a.dtype),
                                    kind="ExternalInput").ap()
    out = nc.dram_tensor("out_0_dram", (1, TOK, D), F32, kind="ExternalOutput").ap()
    build_program(nc, args, out)
    r = _run(nc, [arrays], core_ids=[0])
    return r.results[0]["out_0_dram"]
```

```python
from contextlib import ExitStack, contextmanager

import numpy as np

import concourse.bass as bass
from concourse import mybir
from concourse.alu_op_type import AluOpType as ALU

ACT = mybir.ActivationFunctionType
AX_X = mybir.AxisListType.X
F32 = mybir.dt.float32
F32R = mybir.dt.float32r
I32 = mybir.dt.int32

P = 128
TOK = 256
TT = TOK // P
D = 2048
KD = D // P
COLS = 512
KU = 4
EPS = 1e-6

ATT_H, KV_H, HD = 16, 2, 64
ATT_W, KV_W = ATT_H * HD, KV_H * HD
HG_H, HG_D = 8, 128
HG_W = HG_H * HG_D
CHUNK = 64
FFN = 5632
ROT_HALF = HD // 8
ROPE_THETA = 500000.0
Q0 = 0
KV0 = ATT_W
QH0 = KV0 + 2 * KV_W
FH0 = QH0 + HG_W
IH0 = FH0 + HG_W
GH0 = IH0 + HG_W
GA0 = GH0 + HG_W
GB0 = GA0 + D

A2 = D // 2
GLA_H, GLA_DV, GLA_DK = 4, 256, 128
GLA_W = GLA_H * GLA_DV
RANK = 16
TAU = 16.0
PLE = 256
DIST = 256
QG0 = 3 * A2
KG0 = QG0 + GLA_H * GLA_DK
VG0 = KG0 + GLA_H * GLA_DK
RG0 = VG0 + A2
LR0 = RG0 + A2

NEG = -1.0e30
LOWEST = -3.0e38
LEVELS = [32, 16, 8, 4, 2, 1]

INV_FREQ = np.float32(ROPE_THETA) ** (-np.arange(0, 2 * ROT_HALF, 2, dtype=np.float32)
                                      / np.float32(2 * ROT_HALF))
ROUNDER = 12582912.0
TURN_PARTS = [6.28125, int((2 * np.pi - 6.28125) * 2 ** 21) / 2 ** 21]
TURN_PARTS.append(float(np.float32(2 * np.pi - sum(TURN_PARTS))))

FFN_PARTS = [(0, 6), (6, 5)]


class Phase:

    def __init__(self, plan, iters, groups, mod=None):
        self.iters, self.groups = iters, groups
        self.halves, self.units, self.end, self.items = [], [], [], []
        mod = mod or [0] * len(groups)
        self.mod_units = weight_units = 0
        self.split_at = []

        def mod_unit():
            self.items.append((2 * len(self.units), "mod", self.mod_units))
            self.units.append(("mod", self.mod_units, KU, COLS))
            self.split_at.append(None)
            self.mod_units += 1

        for g, (kt, cols) in enumerate(groups):
            left = mod[g]
            for k0 in range(0, kt, KU):
                j = len(self.units)
                self.units.append((g, k0, min(KU, kt - k0), cols))
                self.split_at.append(2 * weight_units)
                weight_units += 1
                for h in range(0, min(KU, kt - k0), 2):
                    self.items.append((2 * j + h // 2, "half", len(self.halves)))
                    self.halves.append((g, j, h // 2, k0 + h))
                if left and (g or k0 >= 2 * KU):
                    mod_unit()
                    left -= 1
            while left:
                mod_unit()
                left -= 1
            self.end.append(len(self.halves))
        self.mod_base = plan.mod_units
        plan.mod_units += iters * self.mod_units
        self.sums = [next(g for g in range(len(groups)) if sum(mod[:g + 1]) >= 4 * (n + 1))
                     for n in range(self.mod_units // 4)]
        self.buffers = 1 if iters > 1 and len(self.sums) == 1 else 2
        self.turn = -(-len(self.units) // 4) * 4
        self.n0 = plan.n
        plan.n += iters * self.turn
        self.split_turn = -(-weight_units // 2) * 4
        self.split0 = plan.split
        plan.split += iters * self.split_turn
        self.fill0, per = list(plan.fill), [0] * 4
        self.occ = []
        for j in range(len(self.units)):
            self.occ.append(per[j % 4])
            per[j % 4] += 1
        self.per = per
        plan.fill = [a + iters * b for a, b in zip(plan.fill, per)]
        self.q0, self.qper = list(plan.q), [0, 0]
        self.pair, self.use = [], []
        for g in range(len(groups)):
            self.pair.append(g % 2)
            self.use.append(self.qper[g % 2])
            self.qper[g % 2] += 1
        plan.q = [a + iters * b for a, b in zip(plan.q, self.qper)]

    def half(self, i, idx):
        if idx >= len(self.halves):
            i, idx = i + 1, idx - len(self.halves)
        g, j, h, _ = self.halves[idx]
        at = self.split_at[j] + h
        after = self.split_turn
        if idx + 1 < len(self.halves):
            after = self.split_at[self.halves[idx + 1][1]] + self.halves[idx + 1][2]
        full = 16 * (self.fill0[j % 4] + i * self.per[j % 4] + self.occ[j] + 1)
        return (self.split0 + i * self.split_turn + at, at % 4, after - at,
                2 * (self.n0 + i * self.turn + j) + h, j % 4, h, full, self.units[j][3])

    def vector_items(self, i, idx):
        if idx >= len(self.halves):
            i, idx = i + 1, idx - len(self.halves)
        at = next(n for n, x in enumerate(self.items) if x[1:] == ("half", idx))
        found = []
        while True:
            number, kind, n = self.items[at]
            after = self.items[at + 1][0] if at + 1 < len(self.items) else 2 * self.turn
            found.append((kind, i, n, number, after - number))
            at += 1
            if at == len(self.items) or self.items[at][1] == "half":
                return found

    def mod_done(self, i, n):
        number = next(x[0] for x in self.items if x[1:] == ("mod", 4 * n + 3))
        return 8 + 2 * (self.n0 + i * self.turn) + number + 1

    def mod_sum(self, i, n):
        return self.mod_base // 4 + i * len(self.sums) + n

    def unit_number(self, i, j):
        return self.n0 + i * self.turn + j

    def done(self, i, g):
        g_, j, h, _ = self.halves[self.end[g] - 1]
        return 4 + self.split0 + i * self.split_turn + self.split_at[j] + h + 1

    def free(self, i, g):
        p = self.pair[g]
        return 1 + self.q0[p] + i * self.qper[p] + self.use[g]

    def freed(self, i, g):
        return self.free(i, g) + 1


class Plan:
    def __init__(self):
        self.n, self.split, self.fill, self.q, self.mod_units = 0, 0, [0] * 4, [0, 0], 0
        full = (KD, COLS)
        half = (ATT_W // P, COLS)
        self.mix_in = Phase(self, 1, [full, full, (KD, 2 * KV_W)] + [full] * 8
                            + [full, half] * (D // COLS) + [full, half],
                            mod=[4, 4, 2, 2, 4, 2, 2, 2, 2, 2, 2, 2, 0, 2] + [0] * 7)
        self.mix_gate = Phase(self, D // COLS - 1, [full, half])
        self.mix_out = Phase(self, D // COLS // 2, [full, full], mod=[4, 4])
        self.up1, self.down1 = [], []
        for _, n in FFN_PARTS:
            self.up1.append(Phase(self, n, [full, full]))
            self.down1.append(Phase(self, 2, [(4 * n, COLS), (4 * n, COLS)], mod=[0, 4]))
        self.mix_in2 = Phase(self, 1, [full] * 8 + [(KD, RANK)] + [full] * 4
                             + [half] * (D // COLS))
        self.mix_out2 = Phase(self, D // COLS // 2, [half, half])
        self.up2, self.down2 = [], []
        for _, n in FFN_PARTS:
            self.up2.append(Phase(self, n, [full, full]))
            self.down2.append(Phase(self, 2, [(4 * n, COLS), (4 * n, COLS)]))
        self.ple = Phase(self, 1, [full, (PLE // P, COLS)] * (D // COLS))


ALL_BANKS = (1, 1, 1, 1)
RECURRENCE = {
    10: [("att0", ALL_BANKS), ("diag0", ALL_BANKS)],
    11: [("level0", ALL_BANKS), ("level1", ALL_BANKS)],
    13: [("level2", ALL_BANKS), ("level3", ALL_BANKS)],
    15: [("level4", ALL_BANKS), ("level5", ALL_BANKS)],
    16: [("rec0_k", ALL_BANKS)],
    17: [("rec0_u0", (1, 1, 0, 0)), ("rec0_u1", (0, 0, 1, 1)), ("rec0_u2", (1, 1, 0, 0))],
    18: [("rec0_o", ALL_BANKS)],
    19: [("heads0", ALL_BANKS)],
}


RECURRENCE_2 = {
    9: [("low_rank", (1, 0, 0, 0))],
    10: [("gate", (1, 1, 0, 0))],
    12: [("att1", ALL_BANKS), ("gla", (1, 1, 0, 0)), ("rec1_k", (1, 1, 0, 0))],
    13: [("rec1_u0", (1, 1, 0, 0)), ("rec1_u1", (0, 0, 1, 1)), ("rec1_u2", (1, 1, 0, 0))],
    14: [("rec1_o", ALL_BANKS)],
    15: [("heads1", ALL_BANKS)],
}
LEVELS_AT = {11: (0, 1), 13: (2, 3), 15: (4, 5)}


def bank_uses(plan):
    uses = [("cols", (1, 0, 0, 0)), ("conv", (1, 1, 1, 1)), ("bias", (1, 0, 0, 0)), ("norm0", (2, 2, 2, 2))]

    def hooks(r, phase, first):
        for g in range(len(phase.groups)):
            if r == 0 and g == first - 1:
                uses.append(("rope", (2, 1, 1, 1)))
            if first + 2 <= g < first + 6:
                uses.append((f"attn{r}_v{g - first - 2}", (1, 0, 0, 0)))
            if first + 1 <= g < first + 5:
                uses.append((f"attn{r}_t{g - first - 1}", (1, 1, 1, 1)))
            if first <= g < first + 4:
                uses.append((f"attn{r}_s{g - first}", (1, 1, 1, 1)))
            for name, use in (RECURRENCE, RECURRENCE_2)[r].get(g, []):
                uses.append((name, use))
            for n in range(phase.sums.count(g)):
                uses.append((f"mod_in{g}", (0, 0, 0, 1)))

    hooks(0, plan.mix_in, 4)
    uses += [
        ("merged", (2, 2, 2, 2)), ("mod_out", (0, 0, 0, 4)),
        ("norm1", (2, 2, 2, 2)), ("mod_down0", (0, 0, 0, 2)), ("mod_down1", (0, 0, 0, 2)),
        ("norm2", (2, 2, 2, 2))]
    hooks(1, plan.mix_in2, 6)
    return uses + [
        ("norm3", (2, 2, 2, 2)), ("ple", (1, 0, 0, 0)),
        ("norm4", (2, 2, 2, 2))]


def bank_bases(plan):
    at, base = [0] * 4, {}
    for name, uses in bank_uses(plan):
        base[name] = tuple(at)
        at = [a + u for a, u in zip(at, uses)]
    return base


@contextmanager
def turns(eng, n):
    if n == 1:
        yield 0
    else:
        with eng.Fori(0, n) as i:
            yield i


def build_program(nc, a, out):
    plan = Plan()
    bank0 = bank_bases(plan)

    with ExitStack() as ctx:
        def sb(name, shape, dt=F32):
            return ctx.enter_context(nc.sbuf_tensor(name, shape, dt))

        sems = {}

        def sem(name):
            if name not in sems:
                sems[name] = ctx.enter_context(nc.semaphore(name))
            return sems[name]

        X0 = -(-nc.sbuf_base // 32) * 32
        x = sb("x", [P, TT, D])
        tokbuf = sb("tokbuf", [P, TT, D])
        h_hi = sb("h_hi", [P, KD, TOK], F32R)
        h_lo = sb("h_lo", [P, KD, TOK], F32R)
        raw = sb("raw", [P, 4, KU, COLS])
        w_hi = sb("w_hi", [P, 4, 2, COLS], F32R)
        w_lo = sb("w_lo", [P, 4, 2, COLS], F32R)
        GATE0 = -(-nc.sbuf_base // 32) * 32
        gate_row = sb("gate_row", [P, D])
        tmp = sb("tmp", [P, 2, 2, TOK])
        ident = sb("ident", [P, P])
        ones = sb("ones", [P, P])
        cols = sb("cols", [P, P])
        mod_cols = sb("mod_cols", [P, 96])
        a_cols = sb("a_cols", [P, 2, KD])
        conv_cols = sb("conv_cols", [P, 4, 2 * FFN // P])
        band = sb("band", [P, 3 * P])
        chunked = sb("chunked", [P, 3 * P])
        level_mask = sb("level_mask", [P, len(LEVELS), P])
        causal = sb("causal", [P, P])
        scan_keep = sb("scan_keep", [P, COLS])
        stats = sb("stats", [P, 8, 4])
        minus_half = sb("minus_half", [P, 16])
        diag = sb("diag", [P, TT, P])
        trig = sb("trig", [P, 2, TT, ROT_HALF])
        sinks = sb("sinks", [P, ATT_H])
        hg_gain = sb("hg_gain", [P, HG_D])
        gla_gain = sb("gla_gain", [P, GLA_DV])
        lb = sb("lb", [P, 6, HG_H])
        mx = sb("mx", [P, 2, 4, TT, 4])
        nmx = sb("nmx", [P, 2, 4, TT, 4])
        rsum = sb("rsum", [P, 2, 4, TT, 4])
        esink = sb("esink", [P, 4, TT, 4])
        den = sb("den", [P, 2, 4, TT, 4])
        rden = sb("rden", [P, 2, 4, TT, 4])
        hstat = sb("hstat", [P, 2, 2, 16])
        ends = sb("ends", [P, 2, 8, TOK // CHUNK])
        ARENA_KB = 66
        ARENA0 = nc.sbuf_usable_end // 32 * 32 - ARENA_KB * 1024
        assert nc.sbuf_base <= ARENA0, (nc.sbuf_base, ARENA0, nc.sbuf_usable_end)

        def place(name, kb, shape, dt=F32):
            size = 4
            for n in shape[1:]:
                size *= n
            assert kb * 1024 + size <= ARENA_KB * 1024, name
            return nc.alloc_sbuf_tensor_at(name, shape, dt, offset=ARENA0 + int(kb * 1024))

        mod_acc = [nc.alloc_sbuf_tensor_at("mod_acc0", [P, 2, COLS], F32, offset=GATE0),
                   place("mod_acc1", 58, [P, 2, COLS])]
        mod_b = [nc.alloc_sbuf_tensor_at("mod_b0", [1, 2, COLS], F32, offset=GATE0 + 4096),
                 place("mod_b1", 62, [1, 2, COLS])]
        ada_raw = place("ada_raw", 0, [P, 4, KU, COLS])
        ada_acc = place("ada_acc", 32, [P, 2, COLS])
        bias_rows = place("bias_rows", 50, [2 * KD, P])
        bias_cols = place("bias_cols", 53.75, [P, 2 * KD])
        conv_rows = place("conv_rows", 48, [2 * FFN // P, 4, P])
        rows = place("rows", 51, [P, P])
        pos_i = place("pos_i", 53, [P, TT], I32)
        pos_f = place("pos_f", 53.25, [P, TT])
        invf = place("invf", 53.5, [P, ROT_HALF])
        rope = place("rope", 52, [P, 6, 2, TT * ROT_HALF])
        qs = place("qs", 0, [P, HG_H, TOK])
        key = place("key", 8, [P, HG_H, TOK])
        logf = place("logf", 16, [P, HG_H, TOK])
        vh = place("vh", 24, [P, TT, HG_W])
        q_t = place("q_t", 32, [P, ATT_H // 2, TOK])
        k_t = place("k_t", 40, [P, KV_H, TOK])
        sm = place("sm", 42, [P, 4, 3 * P])
        pt = place("pt", 48, [P, 4, 3 * P])
        qk_tok = place("qk_tok", 54, [P, TT, ATT_H + 2 * KV_H, HD])
        v_tok = place("v_tok", 64, [P, TT, KV_W])
        rope_tmp = place("rope_tmp", 8, [P, 4, ATT_H + 2 * KV_H, ROT_HALF])
        fac = [place("fac0", 42, [P, HG_H, TOK]), place("fac1", 58, [P, HG_H, TOK])]
        scores = place("scores", 50, [P, 16, P])
        kend_t = place("kend_t", 58, [P, 16, P])
        state = [place("state1", 16, [P, HG_W]), place("state2", 20, [P, HG_W]),
                 place("state3", 42, [P, HG_W])]
        att_hi = nc.alloc_sbuf_tensor_at("att_hi", [P, ATT_W // P, TOK], F32R, offset=X0)
        att_lo = nc.alloc_sbuf_tensor_at("att_lo", [P, ATT_W // P, TOK], F32R, offset=X0 + 8192)
        rec_hi = place("rec_hi", 0, [P, HG_W // P, TOK], F32R)
        rec_lo = place("rec_lo", 8, [P, HG_W // P, TOK], F32R)
        sig_a = place("sig_a", 32, [P, TT, COLS])
        merged_2 = place("merged_2", 36, [P, TT, COLS])
        sig_b = place("sig_b", 46, [P, TT, COLS])
        part_b = place("part_b", 54, [P, TT, COLS])
        junk = place("junk", 58, [P, D])
        hid_hi = place("hid_hi", 0, [P, 24, TOK], F32R)
        hid_lo = place("hid_lo", 24, [P, 24, TOK], F32R)
        act_g = place("act_g", 48, [P, 4, TOK])
        act_u = place("act_u", 52, [P, 4, TOK])
        hid = place("hid", 56, [P, 4, TOK])
        q2_t = place("q2_t", 0, [P, ATT_H // 2, TOK])
        k2_t = place("k2_t", 8, [P, ATT_H // 2, TOK])
        va = place("va", 16, [P, TT, A2])
        toep = place("toep", 24, [P, ATT_H, TOK])
        sm2 = place("sm2", 40, [P, 4, 3 * P])
        pt2 = place("pt2", 46, [P, 4, 3 * P])
        qg = place("qg", 52, [P, GLA_H, TOK])
        kg = place("kg", 56, [P, GLA_H, TOK])
        w_up_g = place("w_up_g", 60, [RANK, GLA_H * GLA_DK])
        gate_lr = place("gate_lr", 62, [RANK, TOK])
        mirror = place("mirror", 63, [P, P])
        lr_tok = place("lr_tok", 63.5, [P, TT, RANK])
        vg = place("vg", 24, [P, TT, A2])
        lg = place("lg", 0, [P, GLA_H, TOK])
        ebuf = [place("ebuf0", 4, [P, GLA_H, TOK]), place("ebuf1", 8, [P, GLA_H, TOK])]
        k_end = place("k_end", 12, [P, GLA_H, TOK])
        scores2 = place("scores2", 16, [P, 8, P])
        kend2_t = place("kend2_t", 20, [P, 8, P])
        state_2 = [place("state1_2", 32, [P, A2]), place("state2_2", 36, [P, A2]),
                   place("state3_2", 40, [P, A2])]
        p_tok = place("p_tok", 0, [P, TT, PLE])
        p_hi = place("p_hi", 2, [P, PLE // P, TOK], F32R)
        p_lo = place("p_lo", 4, [P, PLE // P, TOK], F32R)
        sig_p = place("sig_p", 8, [P, TT, COLS])
        out_row = place("out_row", 16, [P, D])

        psum = [ctx.enter_context(nc.psum_tensor(f"psum{n}", [P, 2, COLS], F32)) for n in range(2)]
        bank = ctx.enter_context(nc.psum_tensor("bank", [P, 4, COLS], F32))

        merged_att = [tokbuf[:, :, 0:COLS], tokbuf[:, :, COLS:2 * COLS], merged_2[:],
                      tmp[:].rearrange("p t b c -> p t (b c)")]

        raw_full = [sem(f"raw_full{n}") for n in range(4)]
        split_hi, split_lo, w_used = sem("split_hi"), sem("split_lo"), sem("w_used")
        psum_free = [sem("psum_free0"), sem("psum_free1")]
        bank_full = [sem(f"bank_full{n}") for n in range(4)]
        bank_free = [sem(f"bank_free{n}") for n in range(4)]
        ada_full = [sem(f"ada_full{n}") for n in range(4)]
        mod_b_full = [sem(f"mod_b_full{n}") for n in range(2)]
        MODS = [(plan.mix_in, 12, 0, "mod_in"), (plan.mix_out, 8, 1, "mod_out"),
                (plan.down1[0], 20, 1, "mod_down0"), (plan.down1[1], 22, 1, "mod_down1")]

        class Chain:

            def __init__(self, eng, name):
                self.eng, self.sem, self.n = eng, sem(name), 0

            def __call__(self, ins):
                ins.then_inc(self.sem, 1)
                self.n += 1
                self.eng.wait_ge(self.sem, self.n)

        def fill(name, b, k=0):
            return 1 + bank0[name][b] + k

        def filled(name, b, k=0):
            return bank0[name][b] + k + 1

        def emptied(name, b, k=0):
            return fill(name, b, k) + 1

        def mod_of(ph):
            return next(x[1:] for x in MODS if x[0] is ph)

        def mod_buffer(ph, n):
            return n % 2 if ph.buffers == 2 else 0

        def mod_bias_uses(ph, i, n):
            first, per = [0, 0], [0, 0]
            for other, *_ in MODS:
                now = [0, 0]
                for m in range(len(other.sums)):
                    now[mod_buffer(other, m)] += 1
                if other is ph:
                    per = now
                    break
                first = [f + other.iters * x for f, x in zip(first, now)]
            b = mod_buffer(ph, n)
            before = sum(mod_buffer(ph, m) == b for m in range(n))
            return first[b] + i * per[b] + before + 1

        def load_mod(sp, ph, i, j, q):
            g0, place_, _ = mod_of(ph)
            n = q // 4
            g = g0 + i * len(ph.sums) + n
            if q % 4 == 0:
                s_ = ph.mod_sum(i, n) + 1 - ph.buffers
                if ph.iters > 1 or s_ > 0:
                    sp.wait_ge(sem("mod_summed"), s_)
                if ph.iters > 1:
                    sp.sem_inc(sem("slot_seen"), 1)
                b = mod_buffer(ph, n)
                sp.dma_start(mod_b[place_][:, b, :], a["b_ada"][:, bass.ds(g * COLS, COLS)]
                             ).then_inc(mod_b_full[b], 16)
            sp.wait_ge(split_lo, 2 * ph.unit_number(i, j) + 2)
            if ph.iters > 1:
                sp.sem_inc(sem("slot_seen"), 1)
            sp.dma_start(raw[:, j % 4], cut(w_ada, (q % 4) * KU, KU, g * COLS, COLS)
                         ).then_inc(raw_full[j % 4], 16)

        def add_mod(dve, ph, i, q, number, inc):
            _, place_, _ = mod_of(ph)
            n = q // 4
            j = number // 2
            acc = mod_acc[place_][:, mod_buffer(ph, n), :]
            done = 3 * (ph.mod_base + i * ph.mod_units + q)
            dve.wait_ge(raw_full[j % 4], 16 * (ph.fill0[j % 4] + i * ph.per[j % 4] + ph.occ[j] + 1))
            if q % 4 == 0:
                s_ = ph.mod_sum(i, n) + 1 - ph.buffers
                if ph.iters > 1 or s_ > 0:
                    dve.wait_ge(sem("mod_summed"), s_)
            else:
                before = next(x[0] for x in ph.items if x[1:] == ("mod", q - 1))
                dve.wait_ge(split_lo, 8 + 2 * (ph.n0 + i * ph.turn) + before + 1)
            for k in range(KU):
                cc = cols[:, ROW["c"] + (q % 4) * KU + k:ROW["c"] + (q % 4) * KU + k + 1]
                if k:
                    dve.wait_ge(sem("mod_order"), done + k)
                if q % 4 == 0 and k == 0:
                    ins = nc.vector.tensor_scalar(acc, raw[:, j % 4, k, :], cc, None, ALU.mult)
                else:
                    ins = nc.vector.scalar_tensor_tensor(acc, raw[:, j % 4, k, :], cc, acc,
                                                         ALU.mult, ALU.add)
                if k < KU - 1:
                    ins.then_inc(sem("mod_order"), 1)
                else:
                    ins.then_inc(split_lo, inc)

        def sum_pe(pe, acc, bias, o, as_rows):
            if as_rows:
                pe.matmul(o, ones[:], acc, start=True, stop=False, skip_group_check=True)
                return pe.matmul(o, ones[0:1, :], bias, start=False, stop=True,
                                 skip_group_check=True)
            for f in range(4):
                part = slice(f * P, (f + 1) * P)
                pe.matmul(o[:, f:f + 1], acc[:, part], ones[:, 0:1], start=(f == 0), stop=False,
                          skip_group_check=True)
                mm = pe.matmul(o[:, f:f + 1], bias[:, part], ones[0:1, 0:1], start=False,
                               stop=(f == 3), skip_group_check=True)
            return mm

        def mod_bank(ph, i, n):
            name = mod_of(ph)[2]
            if name == "mod_in":
                return f"mod_in{ph.sums[n]}", 0
            return name, i * len(ph.sums) + n

        def mod_pe(pe, ph, i, g):
            g0, place_, _ = mod_of(ph)
            for n, due in enumerate(ph.sums):
                if due != g:
                    continue
                b = mod_buffer(ph, n)
                stage, k = mod_bank(ph, i, n)
                pe.wait_ge(split_lo, ph.mod_done(i, n))
                pe.wait_ge(mod_b_full[b], 16 * mod_bias_uses(ph, i, n))
                pe.wait_ge(bank_free[3], fill(stage, 3, k))
                o = bank[:, 3, :]
                sum_pe(pe, mod_acc[place_][:, b, :], mod_b[place_][:, b, :], o, g0 != 12
                       ).then_inc(bank_full[3], 1)
                pe.wait_ge(bank_full[3], filled(stage, 3, k))
                pe.sem_inc(sem("mod_summed"), 1)

        def mod_dve(dve, ph, i, g):
            g0, _, _ = mod_of(ph)
            for n, due in enumerate(ph.sums):
                if due != g:
                    continue
                stage, k = mod_bank(ph, i, n)
                dve.wait_ge(bank_full[3], filled(stage, 3, k))
                if g0 == 12:
                    ins = nc.vector.tensor_copy(mod_cols[:, 4 * (g0 + n):4 * (g0 + n + 1)],
                                                bank[:, 3, 0:4])
                else:
                    at = (g0 - 8) % 12 if g0 != 22 else 2
                    dst = gate_row[:, bass.ds((at + i * len(ph.sums) + n) * COLS, COLS)]
                    ins = nc.vector.tensor_tensor(dst, dst, bank[:, 3, :], ALU.mult)
                ins.then_inc(bank_free[3], 1)

        def load_phase(sp, ph, source):
            with turns(sp, ph.iters) as i:
                for j, (g, k0, nk, ncol) in enumerate(ph.units):
                    if g == "mod":
                        load_mod(sp, ph, i, j, k0)
                        continue
                    sp.wait_ge(split_lo, 2 * ph.unit_number(i, j) + 2)
                    if ph.iters > 1:
                        sp.sem_inc(sem("slot_seen"), 1)
                    sp.dma_start(raw[:, j % 4, 0:nk, 0:ncol], source(i, g, k0, nk, ncol)
                                 ).then_inc(raw_full[j % 4], 16)

        def split_w_hi(act, ph, i, first, last):
            for idx in range(first, last):
                m, slot, inc, _, rs, h, full, ncol = ph.half(i, idx)
                act.wait_ge(raw_full[rs], full)
                act.wait_ge(w_used, m + 1)
                nc.scalar.activation(w_hi[:, slot, :, 0:ncol], raw[:, rs, 2 * h:2 * h + 2, 0:ncol],
                                     ACT.Copy).then_inc(split_hi, inc)

        def split_w_lo(dve, ph, i, first, last):
            for idx in range(first, last):
                m, slot, _, _, rs, h, full, ncol = ph.half(i, idx)
                for kind, turn, n, number, inc in ph.vector_items(i, idx):
                    if kind == "mod":
                        add_mod(dve, ph, turn, n, number, inc)
                        continue
                    dve.wait_ge(split_hi, m + 1)
                    nc.vector.tensor_tensor(w_lo[:, slot, :, 0:ncol],
                                            raw[:, rs, 2 * h:2 * h + 2, 0:ncol],
                                            w_hi[:, slot, :, 0:ncol].bitcast(F32),
                                            ALU.subtract).then_inc(split_lo, inc)

        def span(ph, g, final=False):
            first = (ph.end[g - 1] if g else 0) + 4
            last = ph.end[g] + 4
            if final:
                first, last = min(first, len(ph.halves)), min(last, len(ph.halves))
            return first, last

        def products(pe, ph, i, g, hi, lo, k_first=0, transposed=False, ready=None,
                     hidden=None):
            ps = psum[ph.pair[g]]
            pe.wait_ge(psum_free[ph.pair[g]], ph.free(i, g))
            start, stop = (ph.end[g - 1] if g else 0), ph.end[g]
            for idx in range(start, stop):
                _, slot, inc, m, _, _, _, ncol = ph.half(i, idx)
                pe.wait_ge(split_lo, 8 + m + 1)
                if hidden and hidden[2] == 0 and idx % 2 == 0:
                    pe.wait_ge(hidden[0], hidden[1] + ph.halves[idx][3] // 4)
                if ready:
                    tile_ready(pe, ready, (k_first + ph.halves[idx][3]) // 2)
                for kk in range(2):
                    k = k_first + ph.halves[idx][3] + kk
                    first = idx == start and kk == 0
                    last = idx == stop - 1 and kk == 1
                    wh, wl = w_hi[:, slot, kk, :], w_lo[:, slot, kk, :]
                    if not transposed:
                        for t in range(TT):
                            o = ps[:, t, 0:ncol]
                            xh, xl = hi[:, k, t * P:(t + 1) * P], lo[:, k, t * P:(t + 1) * P]
                            pe.matmul(o, xh, wh[:, 0:ncol], start=first, stop=False,
                                      skip_group_check=True)
                            pe.matmul(o, xh, wl[:, 0:ncol], start=False, stop=False,
                                      skip_group_check=True)
                            mm = pe.matmul(o, xl, wh[:, 0:ncol], start=False, stop=last,
                                           skip_group_check=True)
                    else:
                        for f in range(-(-ncol // P)):
                            n = min(P, ncol - f * P)
                            o = ps[0:n, f // 2, (f % 2) * TOK:(f % 2 + 1) * TOK]
                            fh, fl = wh[:, f * P:f * P + n], wl[:, f * P:f * P + n]
                            pe.matmul(o, fh, hi[:, k, :], start=first and f % 2 == 0, stop=False,
                                      skip_group_check=True)
                            pe.matmul(o, fh, lo[:, k, :], start=False, stop=False,
                                      skip_group_check=True)
                            mm = pe.matmul(o, fl, hi[:, k, :], start=False, stop=last,
                                           skip_group_check=True)
                mm.then_inc(w_used, inc)

        def transpose_pe(pe, stage, src, tiles, r=None, first=0):
            for b in range(tiles // 2):
                pe.wait_ge(bank_free[b % 4], fill(stage, b % 4, b // 4))
                for k in range(2):
                    for t in range(TT):
                        o = bank[:, b % 4, (2 * k + t) * P:(2 * k + t + 1) * P]
                        tile = src[:, t, (first + 2 * b + k) * P:(first + 2 * b + k + 1) * P]
                        if r is None:
                            mm = pe.transpose(o, tile, ident[:])
                        else:
                            mm = pe.matmul(o, tile, diag[:, t, :], start=(k == 0 and t == 0),
                                           stop=(k == 1 and t == 1), skip_group_check=True)
                mm.then_inc(bank_full[b % 4], 1)

        def split_act(act, stage, hi, tiles, gain=None, shift=None):
            for b in range(tiles // 2):
                if shift is not None:
                    act.wait_ge(sem(f"{stage}_scaled"), b + 1)
                    nc.scalar.activation(hi[:, 2 * b:2 * b + 2, :], tmp[:, b % 2, :, :], ACT.Copy
                                         ).then_inc(sem(f"{stage}_hi"), 1)
                    continue
                act.wait_ge(bank_full[b % 4], filled(stage, b % 4, b // 4))
                if gain is None:
                    nc.scalar.activation(hi[:, 2 * b:2 * b + 2, :],
                                         bank[:, b % 4, :].rearrange("p (k t) -> p k t", k=2),
                                         ACT.Copy).then_inc(sem(f"{stage}_hi"), 1)
                    continue
                for k in range(2):
                    f = 2 * b + k
                    nc.scalar.activation(hi[:, f, :], bank[:, b % 4, k * TOK:(k + 1) * TOK],
                                         ACT.Identity, scale=gain[:, f:f + 1]
                                         ).then_inc(sem(f"{stage}_hi"), 1)

        def split_dve(dve, stage, hi, lo, tiles, gain=None, shift=None):
            def lower(b):
                dve.wait_ge(sem(f"{stage}_hi"), b + 1)
                nc.vector.tensor_tensor(lo[:, 2 * b:2 * b + 2, :], tmp[:, b % 2, :, :],
                                        hi[:, 2 * b:2 * b + 2, :].bitcast(F32), ALU.subtract
                                        ).then_inc(bank_free[b % 4], 1)

            if shift is not None:
                for b in range(tiles // 2):
                    dve.wait_ge(bank_full[b % 4], filled(stage, b % 4, b // 4))
                    if b >= 2:
                        dve.wait_ge(bank_free[(b - 2) % 4], emptied(stage, (b - 2) % 4, (b - 2) // 4))
                    for k in range(2):
                        f = 2 * b + k
                        ins = nc.vector.tensor_scalar(
                            tmp[:, b % 2, k, :], bank[:, b % 4, k * TOK:(k + 1) * TOK],
                            gain[:, f:f + 1], shift[:, f:f + 1], ALU.mult, ALU.add)
                    ins.then_inc(sem(f"{stage}_scaled"), 1)
                    if b:
                        lower(b - 1)
                lower(tiles // 2 - 1)
                return
            for b in range(tiles // 2):
                if gain is None:
                    dve.wait_ge(sem(f"{stage}_hi"), b + 1)
                    nc.vector.tensor_tensor(lo[:, 2 * b:2 * b + 2, :],
                                            bank[:, b % 4, :].rearrange("p (k t) -> p k t", k=2),
                                            hi[:, 2 * b:2 * b + 2, :].bitcast(F32), ALU.subtract
                                            ).then_inc(bank_free[b % 4], 1)
                    continue
                dve.wait_ge(sem(f"{stage}_hi"), 2 * b + 2)
                for k in range(2):
                    f = 2 * b + k
                    ins = nc.vector.scalar_tensor_tensor(
                        lo[:, f, :], bank[:, b % 4, k * TOK:(k + 1) * TOK], gain[:, f:f + 1],
                        hi[:, f, :].bitcast(F32), ALU.mult, ALU.subtract)
                ins.then_inc(bank_free[b % 4], 1)

        def tile_ready(pe, stage, b):
            pe.wait_ge(bank_free[b % 4], emptied(stage, b % 4, b // 4))

        def squares_act(act, r, src, ready=None):
            for t in range(TT):
                if ready is not None:
                    act.wait_ge(sem("x_ready"), ready + t + 1)
                if r or t:
                    act.wait_ge(sem("squares"), 2 * r + t)
                nc.scalar.activation(junk[:], src[:, t, :], ACT.Square,
                                     accum_out=stats[:, r, t:t + 1]).then_inc(sem("squares"), 1)

        def rms_pool(pool, chain, r):
            pool.wait_ge(sem("squares"), 2 * (r + 1))
            chain(nc.gpsimd.tensor_scalar(stats[:, r, 2:4], stats[:, r, 0:2], 1.0 / D, EPS,
                                          ALU.mult, ALU.add))
            nc.gpsimd.tensor_tensor(stats[:, r, 2:4], stats[:, r, 2:4], minus_half[:, 0:2],
                                    ALU.pow).then_inc(sem("rms"), 1)

        def normed_dve(dve, r):
            dve.wait_ge(sem("rms"), r + 1)
            for t in range(TT):
                nc.vector.tensor_scalar(diag[:, t, :], ident[:], stats[:, r, 2 + t:3 + t], None,
                                        ALU.mult).then_inc(sem("normed"), 1)

        def residual_dve(dve, chain, r):
            dve.wait_ge(sem("rms"), r + 1)
            for t in range(TT):
                chain(nc.vector.scalar_tensor_tensor(tokbuf[:, t, :], tokbuf[:, t, :],
                                                     stats[:, r, 2 + t:3 + t], gate_row[:],
                                                     ALU.mult, ALU.mult))
                ins = nc.vector.tensor_tensor(x[:, t, :], x[:, t, :], tokbuf[:, t, :], ALU.add)
                ins.then_inc(sem("x_ready"), 1)

        def scores_pe(pe, r, b, q, k, k_tile):
            for hh in range(4):
                h = 4 * b + hh
                o = bank[:, hh, :]
                rows_ = slice(HD * (h % 2), HD * (h % 2) + HD)
                kk = k[rows_, k_tile(h), :]
                pe.wait_ge(bank_free[hh], fill(f"attn{r}_s{b}", hh))
                mm = pe.matmul(o[:, 0:P], q[rows_, h // 2, 0:P], kk[:, 0:P], start=True,
                               stop=(r == 0), skip_group_check=True)
                mm = pe.matmul(o[:, P:3 * P], q[rows_, h // 2, P:2 * P], kk, start=False,
                               stop=(r == 0), skip_group_check=True)
                if r == 1:
                    pe.matmul(o[:, 0:P], toep[:, h, 0:P], mirror[:], start=False, stop=False,
                              skip_group_check=True)
                    pe.matmul(o[:, P:2 * P], toep[:, h, P:2 * P], mirror[:], start=False,
                              stop=False, skip_group_check=True)
                    mm = pe.matmul(o[:, 2 * P:3 * P], toep[:, h, 0:P], mirror[:], start=False,
                                   stop=True, skip_group_check=True)
                mm.then_inc(bank_full[hh], 1)

        def softmax_dve(dve, chain, r, b, s, mask):
            for hh in range(4):
                h = 4 * b + hh
                dve.wait_ge(bank_full[hh], filled(f"attn{r}_s{b}", hh))
                start = sinks[:, h:h + 1] if r == 0 else LOWEST
                for t, part in ((0, slice(0, P)), (1, slice(P, 3 * P))):
                    ins = nc.vector.tensor_tensor_reduce(s[:, hh, part], bank[:, hh, part],
                                                         mask[:, part], 1.0, start, ALU.add, ALU.max,
                                                         mx[:, r, b, t, hh:hh + 1])
                ins.then_inc(bank_free[hh], 1)
            dve.wait_ge(bank_free[3], emptied(f"attn{r}_s{b}", 3))
            if r == 0:
                for t in range(TT):
                    nc.vector.tensor_tensor(esink[:, b, t, :], sinks[:, 4 * b:4 * b + 4],
                                            mx[:, r, b, t, :], ALU.subtract)
            nc.vector.tensor_scalar(nmx[:, r, b], mx[:, r, b], -1.0, None, ALU.mult
                                    ).then_inc(sem(f"attn{r}_max"), 1)

        def softmax_act(act, r, b, s):
            act.wait_ge(sem(f"attn{r}_max"), b + 1)
            for hh in range(4):
                for t, part in ((0, slice(0, P)), (1, slice(P, 3 * P))):
                    nc.scalar.activation(s[:, hh, part], s[:, hh, part], ACT.Exp,
                                         bias=nmx[:, r, b, t, hh:hh + 1],
                                         accum_out=rsum[:, r, b, t, hh:hh + 1]
                                         ).then_inc(sem(f"attn{r}_exp"), 1)
            if r == 0:
                nc.scalar.activation(esink[:, b], esink[:, b], ACT.Exp).then_inc(sem(f"attn{r}_exp"), 1)

        EXPS = [9, 8]

        def turn_pe(pe, r, b, s):
            pe.wait_ge(sem(f"attn{r}_exp"), EXPS[r] * (b + 1))
            for hh in range(4):
                pe.wait_ge(bank_free[hh], fill(f"attn{r}_t{b}", hh))
                for n in range(3):
                    mm = pe.transpose(bank[:, hh, n * P:(n + 1) * P], s[:, hh, n * P:(n + 1) * P],
                                      ident[:])
                mm.then_inc(bank_full[hh], 1)

        def turn_act(act, r, b, p_):
            if b:
                act.wait_ge(bank_full[0], filled(f"attn{r}_v{b - 1}", 0))
            for hh in range(4):
                act.wait_ge(bank_full[hh], filled(f"attn{r}_t{b}", hh))
                nc.scalar.activation(p_[:, hh, :], bank[:, hh, 0:3 * P], ACT.Copy
                                     ).then_inc(bank_free[hh], 1)

        def values_pe(pe, r, b, p_, v):
            for hh in range(4):
                pe.wait_ge(bank_free[hh], emptied(f"attn{r}_t{b}", hh))
            pe.wait_ge(bank_free[0], fill(f"attn{r}_v{b}", 0))
            for hh in range(4):
                c = (4 * b + hh) * HD if r == 1 else (4 * b + hh) // (ATT_H // KV_H) * HD
                lo_, hi_ = hh * HD, 4 * HD + hh * HD
                pe.matmul(bank[:, 0, lo_:lo_ + HD], p_[:, hh, 0:P], v[:, 0, c:c + HD],
                          start=(hh == 0), stop=False, skip_group_check=True)
                pe.matmul(bank[:, 0, hi_:hi_ + HD], p_[:, hh, P:2 * P], v[:, 0, c:c + HD],
                          start=False, stop=False, skip_group_check=True)
                mm = pe.matmul(bank[:, 0, hi_:hi_ + HD], p_[:, hh, 2 * P:3 * P], v[:, 1, c:c + HD],
                               start=False, stop=(hh == 3), skip_group_check=True)
            mm.then_inc(bank_full[0], 1)

        def values_dve(dve, chain, r, b):
            dve.wait_ge(sem(f"attn{r}_exp"), EXPS[r] * (b + 1))
            if r == 0:
                chain(nc.vector.tensor_tensor(den[:, r, b], rsum[:, r, b], esink[:, b], ALU.add))
            d = den if r == 0 else rsum
            chain(nc.vector.reciprocal(rden[:, r, b], d[:, r, b]))
            dve.wait_ge(bank_full[0], filled(f"attn{r}_v{b}", 0))
            for t in range(TT):
                ins = nc.vector.tensor_tensor(
                    tokbuf[:, t, 4 * b * HD:4 * (b + 1) * HD].rearrange("p (h d) -> p h d", h=4),
                    bank[:, 0, 4 * HD * t:4 * HD * (t + 1)].rearrange("p (h d) -> p h d", h=4),
                    rden[:, r, b, t, :].unsqueeze(2).to_broadcast([P, 4, HD]), ALU.mult)
            ins.then_inc(bank_free[0], 1)

        REC = [(HG_H, HG_D, qs, key, kend_t, scores, vh, state, fac[0]),
               (GLA_H, GLA_DV, qg, k_end, kend2_t, scores2, vg, state_2, ebuf[0])]

        def chunk_place(c):
            return c // 2, slice(CHUNK * (c % 2), CHUNK * (c % 2 + 1))

        def recurrence_keys_pe(pe, r, ready):
            heads, dv, q, k, kt, sc, v, st, _ = REC[r]
            per_bank = COLS // dv
            pe.wait_ge(sem(f"rec{r}_k_ready"), ready)
            for b in range(2 * heads // 4):
                pe.wait_ge(bank_free[b], fill(f"rec{r}_k", b))
                for n in range(4):
                    z = 4 * b + n
                    mm = pe.transpose(bank[:, b, n * P:(n + 1) * P],
                                      k[:, z // 2, (z % 2) * P:(z % 2 + 1) * P], ident[:])
                mm.then_inc(bank_full[b], 1)

        def recurrence_updates_pe(pe, r):
            heads, dv, q, k, kt, sc, v, st, _ = REC[r]
            per_bank = COLS // dv
            for b in range(2 * heads // 4):
                pe.wait_ge(bank_free[b], emptied(f"rec{r}_k", b))
            for c in range(3):
                t, ps = chunk_place(c)
                for n in range(2):
                    b = 2 * (c % 2) + n
                    pe.wait_ge(bank_free[b], fill(f"rec{r}_u{c}", b))
                    for hh in range(per_bank):
                        h = n * per_bank + hh
                        mm = pe.matmul(bank[:, b, hh * dv:(hh + 1) * dv], kt[ps, 2 * h + t, :],
                                       v[ps, t, h * dv:(h + 1) * dv], start=(hh == 0),
                                       stop=(hh == per_bank - 1), skip_group_check=True)
                    mm.then_inc(bank_full[b], 1)

        def recurrence_outputs_pe(pe, r):
            heads, dv, q, k, kt, sc, v, st, _ = REC[r]
            per_bank = COLS // dv
            for b in range(4):
                pe.wait_ge(bank_free[b], fill(f"rec{r}_o", b))
            for b in range(4):
                t, n = b // 2, b % 2
                for hh in range(per_bank):
                    h = n * per_bank + hh
                    part = slice(hh * dv, (hh + 1) * dv)
                    pe.matmul(bank[:, b, part], sc[:, 2 * h + t, :], v[:, t, h * dv:(h + 1) * dv],
                              start=(hh == 0), stop=False, skip_group_check=True)
                    for c in (2 * t, 2 * t + 1):
                        if c:
                            _, ps = chunk_place(c)
                            mm = pe.matmul(bank[ps, b, part], q[:, h, c * CHUNK:(c + 1) * CHUNK],
                                           st[c - 1][:, h * dv:(h + 1) * dv], start=False,
                                           stop=(hh == per_bank - 1), skip_group_check=True)
                mm.then_inc(bank_full[b], 1)

        def recurrence_keys_act(act, r):
            heads, dv, _, _, kt, _, _, _, sq = REC[r]
            for b in range(2 * heads // 4):
                act.wait_ge(bank_full[b], filled(f"rec{r}_k", b))
                nc.scalar.activation(kt[:, 4 * b:4 * b + 4, :],
                                     bank[:, b, :].rearrange("p (z k) -> p z k", z=4), ACT.Copy
                                     ).then_inc(bank_free[b], 1)

        def recurrence_squares_act(act, r):
            for b in range(4):
                act.wait_ge(bank_full[b], filled(f"rec{r}_o", b))
            nc.scalar.activation(junk[:], bank[:].rearrange("p b c -> p (b c)"), ACT.Square
                                 ).then_inc(sem(f"rec{r}_sq"), 1)

        def recurrence_states_dve(dve, r):
            heads, dv, _, _, _, _, _, st, _ = REC[r]
            per_bank = COLS // dv
            for c in range(3):
                for n in range(2):
                    b = 2 * (c % 2) + n
                    dve.wait_ge(bank_full[b], filled(f"rec{r}_u{c}", b))
                    part = slice(n * COLS, (n + 1) * COLS)
                    if c == 0:
                        ins = nc.vector.tensor_copy(st[0][:, part], bank[:, b, :])
                    else:
                        for hh in range(per_bank):
                            h = n * per_bank + hh
                            cols_ = slice(h * dv, (h + 1) * dv)
                            ins = nc.vector.scalar_tensor_tensor(
                                st[c][:, cols_], st[c - 1][:, cols_],
                                ends[:, r, h, c:c + 1],
                                bank[:, b, hh * dv:(hh + 1) * dv], ALU.mult, ALU.add)
                    ins.then_inc(bank_free[b], 1)
                    dve.wait_ge(bank_free[b], emptied(f"rec{r}_u{c}", b))

        def recurrence_outputs_dve(dve, r):
            heads, dv = REC[r][0], REC[r][1]
            per_bank = COLS // dv
            dve.wait_ge(sem(f"rec{r}_sq"), 1)
            groups = TT * heads
            nc.vector.tensor_reduce(hstat[:, r, 0, 0:groups],
                                    junk[:].rearrange("p (g v) -> p g v", v=dv), AX_X, ALU.add
                                    ).then_inc(sem(f"rec{r}_sum"), 1)
            dve.wait_ge(sem(f"rec{r}_rms"), 1)
            for b in range(4):
                part = slice(b * COLS, (b + 1) * COLS)
                ins = nc.vector.tensor_tensor(
                    junk[:, part].rearrange("p (g v) -> p g v", v=dv),
                    bank[:, b, :].rearrange("p (g v) -> p g v", v=dv),
                    hstat[:, r, 1, b * per_bank:(b + 1) * per_bank].unsqueeze(2)
                    .to_broadcast([P, per_bank, dv]), ALU.mult)
                ins.then_inc(bank_free[b], 1)
            dve.wait_ge(bank_free[3], emptied(f"rec{r}_o", 3))
            nc.vector.tensor_tensor(tokbuf[:, :, D // 2:], junk[:].rearrange("p (t c) -> p t c", t=TT),
                                    tokbuf[:, :, D // 2:], ALU.mult).then_inc(sem(f"heads{r}_ready"), 1)

        def recurrence_pool(pool, chain, r, gain):
            heads, dv = REC[r][0], REC[r][1]
            for t in range(TT):
                g = tokbuf[:, t, D // 2:].rearrange("p (h v) -> p h v", v=dv)
                chain(nc.gpsimd.tensor_tensor(g, g, gain[:].unsqueeze(1).to_broadcast([P, heads, dv]),
                                              ALU.mult))
            pool.wait_ge(sem(f"rec{r}_sum"), 1)
            n = TT * heads
            chain(nc.gpsimd.tensor_scalar(hstat[:, r, 1, 0:n], hstat[:, r, 0, 0:n], 1.0 / dv, EPS,
                                          ALU.mult, ALU.add))
            nc.gpsimd.tensor_tensor(hstat[:, r, 1, 0:n], hstat[:, r, 1, 0:n], minus_half[:, 0:n],
                                    ALU.pow).then_inc(sem(f"rec{r}_rms"), 1)

        ADA = [(8, 0)]

        w_ada = a["w_ada"].rearrange("l (k p) c -> (l p) k c", p=P)

        def weights(name):
            return a[name].rearrange("l (k p) c -> (l p) k c", p=P)

        W_in, W_ap, W_hp, W_out = (weights(n) for n in ("w_in", "w_attn_proj", "w_hgrn_proj", "w_out"))
        W_fi, W_fo = weights("w_ffn_in"), weights("w_ffn_out")
        W_in2, W_out2, W_fu2, W_fd2 = (weights(n) for n in
                                       ("w_in_2", "w_out_2", "w_ffn_up_2", "w_ffn_down_2"))
        W_pg, W_pp = weights("w_ple_gate_2"), weights("w_ple_proj_2")

        def cut(w, k0, nk, c0, ncol):
            return w[:, k0:k0 + nk, bass.ds(c0, ncol)]

        PARAMS = []

        def param(dst, src):
            PARAMS.append((dst, src))

        tiles_of = lambda ap: ap.rearrange("l (k p) -> (l k) p", p=P)
        ROW = {}
        at = 0
        for name, n in (("c", KD), ("g_pre_mix", KD), ("g_pre_ffn", KD), ("norm_mix_w_2", KD),
                        ("norm_ffn_w_2", KD), ("norm_ple_w_2", KD), ("hg_lower_bounds", 2 * HG_H),
                        ("b_gla_gate_2", GLA_H)):
            ROW[name] = at
            param(rows[at:at + n, :], tiles_of(a[name]))
            at += n
        N_ROWS = at

        def gain_of(name):
            return cols[:, ROW[name]:ROW[name] + KD]

        param(x[:, :, :], a["x"].rearrange("b (t p) d -> p (b t) d", p=P))
        N_FIRST = len(PARAMS)
        nconv = 2 * FFN // P
        param(conv_rows[:, 0:3, :], a["w_ffn_conv_2"].rearrange("l t (j p) -> j (l t) p", p=P))
        param(conv_rows[:, 3, :], tiles_of(a["b_ffn_conv_2"]))
        param(bias_rows[:], a["b_ada"][:, 0:2 * D].rearrange("l (k p) -> (l k) p", p=P))
        ctx.enter_context(nc.allow_non_contiguous_dma(reason="positions, one number a partition"))
        param(pos_i[:], a["positions"].rearrange("b (t p) -> p (b t)", p=P))
        param(sinks[:], a["attn_sinks"][0, :].partition_broadcast(P))
        param(hg_gain[:], a["hg_norm"][0, :].partition_broadcast(P))
        param(gla_gain[:], a["gla_norm_w_2"][0, :].partition_broadcast(P))
        N_ALL = len(PARAMS)
        bias_tab = a["att_rel_bias_2"]

        block = ctx.enter_context(nc.Block())

        @block.sync
        def _(sp):
            for i in range(N_FIRST):
                sp.dma_start(*PARAMS[i]).then_inc(sem("params_first"), 16)
            group = 0
            for n, g0 in ADA:
                with turns(sp, n // 2) as i:
                    for gg in range(2):
                        g = g0 + 2 * i + gg
                        for u in range(4):
                            sp.wait_ge(sem("ada_used"), 4 * g + u + 1)
                            sp.sem_inc(sem("slot_seen"), 1)
                            sp.dma_start(ada_raw[:, u], cut(w_ada, u * KU, KU, g * COLS, COLS)
                                         ).then_inc(ada_full[u], 16)

            def mix_in_source(i, g, k0, nk, ncol):
                if g > 18:
                    return cut((W_in, W_hp)[g - 19], k0, nk, (GB0, 0)[g - 19], ncol)
                if g > 10:
                    n, which = (g - 11) // 2, (g - 11) % 2
                    return cut((W_in, W_ap)[which], k0, nk, (GA0, 0)[which] + n * COLS, ncol)
                c0 = [Q0, Q0 + COLS, KV0, QH0, QH0 + COLS, FH0, FH0 + COLS, IH0, IH0 + COLS, GH0,
                      GH0 + COLS][g]
                return cut(W_in, k0, nk, c0, ncol)
            load_phase(sp, plan.mix_in, mix_in_source)
            load_phase(sp, plan.mix_gate, lambda i, g, k0, nk, ncol: cut(
                (W_in, W_hp)[g], k0, nk, (i + 1) * COLS + (GB0, 0)[g], ncol))
            load_phase(sp, plan.mix_out, lambda i, g, k0, nk, ncol: cut(
                W_out, k0, nk, i * 2 * COLS + g * COLS, ncol))
            for part, (g0, n) in enumerate(FFN_PARTS):
                load_phase(sp, plan.up1[part], lambda i, g, k0, nk, ncol: cut(
                    W_fi, k0, nk, (i + g0) * COLS + g * FFN, ncol))
                if part == 0:
                    sp.wait_ge(sem("x_ready"), 2)
                    sp.dma_start(gate_row[:], a["g_post_ffn"][0, :].partition_broadcast(P)
                                 ).then_inc(sem("ffn_gain_full"), 16)
                load_phase(sp, plan.down1[part], lambda i, g, k0, nk, ncol: cut(
                    W_fo, 4 * g0 + k0, nk, i * 2 * COLS + g * COLS, ncol))

            def mix_in2_source(i, g, k0, nk, ncol):
                if g > 12:
                    return cut(W_out2, k0, nk, (g - 13) * COLS, ncol)
                c0 = [0, COLS, A2, A2 + COLS, 2 * A2, 2 * A2 + COLS, QG0, KG0, LR0, RG0, RG0 + COLS,
                      VG0, VG0 + COLS][g]
                return cut(W_in2, k0, nk, c0, ncol)
            load_phase(sp, plan.mix_in2, mix_in2_source)
            load_phase(sp, plan.mix_out2, lambda i, g, k0, nk, ncol: cut(
                W_out2, k0 + A2 // P, nk, i * 2 * COLS + g * COLS, ncol))
            for part, (g0, n) in enumerate(FFN_PARTS):
                load_phase(sp, plan.up2[part], lambda i, g, k0, nk, ncol: cut(
                    W_fu2, k0, nk, (i + g0) * COLS + g * FFN, ncol))
                load_phase(sp, plan.down2[part], lambda i, g, k0, nk, ncol: cut(
                    W_fd2, 4 * g0 + k0, nk, i * 2 * COLS + g * COLS, ncol))
            load_phase(sp, plan.ple, lambda i, g, k0, nk, ncol: cut(
                (W_pg, W_pp)[g % 2], k0, nk, g // 2 * COLS, ncol))
            o = out.rearrange("b (t p) d -> p (b t) d", p=P)
            for t in range(TT):
                sp.wait_ge(sem("result"), t + 1)
                sp.dma_start(o[:, t, :], tokbuf[:, t, :]).then_inc(sem("stored"), 16)
            sp.wait_ge(sem("stored"), 16 * TT)

        @block.scalar
        def _(act):
            for i in range(N_FIRST, N_ALL):
                act.dma_start(*PARAMS[i]).then_inc(sem("params"), 16)
            act.wait_ge(sem("angles"), 1)
            nc.scalar.activation(trig[:].rearrange("p s t f -> p s (t f)"), rope[:, 5],
                                 ACT.Sin).then_inc(sem("trig"), 1)
            act.wait_ge(sem("lb_shifted"), 2)
            nc.scalar.activation(lb[:, 3:5, :], lb[:, 1:3, :], ACT.Exp).then_inc(sem("lb_exp"), 1)
            act.wait_ge(sem("params_first"), 16 * N_FIRST)
            squares_act(act, 0, x)
            split_act(act, "norm0", h_hi, KD, a_cols[:, 0, :], mod_cols[:, 0:KD])
            ph = plan.mix_in
            split_w_hi(act, ph, 0, 0, 4)
            for g in range(len(ph.groups)):
                split_w_hi(act, ph, 0, *span(ph, g))
                if g == 9:
                    act.wait_ge(sem("f_ready"), 1)
                    nc.scalar.activation(logf[:], logf[:], ACT.Ln).then_inc(sem("logf_ready"), 1)
                if g in LEVELS_AT:
                    for n in LEVELS_AT[g]:
                        act.wait_ge(sem("level_diff"), 2 * (n + 1))
                        nc.scalar.activation(fac[n % 2][:], fac[n % 2][:], ACT.Exp
                                             ).then_inc(sem("level_exp"), 1)
                if g == 16:
                    for b in range(4):
                        act.wait_ge(bank_free[b], emptied(f"level{len(LEVELS) - 1}", b))
                    nc.scalar.activation(fac[0][:], logf[:], ACT.Exp).then_inc(sem("decay_exp"), 1)
                    act.wait_ge(sem("decay_diff"), 1)
                    nc.scalar.activation(fac[1][:], fac[1][:], ACT.Exp).then_inc(sem("decay_exp"), 1)
                act.wait_ge(w_used, ph.done(0, g))
                ps, free = psum[ph.pair[g]], psum_free[ph.pair[g]]
                if g < 2:
                    nc.scalar.activation(
                        qk_tok[:, :, 8 * g:8 * g + 8, :], ps[:].rearrange("p t (h d) -> p t h d", d=HD),
                        ACT.Copy, scale=HD ** -0.5).then_inc(free, 1)
                elif g == 2:
                    for t in range(TT):
                        for dup in range(2):
                            nc.scalar.activation(
                                qk_tok[:, t, ATT_H:, :].rearrange("p (k u) d -> p k u d", u=2)[:, :, dup, :],
                                ps[:, t, 0:KV_W].rearrange("p (k d) -> p k d", d=HD), ACT.Copy)
                    nc.scalar.activation(v_tok[:], ps[:, :, KV_W:2 * KV_W], ACT.Copy
                                         ).then_inc(free, 1)
                elif g < 5:
                    nc.scalar.activation(qs[:, 4 * (g - 3):4 * (g - 2), :].rearrange("p h t -> p (h t)"),
                                         ps[:].rearrange("p b c -> p (b c)"), ACT.Silu
                                         ).then_inc(free, 1)
                elif g < 7:
                    nc.scalar.activation(logf[:, 4 * (g - 5):4 * (g - 4), :].rearrange("p h t -> p (h t)"),
                                         ps[:].rearrange("p b c -> p (b c)"), ACT.Sigmoid
                                         ).then_inc(free, 1)
                elif g < 9:
                    nc.scalar.activation(vh[:, :, (g - 7) * COLS:(g - 6) * COLS], ps[:], ACT.Copy
                                         ).then_inc(free, 1)
                elif g < 11:
                    nc.scalar.activation(tokbuf[:, :, D // 2 + (g - 9) * COLS:D // 2 + (g - 8) * COLS],
                                         ps[:], ACT.Sigmoid).then_inc(free, 1)
                elif g < 19 and g % 2:
                    if g > 11:
                        act.wait_ge(psum_free[ph.pair[g - 1]], ph.freed(0, g - 1))
                    nc.scalar.activation(sig_a[:], ps[:], ACT.Sigmoid).then_inc(free, 1)
                elif g == 19:
                    nc.scalar.activation(sig_b[:], ps[:], ACT.Sigmoid).then_inc(free, 1)
                if g == 3:
                    for b in range(5):
                        dst = q_t[:, 2 * b:2 * b + 2, :] if b < 4 else k_t[:]
                        act.wait_ge(bank_full[b % 4], filled("rope", b % 4, b // 4))
                        nc.scalar.activation(dst, bank[:, b % 4, :].rearrange("p (k t) -> p k t", k=2),
                                             ACT.Copy).then_inc(bank_free[b % 4], 1)
                if 5 <= g < 9:
                    turn_act(act, 0, g - 5, pt)
                if 4 <= g < 8:
                    softmax_act(act, 0, g - 4, sm)
                if g == 10:
                    split_act(act, "att0", att_hi, ATT_W // P)
                if g == 16:
                    recurrence_keys_act(act, 0)
                if g == 18:
                    recurrence_squares_act(act, 0)
                    act.dma_start(x[:, :, :], a["x"].rearrange("b (t p) d -> p (b t) d", p=P)
                                  ).then_inc(sem("x_again"), 16)
                if g == 19:
                    split_act(act, "heads0", rec_hi, HG_W // P)
            act.wait_ge(sem("mod_summed"), len(plan.mix_in.sums))
            act.dma_start(gate_row[:], a["g_post_mix"][0, :].partition_broadcast(P)
                          ).then_inc(sem("mix_gain_full"), 16)
            act.wait_ge(psum_free[plan.mix_in.pair[20]], plan.mix_in.freed(0, 20))
            ph = plan.mix_gate
            with turns(act, ph.iters) as i:
                for g in range(2):
                    split_w_hi(act, ph, i, *span(ph, g))
                    if g == 0:
                        act.wait_ge(w_used, ph.done(i, g))
                        act.wait_ge(psum_free[1], ph.freed(i, 1) - 1)
                        nc.scalar.activation(sig_b[:], psum[0][:], ACT.Sigmoid
                                             ).then_inc(psum_free[0], 1)
            split_act(act, "merged", h_hi, KD)

            ph = plan.mix_out
            with turns(act, ph.iters) as i:
                for g in range(2):
                    split_w_hi(act, ph, i, *span(ph, g))
                    act.wait_ge(w_used, ph.done(i, g))
                    nc.scalar.activation(tokbuf[:, :, bass.ds(i * 2 * COLS + g * COLS, COLS)],
                                         psum[g][:], ACT.Copy).then_inc(psum_free[g], 1)
            act.wait_ge(psum_free[1], plan.mix_out.freed(1, 1))
            act.wait_ge(psum_free[0], plan.mix_out.freed(1, 0))
            act.wait_ge(sem("mod_summed"), 12)
            squares_act(act, 1, tokbuf)
            squares_act(act, 2, x, ready=0)
            split_act(act, "norm1", h_hi, KD, a_cols[:, 1, :], mod_cols[:, 3 * KD:4 * KD])
            for part, (g0, n) in enumerate(FFN_PARTS):
                ph = plan.up1[part]
                n0 = g0
                with turns(act, ph.iters) as i:
                    split_w_hi(act, ph, i, *span(ph, 0))
                    act.wait_ge(w_used, ph.done(i, 0))
                    act.wait_ge(psum_free[1], ph.freed(i, 1) - 1)
                    nc.scalar.activation(act_g[:], psum[0][:].rearrange("p b (f t) -> p (b f) t", t=TOK),
                                         ACT.Silu).then_inc(psum_free[0], 1)
                    split_w_hi(act, ph, i, *span(ph, 1))
                ph = plan.down1[part]
                with turns(act, ph.iters) as i:
                    for g in range(2):
                        split_w_hi(act, ph, i, *span(ph, g))
                        if part == 0:
                            act.wait_ge(w_used, ph.done(i, g))
                            nc.scalar.activation(tokbuf[:, :, bass.ds(i * 2 * COLS + g * COLS, COLS)],
                                                 psum[g][:], ACT.Copy).then_inc(psum_free[g], 1)
            act.wait_ge(psum_free[1], plan.down1[1].freed(1, 1))
            act.wait_ge(sem("mod_summed"), 16)
            squares_act(act, 3, tokbuf)
            squares_act(act, 4, x, ready=2)
            act.dma_start(toep[:], bass.AP(tensor=bias_tab.tensor, offset=DIST - (P - 1),
                                           ap=[[1, P], [2 * DIST + 1, ATT_H], [1, TOK]])
                          ).then_inc(sem("toep_full"), 16)
            split_act(act, "norm2", h_hi, KD, gain_of("norm_mix_w_2"))
            act.wait_ge(sem("rms"), 5)
            act.dma_start(w_up_g[:], a["w_gla_gate_up_2"][0]).then_inc(sem("w_up_g_full"), 16)

            ph = plan.mix_in2
            for g in range(len(ph.groups)):
                split_w_hi(act, ph, 0, *span(ph, g))
                if g == 11:
                    act.wait_ge(sem("gate_abs"), 1)
                    nc.scalar.activation(ebuf[0][:], ebuf[0][:], ACT.Exp, scale=-1.0
                                         ).then_inc(sem("gate_exp"), 1)
                    act.wait_ge(sem("gate_exp"), 1)
                    nc.scalar.activation(ebuf[0][:], ebuf[0][:], ACT.Ln, bias=1.0
                                         ).then_inc(sem("gate_ln"), 1)
                if g == 12:
                    act.wait_ge(sem("gla_sum"), 2)
                    nc.scalar.activation(ebuf[0][:], lg[:], ACT.Exp).then_inc(sem("gla_exp"), 1)
                    nc.scalar.activation(ebuf[1][:], lg[:], ACT.Exp, scale=-1.0
                                         ).then_inc(sem("gla_exp"), 1)
                    act.wait_ge(sem("gla_diff"), 1)
                    nc.scalar.activation(k_end[:], k_end[:], ACT.Exp).then_inc(sem("gla_exp"), 1)
                if g == 14:
                    recurrence_squares_act(act, 1)
                if g == 15:
                    split_act(act, "heads1", h_hi[:, A2 // P:, :], GLA_W // P)
                if g > 12:
                    continue
                act.wait_ge(w_used, ph.done(0, g))
                ps, free = psum[ph.pair[g]], psum_free[ph.pair[g]]
                flat = ps[:].rearrange("p b (f t) -> p (b f) t", t=TOK)
                if g < 2:
                    nc.scalar.activation(q2_t[:, 4 * g:4 * g + 4, :], flat, ACT.Copy,
                                         scale=HD ** -0.5).then_inc(free, 1)
                elif g < 4:
                    nc.scalar.activation(k2_t[:, 4 * (g - 2):4 * (g - 1), :], flat, ACT.Copy
                                         ).then_inc(free, 1)
                elif g < 6:
                    nc.scalar.activation(va[:, :, (g - 4) * COLS:(g - 3) * COLS], ps[:], ACT.Copy
                                         ).then_inc(free, 1)
                elif g == 6:
                    nc.scalar.activation(qg[:], flat, ACT.Copy).then_inc(free, 1)
                elif g == 7:
                    nc.scalar.activation(kg[:], flat, ACT.Copy).then_inc(free, 1)
                elif g == 8:
                    nc.scalar.activation(lr_tok[:], ps[:, :, 0:RANK], ACT.Copy).then_inc(free, 1)
                elif g < 11:
                    nc.scalar.activation(tokbuf[:, :, D // 2 + (g - 9) * COLS:D // 2 + (g - 8) * COLS],
                                         ps[:], ACT.Silu).then_inc(free, 1)
                else:
                    act.wait_ge(bank_full[3], filled("attn1_s3", 3))
                    nc.scalar.activation(vg[:, :, (g - 11) * COLS:(g - 10) * COLS], ps[:], ACT.Copy
                                         ).then_inc(free, 1)
                if 7 <= g < 11:
                    turn_act(act, 1, g - 7, pt2)
                if 6 <= g < 10:
                    softmax_act(act, 1, g - 6, sm2)
                if g == 9:
                    act.wait_ge(bank_full[0], filled("low_rank", 0))
                    nc.scalar.activation(gate_lr[:], bank[0:RANK, 0, 0:TOK], ACT.Copy
                                         ).then_inc(bank_free[0], 1)
                if g == 12:
                    split_act(act, "att1", h_hi, A2 // P)
                    recurrence_keys_act(act, 1)
            ph = plan.mix_out2
            with turns(act, ph.iters) as i:
                for g in range(2):
                    split_w_hi(act, ph, i, *span(ph, g))
            act.wait_ge(psum_free[1], ph.freed(1, 1))
            squares_act(act, 5, x)
            split_act(act, "norm3", h_hi, KD, gain_of("norm_ffn_w_2"))
            for part, (g0, n) in enumerate(FFN_PARTS):
                ph = plan.up2[part]
                with turns(act, ph.iters) as i:
                    for g in range(2):
                        split_w_hi(act, ph, i, *span(ph, g))
                        act.wait_ge(w_used, ph.done(i, g))
                        if g == 0:
                            act.wait_ge(sem("hid_ready"), 1 + g0 + i)
                        dst = (act_g, act_u)[g]
                        for f in range(4):
                            c = bass.ds((i + g0) * 4 + g * (FFN // P) + f, 1)
                            nc.scalar.activation(dst[:, f, :], psum[g][:, f // 2, (f % 2) * TOK:(f % 2 + 1) * TOK],
                                                 ACT.Identity, scale=conv_cols[:, 2, c],
                                                 bias=conv_cols[:, 3, c]).then_inc(sem("conv_tap2"), 1)
                        if g == 0:
                            act.wait_ge(psum_free[0], ph.freed(i, 0))
                            nc.scalar.activation(act_g[:], act_g[:], ACT.Gelu_apprx_tanh
                                                 ).then_inc(sem("gelu"), 1)
                ph = plan.down2[part]
                with turns(act, ph.iters) as i:
                    for g in range(2):
                        split_w_hi(act, ph, i, *span(ph, g))
            act.wait_ge(psum_free[1], plan.down2[1].freed(1, 1))
            act.dma_start(p_tok[:], a["p_2"].rearrange("l b (t p) c -> p (l b t) c", p=P)
                          ).then_inc(sem("p_full"), 16)
            act.dma_start(out_row[:], a["final_norm_w_2"].partition_broadcast(P)
                          ).then_inc(sem("out_row_full"), 16)
            squares_act(act, 6, x)
            split_act(act, "ple", p_hi, 2)
            split_act(act, "norm4", h_hi, KD, gain_of("norm_ple_w_2"))
            ph = plan.ple
            for g in range(len(ph.groups)):
                split_w_hi(act, ph, 0, *span(ph, g, True))
                if g % 2 == 0:
                    act.wait_ge(w_used, ph.done(0, g))
                    if g:
                        act.wait_ge(sem("ple_added"), g // 2)
                    nc.scalar.activation(sig_p[:], psum[0][:], ACT.Sigmoid).then_inc(psum_free[0], 1)
            act.wait_ge(sem("ple_added"), 4)
            squares_act(act, 7, x)

        @block.vector
        def _(dve):
            chain = Chain(dve, "dve_order")
            dve.sem_inc(split_lo, 8)
            dve.sem_inc(psum_free[0], 1)
            dve.sem_inc(psum_free[1], 1)
            for b in range(4):
                dve.sem_inc(bank_free[b], 1)
            dve.sem_inc(sem("ada_used"), 4)
            dve.sem_inc(sem("ada_read"), 2)
            dve.wait_ge(bank_full[0], filled("cols", 0))
            nc.vector.tensor_copy(cols[:, 0:N_ROWS], bank[:, 0, 0:N_ROWS]).then_inc(bank_free[0], 1)
            for b in range(4):
                dve.wait_ge(bank_full[b], filled("conv", b))
                nc.vector.tensor_copy(conv_cols[:, b, :], bank[:, b, 0:nconv]).then_inc(bank_free[b], 1)
            dve.wait_ge(bank_full[0], filled("bias", 0))
            nc.vector.tensor_copy(bias_cols[:], bank[:, 0, 0:2 * KD]).then_inc(bank_free[0], 1)
            dve.wait_ge(bank_free[0], emptied("bias", 0))
            dve.wait_ge(bank_free[0], emptied("cols", 0))

            dve.wait_ge(sem("params"), 16 * (N_ALL - N_FIRST))
            chain(nc.vector.tensor_copy(pos_f[:], pos_i[:]))
            dve.wait_ge(sem("freqs"), 1)
            for t in range(TT):
                for s in range(2):
                    chain(nc.vector.tensor_scalar(rope[:, 0, s, t * ROT_HALF:(t + 1) * ROT_HALF],
                                                  invf[:], pos_f[:, t:t + 1], None, ALU.mult))
            for s in range(2):
                chain(nc.vector.tensor_scalar(rope[:, 1, s, :], rope[:, 0, s, :],
                                              float(1 / (2 * np.pi)), 0.25 * s, ALU.mult, ALU.add))
            chain(nc.vector.tensor_scalar(rope[:, 2], rope[:, 1], ROUNDER, None, ALU.add))
            chain(nc.vector.tensor_scalar(rope[:, 2], rope[:, 2], ROUNDER, None, ALU.subtract))
            src = 0
            for n, part in enumerate(TURN_PARTS):
                chain(nc.vector.scalar_tensor_tensor(rope[:, 3 + n % 2], rope[:, 2], -part,
                                                     rope[:, src], ALU.mult, ALU.add))
                src = 3 + n % 2
            chain(nc.vector.tensor_scalar(rope[:, src, 1, :], rope[:, src, 1, :], float(np.pi / 2),
                                          None, ALU.add))
            nc.vector.tensor_scalar(rope[:, 5], rope[:, src], 3.1415925, -3.1415925, ALU.min, ALU.max
                                    ).then_inc(sem("angles"), 1)
            l0 = ROW["hg_lower_bounds"]
            chain(nc.vector.tensor_tensor(lb[:, 0, :], cols[:, l0:l0 + HG_H],
                                          cols[:, l0 + HG_H:l0 + 2 * HG_H], ALU.max))
            for n in range(2):
                nc.vector.tensor_tensor(lb[:, 1 + n, :], cols[:, l0 + n * HG_H:l0 + (n + 1) * HG_H],
                                        lb[:, 0, :], ALU.subtract).then_inc(sem("lb_shifted"), 1)
            dve.wait_ge(sem("lb_exp"), 1)
            chain(nc.vector.tensor_tensor(lb[:, 0, :], lb[:, 3, :], lb[:, 4, :], ALU.add))
            chain(nc.vector.reciprocal(lb[:, 5, :], lb[:, 0, :]))
            chain(nc.vector.tensor_tensor(lb[:, 0, :], lb[:, 3, :], lb[:, 5, :], ALU.mult))
            chain(nc.vector.tensor_scalar(lb[:, 1, :], lb[:, 0, :], -1.0, 1.0, ALU.mult, ALU.add))

            for n, g0 in ADA:
                with turns(dve, n // 2) as i:
                    for gg in range(2):
                        g = g0 + 2 * i + gg
                        dve.wait_ge(sem("ada_summed"), g + 1)
                        for k in range(KD):
                            if k % KU == 0:
                                dve.wait_ge(ada_full[k // KU], 16 * (g + 1))
                            unit = ada_raw[:, k // KU, k % KU, :]
                            cc = cols[:, ROW["c"] + k:ROW["c"] + k + 1]
                            if k == 0:
                                ins = nc.vector.tensor_scalar(ada_acc[:, gg, :], unit, cc, None, ALU.mult)
                            else:
                                if k % KU == 0:
                                    dve.wait_ge(sem("ada_used"), 4 + 4 * g + k // KU)
                                else:
                                    dve.wait_ge(sem("ada_order"), 12 * g + 3 * (k // KU) + k % KU)
                                ins = nc.vector.scalar_tensor_tensor(ada_acc[:, gg, :], unit, cc,
                                                                     ada_acc[:, gg, :], ALU.mult, ALU.add)
                            ins.then_inc(sem("ada_used") if k % KU == KU - 1 else sem("ada_order"), 1)
                    for gg in range(2):
                        g = g0 + 2 * i + gg
                        dve.wait_ge(sem("ada_summed"), g + 3)
                        nc.vector.tensor_tensor(mod_cols[:, bass.ds(4 * g, 4)], bank[:, gg, 0:4],
                                                bias_cols[:, bass.ds(4 * g, 4)], ALU.add
                                                ).then_inc(sem("ada_read"), 1)
            dve.wait_ge(sem("ada_read"), 10)

            def modulate_dve(n):
                s0 = (3 * n + 1) * KD
                at = ROW[("g_pre_mix", "g_pre_ffn")[n]]
                chain(nc.vector.scalar_tensor_tensor(a_cols[:, n, :], mod_cols[:, s0:s0 + KD], 1.0,
                                                     cols[:, at:at + KD], ALU.add, ALU.mult))

            modulate_dve(0)
            normed_dve(dve, 0)
            split_dve(dve, "norm0", h_hi, h_lo, KD, a_cols[:, 0, :], mod_cols[:, 0:KD])

            def pick(stage, sc, mask, nbanks):
                for b in range(nbanks):
                    dve.wait_ge(bank_full[b], filled(stage, b))
                    nc.vector.copy_predicated(
                        sc[:, 4 * b:4 * b + 4, :],
                        mask.bitcast(I32).unsqueeze(1).to_broadcast([P, 4, P]),
                        bank[:, b, :].rearrange("p (z t) -> p z t", z=4)).then_inc(bank_free[b], 1)

            def level_factors(n):
                half = LEVELS[n]
                dve.wait_ge(sem("level_exp"), n + 1)
                for part, other in ((slice(half, 2 * half), qs), (slice(0, half), key)):
                    v_ = fac[n % 2][:].rearrange("p h (b e) -> p (h b) e", e=2 * half)[:, :, part]
                    o_ = other[:].rearrange("p h (b e) -> p (h b) e", e=2 * half)[:, :, part]
                    nc.vector.tensor_tensor(v_, v_, o_, ALU.mult).then_inc(sem("level_fac"), 1)

            ph = plan.mix_in
            split_w_lo(dve, ph, 0, 0, 4)
            for g in range(len(ph.groups)):
                split_w_lo(dve, ph, 0, *span(ph, g))
                for n in LEVELS_AT.get(g, ()):
                    level_factors(n)
                if g == 16:
                    dve.wait_ge(sem("decay_exp"), 1)
                    nc.vector.tensor_copy(ends[:, 0], fac[0][:].rearrange("p h (c e) -> p h c e", e=CHUNK)
                                          [:, :, :, CHUNK - 1]).then_inc(sem("rec0_k_ready"), 1)
                    nc.vector.tensor_tensor(qs[:], qs[:], fac[0][:], ALU.mult).then_inc(sem("rec0_k_ready"), 1)
                    dve.wait_ge(sem("decay_exp"), 2)
                    nc.vector.tensor_tensor(key[:], key[:], fac[1][:], ALU.mult).then_inc(sem("rec0_k_ready"), 1)
                    dve.wait_ge(sem("rec0_k_ready"), 3)
                if 12 <= g < 19 and g % 2 == 0:
                    dve.wait_ge(psum_free[ph.pair[g - 1]], ph.freed(0, g - 1))
                    dve.wait_ge(w_used, ph.done(0, g))
                    nc.vector.tensor_tensor(merged_att[(g - 12) // 2], sig_a[:],
                                            psum[ph.pair[g]][:], ALU.mult
                                            ).then_inc(psum_free[ph.pair[g]], 1)
                if g == 20:
                    dve.wait_ge(psum_free[ph.pair[19]], ph.freed(0, 19))
                    dve.wait_ge(w_used, ph.done(0, g))
                    nc.vector.tensor_tensor(part_b[:], sig_b[:], psum[ph.pair[g]][:], ALU.mult
                                            ).then_inc(psum_free[ph.pair[g]], 1)
                if 6 <= g < 10:
                    values_dve(dve, chain, 0, g - 6)
                if 4 <= g < 8:
                    softmax_dve(dve, chain, 0, g - 4, sm, band)
                if g == 8:
                    for n in (5, 6):
                        dve.wait_ge(psum_free[ph.pair[n]], ph.freed(0, n))
                    for h in range(HG_H):
                        ins = nc.vector.tensor_scalar(logf[:, h, :], logf[:, h, :], lb[:, 1, h:h + 1],
                                                      lb[:, 0, h:h + 1], ALU.mult, ALU.add)
                    chain(ins)
                    nc.vector.tensor_scalar(key[:], logf[:], -1.0, 1.0, ALU.mult, ALU.add
                                            ).then_inc(sem("f_ready"), 1)
                if g == 9:
                    dve.wait_ge(sem("logf_ready"), 1)
                    flat = logf[:].rearrange("p h t -> p (h t)")
                    for n in range(4):
                        seg = flat[:, n * COLS:(n + 1) * COLS]
                        nc.vector.tensor_tensor_scan(seg, scan_keep[:], seg, 0.0, ALU.mult, ALU.add
                                                     ).then_inc(sem("scanned"), 1)
                if g == 10:
                    split_dve(dve, "att0", att_hi, att_lo, ATT_W // P)
                    dve.wait_ge(sem("scores_zero"), 1)
                    pick("diag0", scores, ident[:], 4)
                if g in LEVELS_AT:
                    for n in LEVELS_AT[g]:
                        before = f"level{n - 1}" if n else "diag0"
                        dve.wait_ge(bank_free[3], emptied(before, 3))
                        pick(f"level{n}", scores, level_mask[:, n, :], 4)
                if g == 17:
                    recurrence_states_dve(dve, 0)
                if g == 18:
                    recurrence_outputs_dve(dve, 0)
                if g == 19:
                    split_dve(dve, "heads0", rec_hi, rec_lo, HG_W // P)
                mod_dve(dve, ph, 0, g)
            dve.wait_ge(bank_free[3], emptied(mod_bank(ph, 0, len(ph.sums) - 1)[0], 3))
            modulate_dve(1)

            ph = plan.mix_gate
            with turns(dve, ph.iters) as i:
                for g in range(2):
                    split_w_lo(dve, ph, i, *span(ph, g))
                    if g == 1:
                        dve.wait_ge(psum_free[0], ph.freed(i, 0))
                        dve.wait_ge(w_used, ph.done(i, 1))
                        dve.wait_ge(sem("merged_sum"), i + 1)
                        nc.vector.tensor_tensor(part_b[:], sig_b[:], psum[1][:], ALU.mult
                                                ).then_inc(psum_free[1], 1)
            split_dve(dve, "merged", h_hi, h_lo, KD)
            ph = plan.mix_out
            with turns(dve, ph.iters) as i:
                for g in range(2):
                    split_w_lo(dve, ph, i, *span(ph, g))
                    if g == 0:
                        dve.wait_ge(sem("mix_gain_full"), 16)
                    mod_dve(dve, ph, i, g)
            dve.wait_ge(bank_free[3], emptied("mod_out", 3, 3))
            dve.wait_ge(sem("x_again"), 16)
            residual_dve(dve, chain, 1)
            normed_dve(dve, 2)
            split_dve(dve, "norm1", h_hi, h_lo, KD, a_cols[:, 1, :], mod_cols[:, 3 * KD:4 * KD])

            for part, (g0, n) in enumerate(FFN_PARTS):
                ph = plan.up1[part]
                with turns(dve, ph.iters) as i:
                    split_w_lo(dve, ph, i, *span(ph, 0))
                    split_w_lo(dve, ph, i, *span(ph, 1))
                    dve.wait_ge(psum_free[0], ph.freed(i, 0))
                    dve.wait_ge(w_used, ph.done(i, 1))
                    dve.wait_ge(sem("hid_lo"), g0 + i + 1)
                    nc.vector.tensor_tensor(hid[:], act_g[:],
                                            psum[1][:].rearrange("p b (f t) -> p (b f) t", t=TOK),
                                            ALU.mult).then_inc(psum_free[1], 1)
                ph = plan.down1[part]
                if part == 1:
                    for g in range(2):
                        dve.wait_ge(psum_free[g], plan.down1[0].freed(1, g))
                with turns(dve, ph.iters) as i:
                    for g in range(2):
                        if g == 0:
                            dve.wait_ge(sem("hid_lo"), g0 + n + 1)
                        split_w_lo(dve, ph, i, *span(ph, g))
                        if part == 1:
                            dve.wait_ge(w_used, ph.done(i, g))
                            y = tokbuf[:, :, bass.ds(i * 2 * COLS + g * COLS, COLS)]
                            nc.vector.tensor_tensor(y, y, psum[g][:], ALU.add).then_inc(psum_free[g], 1)
                        if g == 1:
                            dve.wait_ge(sem("ffn_gain_full"), 16)
                        mod_dve(dve, ph, i, g)
            dve.wait_ge(bank_free[3], emptied("mod_down1", 3, 1))
            residual_dve(dve, chain, 3)
            normed_dve(dve, 4)
            split_dve(dve, "norm2", h_hi, h_lo, KD, gain_of("norm_mix_w_2"))

            ph = plan.mix_in2
            for g in range(len(ph.groups)):
                split_w_lo(dve, ph, 0, *span(ph, g))
                if 8 <= g < 12:
                    values_dve(dve, chain, 1, g - 8)
                if 6 <= g < 10:
                    softmax_dve(dve, chain, 1, g - 6, sm2, chunked)
                if g == 10:
                    for f in range(GLA_H):
                        if f % 2 == 0:
                            dve.wait_ge(bank_full[f // 2], filled("gate", f // 2))
                        bias = cols[:, ROW["b_gla_gate_2"] + f:ROW["b_gla_gate_2"] + f + 1]
                        ins = nc.vector.tensor_scalar(k_end[:, f, :],
                                                      bank[:, f // 2, (f % 2) * TOK:(f % 2 + 1) * TOK],
                                                      bias, None, ALU.add)
                        if f % 2:
                            ins.then_inc(bank_free[f // 2], 1)
                    for b in range(2):
                        dve.wait_ge(bank_free[b], emptied("gate", b))
                    nc.vector.scalar_tensor_tensor(ebuf[0][:], k_end[:], -1.0, k_end[:], ALU.mult, ALU.max
                                                   ).then_inc(sem("gate_abs"), 1)
                    chain(nc.vector.tensor_scalar(k_end[:], k_end[:], 0.0, 1.0 / TAU, ALU.min, ALU.mult))
                if g == 11:
                    dve.wait_ge(sem("gate_ln"), 1)
                    chain(nc.vector.scalar_tensor_tensor(lg[:], ebuf[0][:], -1.0 / TAU, k_end[:],
                                                         ALU.mult, ALU.add))
                    flat = lg[:].rearrange("p h t -> p (h t)")
                    for n in range(2):
                        seg = flat[:, n * COLS:(n + 1) * COLS]
                        nc.vector.tensor_tensor_scan(seg, scan_keep[:], seg, 0.0, ALU.mult, ALU.add
                                                     ).then_inc(sem("gla_sum"), 1)
                    dve.wait_ge(sem("gla_sum"), 2)
                    chunks = lg[:].rearrange("p h (c e) -> p (h c) e", e=CHUNK)
                    nc.vector.tensor_tensor(
                        k_end[:].rearrange("p h (c e) -> p (h c) e", e=CHUNK),
                        chunks[:, :, CHUNK - 1:CHUNK].to_broadcast([P, GLA_H * TOK // CHUNK, CHUNK]), chunks,
                        ALU.subtract).then_inc(sem("gla_diff"), 1)
                if g == 12:
                    split_dve(dve, "att1", h_hi, h_lo, A2 // P)
                    dve.wait_ge(sem("gla_exp"), 1)
                    nc.vector.tensor_copy(ends[:, 1, 0:GLA_H], ebuf[0][:].rearrange(
                        "p h (c e) -> p h c e", e=CHUNK)[:, :, :, CHUNK - 1]).then_inc(sem("gla_fac"), 1)
                    nc.vector.scalar_tensor_tensor(qg[:], qg[:], GLA_DK ** -0.5, ebuf[0][:], ALU.mult, ALU.mult
                                                   ).then_inc(sem("gla_fac"), 1)
                    dve.wait_ge(sem("gla_exp"), 2)
                    nc.vector.tensor_tensor(ebuf[1][:], ebuf[1][:], kg[:], ALU.mult).then_inc(sem("gla_fac"), 1)
                    dve.wait_ge(sem("gla_exp"), 3)
                    nc.vector.tensor_tensor(k_end[:], k_end[:], kg[:], ALU.mult).then_inc(sem("rec1_k_ready"), 1)
                    dve.wait_ge(sem("scores2_zero"), 1)
                    pick("gla", scores2, causal[:], 2)
                if g > 12:
                    dve.wait_ge(w_used, ph.done(0, g))
                    xs = x[:, :, (g - 13) * COLS:(g - 12) * COLS]
                    nc.vector.tensor_tensor(xs, xs, psum[ph.pair[g]][:], ALU.add
                                            ).then_inc(psum_free[ph.pair[g]], 1)
                if g == 13:
                    recurrence_states_dve(dve, 1)
                if g == 14:
                    recurrence_outputs_dve(dve, 1)
                if g == 15:
                    split_dve(dve, "heads1", h_hi[:, A2 // P:, :], h_lo[:, A2 // P:, :],
                              GLA_W // P)


            ph = plan.mix_out2
            with turns(dve, ph.iters) as i:
                for g in range(2):
                    split_w_lo(dve, ph, i, *span(ph, g))
                    dve.wait_ge(w_used, ph.done(i, g))
                    xs = x[:, :, bass.ds(i * 2 * COLS + g * COLS, COLS)]
                    nc.vector.tensor_tensor(xs, xs, psum[g][:], ALU.add).then_inc(psum_free[g], 1)
            normed_dve(dve, 5)
            split_dve(dve, "norm3", h_hi, h_lo, KD, gain_of("norm_ffn_w_2"))

            for part, (g0, n) in enumerate(FFN_PARTS):
                ph = plan.up2[part]
                with turns(dve, ph.iters) as i:
                    for g in range(2):
                        split_w_lo(dve, ph, i, *span(ph, g))
                        dst = (act_g, act_u)[g]
                        dve.wait_ge(sem("conv_tap2"), 8 * (g0 + i) + 4 * g + 4)
                        for tap, back in ((1, 1), (0, 2)):
                            for f in range(4):
                                c = bass.ds((i + g0) * 4 + g * (FFN // P) + f, 1)
                                u = psum[g][:, f // 2, (f % 2) * TOK:(f % 2 + 1) * TOK - back]
                                ins = nc.vector.scalar_tensor_tensor(
                                    dst[:, f, back:], u, conv_cols[:, tap, c], dst[:, f, back:],
                                    ALU.mult, ALU.add)
                            if tap == 1:
                                ins.then_inc(sem("conv_tap1"), 1)
                                dve.wait_ge(sem("conv_tap1"), 2 * (g0 + i) + g + 1)
                        ins.then_inc(psum_free[g], 1)
                ph = plan.down2[part]
                with turns(dve, ph.iters) as i:
                    for g in range(2):
                        split_w_lo(dve, ph, i, *span(ph, g))
                        dve.wait_ge(w_used, ph.done(i, g))
                        xs = x[:, :, bass.ds(i * 2 * COLS + g * COLS, COLS)]
                        nc.vector.tensor_tensor(xs, xs, psum[g][:], ALU.add).then_inc(psum_free[g], 1)
            split_dve(dve, "ple", p_hi, p_lo, 2)
            normed_dve(dve, 6)
            split_dve(dve, "norm4", h_hi, h_lo, KD, gain_of("norm_ple_w_2"))
            ph = plan.ple
            for g in range(len(ph.groups)):
                split_w_lo(dve, ph, 0, *span(ph, g, True))
                if g % 2:
                    dve.wait_ge(psum_free[0], ph.freed(0, g - 1))
                    dve.wait_ge(w_used, ph.done(0, g))
                    nc.vector.tensor_tensor(sig_p[:], sig_p[:], psum[1][:], ALU.mult
                                            ).then_inc(psum_free[1], 1)
                    dve.wait_ge(psum_free[1], ph.freed(0, g))
                    xs = x[:, :, g // 2 * COLS:(g // 2 + 1) * COLS]
                    nc.vector.tensor_tensor(xs, xs, sig_p[:], ALU.add).then_inc(sem("ple_added"), 1)
            dve.wait_ge(sem("out_row_full"), 16)
            dve.wait_ge(sem("rms"), 8)
            for t in range(TT):
                nc.vector.scalar_tensor_tensor(tokbuf[:, t, :], x[:, t, :], stats[:, 7, 2 + t:3 + t],
                                               out_row[:], ALU.mult, ALU.mult).then_inc(sem("result"), 1)

        @block.gpsimd
        def _(pool):
            chain = Chain(pool, "pool_order")
            pool.sem_inc(sem("hid_lo"), 1)
            pool.sem_inc(sem("hid2_lo"), 1)
            pool.sem_inc(sem("hid_ready"), 1)

            def keep_where(view, base, channel, pattern, fill_value, op=ALU.is_ge):
                chain(nc.gpsimd.affine_select(out=view, in_=view, compare_op=op, fill=fill_value,
                                              base=base, pattern=pattern, channel_multiplier=channel))

            def split_hidden(pool, i, g0, name):
                nc.gpsimd.tensor_copy(hid_hi[:, bass.ds(4 * i, 4), :], hid[:]
                                      ).then_inc(sem(f"{name}_hi"), 1)
                pool.wait_ge(sem(f"{name}_hi"), g0 + i + 1)
                nc.gpsimd.tensor_tensor(hid_lo[:, bass.ds(4 * i, 4), :], hid[:],
                                        hid_hi[:, bass.ds(4 * i, 4), :].bitcast(F32), ALU.subtract
                                        ).then_inc(sem(f"{name}_lo"), 1)

            chain(nc.gpsimd.memset(ident[:], 0.0))
            nc.gpsimd.affine_select(out=ident[:], in_=ident[:], compare_op=ALU.not_equal, fill=1.0,
                                    base=0, pattern=[[-1, P]], channel_multiplier=1
                                    ).then_inc(sem("ident_ready"), 1)
            nc.gpsimd.memset(ones[:], 1.0).then_inc(sem("ones_ready"), 1)
            for f in range(ROT_HALF):
                ins = nc.gpsimd.memset(invf[:, f:f + 1], float(INV_FREQ[f]))
            ins.then_inc(sem("freqs"), 1)
            chain(nc.gpsimd.memset(minus_half[:], -0.5))
            rms_pool(pool, chain, 0)
            chain(nc.gpsimd.memset(band[:], 0.0))
            keep_where(band[:, 0:P], 0, 1, [[-1, P]], NEG)
            keep_where(band[:, P:2 * P], -1, -1, [[1, P]], NEG)
            keep_where(band[:, 2 * P:3 * P], 0, 1, [[-1, P]], NEG)
            chain(nc.gpsimd.memset(chunked[:], 0.0))
            keep_where(chunked[:, CHUNK:P], -CHUNK, 1, [[0, CHUNK]], NEG)
            keep_where(chunked[:, 2 * P + CHUNK:3 * P], -CHUNK, 1, [[0, CHUNK]], NEG)
            chain(nc.gpsimd.memset(level_mask[:], 0.0))
            for n, half in enumerate(LEVELS):
                blocks = P // (2 * half)
                view = level_mask[:, n, :].rearrange("p (b e) -> p b e", e=2 * half)[:, :, half:]
                chain(nc.gpsimd.memset(view, 1.0))
                keep_where(view, 0, 1, [[-2 * half, blocks], [0, half]], 0.0)
                keep_where(view, half - 1, -1, [[2 * half, blocks], [0, half]], 0.0)
            chain(nc.gpsimd.memset(causal[:], 1.0))
            view = causal[:].rearrange("p (b e) -> p b e", e=CHUNK)
            keep_where(view, 0, -1, [[CHUNK, 2], [1, CHUNK]], 0.0)
            keep_where(view, 0, 1, [[-CHUNK, 2], [0, CHUNK]], 0.0)
            chain(nc.gpsimd.memset(scan_keep[:], 1.0))
            chain(nc.gpsimd.memset(scan_keep[:].rearrange("p (c e) -> p c e", e=CHUNK)[:, :, 0:1], 0.0))
            pool.sem_inc(sem("masks_ready"), 1)

            pool.wait_ge(sem("trig"), 1)
            for g in range(3):
                pool.wait_ge(psum_free[plan.mix_in.pair[g]], plan.mix_in.freed(0, g))
            nh = ATT_H + 2 * KV_H
            for t in range(TT):
                one = qk_tok[:, t, :, 0:ROT_HALF]
                two = qk_tok[:, t, :, ROT_HALF:2 * ROT_HALF]
                sin = trig[:, 0, t, :].unsqueeze(1).to_broadcast([P, nh, ROT_HALF])
                cos = trig[:, 1, t, :].unsqueeze(1).to_broadcast([P, nh, ROT_HALF])
                for n, (v_, w_) in enumerate(((one, cos), (two, sin), (two, cos), (one, sin))):
                    chain(nc.gpsimd.tensor_tensor(rope_tmp[:, n], v_, w_, ALU.mult))
                nc.gpsimd.tensor_tensor(one, rope_tmp[:, 0], rope_tmp[:, 1], ALU.subtract
                                        ).then_inc(sem("roped"), 1)
                nc.gpsimd.tensor_tensor(two, rope_tmp[:, 2], rope_tmp[:, 3], ALU.add
                                        ).then_inc(sem("roped"), 1)
                pool.wait_ge(sem("roped"), 2 * t + 2)

            pool.wait_ge(bank_free[0], emptied("attn0_v3", 0))
            nc.gpsimd.memset(scores[:], 0.0).then_inc(sem("scores_zero"), 1)
            pool.wait_ge(sem("scanned"), 4)
            for n, half in enumerate(LEVELS):
                if n >= 2:
                    pool.wait_ge(bank_free[3], emptied(f"level{n - 2}", 3))
                nb = HG_H * TOK // (2 * half)
                b_ = logf[:].rearrange("p h (b e) -> p (h b) e", e=2 * half)
                f_ = fac[n % 2][:].rearrange("p h (b e) -> p (h b) e", e=2 * half)
                mid = b_[:, :, half - 1:half].to_broadcast([P, nb, half])
                nc.gpsimd.tensor_tensor(f_[:, :, half:], b_[:, :, half:], mid, ALU.subtract
                                        ).then_inc(sem("level_diff"), 1)
                nc.gpsimd.tensor_tensor(f_[:, :, 0:half], mid, b_[:, :, 0:half], ALU.subtract
                                        ).then_inc(sem("level_diff"), 1)
            for b in range(4):
                pool.wait_ge(bank_free[b], emptied(f"level{len(LEVELS) - 1}", b))
            chunks = logf[:].rearrange("p h (c e) -> p (h c) e", e=CHUNK)
            nc.gpsimd.tensor_tensor(
                fac[1][:].rearrange("p h (c e) -> p (h c) e", e=CHUNK),
                chunks[:, :, CHUNK - 1:CHUNK].to_broadcast([P, HG_H * TOK // CHUNK, CHUNK]), chunks,
                ALU.subtract).then_inc(sem("decay_diff"), 1)
            for g in (9, 10):
                pool.wait_ge(psum_free[plan.mix_in.pair[g]], plan.mix_in.freed(0, g))
            recurrence_pool(pool, chain, 0, hg_gain)

            for b in range(4):
                pool.wait_ge(bank_free[b], emptied("heads0", b))
            for n in (2, 3):
                pool.wait_ge(psum_free[plan.mix_in.pair[12 + 2 * n]], plan.mix_in.freed(0, 12 + 2 * n))
                chain(nc.gpsimd.tensor_copy(tokbuf[:, :, n * COLS:(n + 1) * COLS], merged_att[n]))
            pool.wait_ge(psum_free[plan.mix_in.pair[20]], plan.mix_in.freed(0, 20))
            first = tokbuf[:, :, 0:COLS]
            nc.gpsimd.tensor_tensor(first, first, part_b[:], ALU.add).then_inc(sem("merged_sum"), 1)
            ph = plan.mix_gate
            with turns(pool, ph.iters) as i:
                pool.wait_ge(psum_free[1], ph.freed(i, 1))
                now = tokbuf[:, :, bass.ds((i + 1) * COLS, COLS)]
                nc.gpsimd.tensor_tensor(now, now, part_b[:], ALU.add).then_inc(sem("merged_sum"), 1)
            rms_pool(pool, chain, 1)
            rms_pool(pool, chain, 2)
            for part, (g0, n) in enumerate(FFN_PARTS):
                ph = plan.up1[part]
                if part:
                    pool.wait_ge(w_used, plan.down1[0].done(1, 1))
                with turns(pool, n) as i:
                    pool.wait_ge(psum_free[1], ph.freed(i, 1))
                    split_hidden(pool, i, g0, "hid")
            rms_pool(pool, chain, 3)
            rms_pool(pool, chain, 4)
            chain(nc.gpsimd.memset(mirror[:], 0.0))
            nc.gpsimd.affine_select(out=mirror[:], in_=mirror[:], compare_op=ALU.not_equal, fill=1.0,
                                    base=-(P - 1), pattern=[[1, P]], channel_multiplier=1
                                    ).then_inc(sem("mirror_ready"), 1)
            pool.wait_ge(bank_free[0], emptied("attn1_v3", 0))
            nc.gpsimd.memset(scores2[:], 0.0).then_inc(sem("scores2_zero"), 1)
            for g in (9, 10):
                pool.wait_ge(psum_free[plan.mix_in2.pair[g]], plan.mix_in2.freed(0, g))
            recurrence_pool(pool, chain, 1, gla_gain)
            rms_pool(pool, chain, 5)
            for part, (g0, n) in enumerate(FFN_PARTS):
                ph = plan.up2[part]
                if part:
                    pool.wait_ge(w_used, plan.down2[0].done(1, 1))
                with turns(pool, n) as i:
                    pool.wait_ge(psum_free[1], ph.freed(i, 1))
                    pool.wait_ge(sem("gelu"), g0 + i + 1)
                    pool.wait_ge(sem("hid2_lo"), g0 + i + 1)
                    nc.gpsimd.tensor_tensor(hid[:], act_g[:], act_u[:], ALU.mult
                                            ).then_inc(sem("hid_ready"), 1)
                    pool.wait_ge(sem("hid_ready"), 2 + g0 + i)
                    split_hidden(pool, i, g0, "hid2")
            rms_pool(pool, chain, 6)
            rms_pool(pool, chain, 7)

        @block.tensor
        def _(pe):
            pe.sem_inc(w_used, 4)
            pe.sem_inc(sem("ada_summed"), 2)
            pe.wait_ge(sem("ident_ready"), 1)
            pe.wait_ge(sem("params_first"), 16 * N_FIRST)
            pe.wait_ge(bank_free[0], fill("cols", 0))
            pe.transpose(bank[:, 0, 0:N_ROWS], rows[0:N_ROWS, :], ident[0:N_ROWS, 0:N_ROWS]
                         ).then_inc(bank_full[0], 1)
            pe.wait_ge(sem("params"), 16 * (N_ALL - N_FIRST))
            for b in range(4):
                pe.wait_ge(bank_free[b], fill("conv", b))
                pe.transpose(bank[:, b, 0:nconv], conv_rows[:, b, :], ident[0:nconv, 0:nconv]
                             ).then_inc(bank_full[b], 1)

            pe.wait_ge(bank_free[0], fill("bias", 0))
            pe.transpose(bank[:, 0, 0:2 * KD], bias_rows[:], ident[0:2 * KD, 0:2 * KD]
                         ).then_inc(bank_full[0], 1)

            pe.wait_ge(sem("ones_ready"), 1)
            pe.wait_ge(bank_free[0], emptied("bias", 0))
            pe.wait_ge(bank_free[1], emptied("conv", 1))
            for n, g0 in ADA:
                with turns(pe, n // 2) as i:
                    for gg in range(2):
                        g = g0 + 2 * i + gg
                        pe.wait_ge(sem("ada_used"), 4 + 4 * g + 4)
                        pe.wait_ge(sem("ada_read"), g + 1)
                        for f in range(4):
                            mm = pe.matmul(bank[:, gg, f:f + 1], ada_acc[:, gg, f * P:(f + 1) * P],
                                           ones[:, 0:1], start=(f == 0), stop=(f == 3),
                                           skip_group_check=True)
                        mm.then_inc(sem("ada_summed"), 1)

            def gram(stage, stationary, moving, nbanks):
                for b in range(nbanks):
                    pe.wait_ge(bank_free[b], fill(stage, b))
                    for n in range(4):
                        z = 4 * b + n
                        part = slice((z % 2) * P, (z % 2 + 1) * P)
                        mm = pe.matmul(bank[:, b, n * P:(n + 1) * P], stationary[:, z // 2, part],
                                       moving[:, z // 2, part], start=(n == 0), stop=(n == 3),
                                       skip_group_check=True)
                    mm.then_inc(bank_full[b], 1)

            pe.wait_ge(sem("normed"), 2)
            transpose_pe(pe, "norm0", x, KD, 0)
            ph = plan.mix_in
            for g in range(len(ph.groups)):
                if g == 20:
                    products(pe, ph, 0, g, rec_hi, rec_lo, ready="heads0")
                elif g in (12, 14, 16, 18):
                    products(pe, ph, 0, g, att_hi, att_lo, ready="att0" if g == 12 else None)
                else:
                    products(pe, ph, 0, g, h_hi, h_lo, transposed=3 <= g < 7,
                             ready="norm0" if g == 0 else None)
                if g == 3:
                    pe.wait_ge(sem("roped"), 4)
                    for b in range(5):
                        pe.wait_ge(bank_free[b % 4], fill("rope", b % 4, b // 4))
                        for n in range(2):
                            for t in range(TT):
                                pair = 2 * b + n
                                mm = pe.transpose(
                                    bank[:, b % 4, (2 * n + t) * P:(2 * n + t + 1) * P],
                                    qk_tok[:, t, 2 * pair:2 * pair + 2, :].rearrange("p h d -> p (h d)"),
                                    ident[:])
                        mm.then_inc(bank_full[b % 4], 1)
                if 6 <= g < 10:
                    values_pe(pe, 0, g - 6, pt, v_tok)
                if 5 <= g < 9:
                    turn_pe(pe, 0, g - 5, sm)
                if g == 4:
                    pe.wait_ge(bank_free[0], emptied("rope", 0, 1))
                    for b in range(1, 4):
                        pe.wait_ge(bank_free[b], emptied("rope", b, 0))
                    pe.wait_ge(sem("masks_ready"), 1)
                if 4 <= g < 8:
                    scores_pe(pe, 0, g - 4, q_t, k_t, lambda h: h // (ATT_H // KV_H))
                if g == 10:
                    pe.wait_ge(bank_free[0], emptied("attn0_v3", 0))
                    transpose_pe(pe, "att0", tokbuf, ATT_W // P)
                    pe.wait_ge(sem("f_ready"), 1)
                    gram("diag0", key, qs, 4)
                if g in LEVELS_AT:
                    for n in LEVELS_AT[g]:
                        pe.wait_ge(sem("level_fac"), 2 * (n + 1))
                        gram(f"level{n}", fac[n % 2], fac[n % 2], 4)
                if g == 16:
                    recurrence_keys_pe(pe, 0, 3)
                if g == 17:
                    recurrence_updates_pe(pe, 0)
                if g == 18:
                    recurrence_outputs_pe(pe, 0)
                if g == 19:
                    pe.wait_ge(sem("heads0_ready"), 1)
                    transpose_pe(pe, "heads0", tokbuf, HG_W // P, first=D // 2 // P)
                mod_pe(pe, ph, 0, g)

            ph = plan.mix_gate
            with turns(pe, ph.iters) as i:
                products(pe, ph, i, 0, h_hi, h_lo)
                products(pe, ph, i, 1, rec_hi, rec_lo)
            pe.wait_ge(sem("merged_sum"), D // COLS)
            transpose_pe(pe, "merged", tokbuf, KD)
            ph = plan.mix_out
            with turns(pe, ph.iters) as i:
                for g in range(2):
                    products(pe, ph, i, g, h_hi, h_lo, ready="merged" if g == 0 else None)
                    mod_pe(pe, ph, i, g)
            pe.wait_ge(sem("normed"), 4)
            transpose_pe(pe, "norm1", x, KD, 2)
            for part, (g0, n) in enumerate(FFN_PARTS):
                ph = plan.up1[part]
                with turns(pe, ph.iters) as i:
                    for g in range(2):
                        products(pe, ph, i, g, h_hi, h_lo, transposed=True,
                                 ready="norm1" if g == 0 and part == 0 else None)
                ph = plan.down1[part]
                with turns(pe, ph.iters) as i:
                    for g in range(2):
                        products(pe, ph, i, g, hid_hi, hid_lo, hidden=(sem("hid_lo"), g0 + 2, g))
                        mod_pe(pe, ph, i, g)
            pe.wait_ge(sem("normed"), 6)
            transpose_pe(pe, "norm2", x, KD, 4)

            ph = plan.mix_in2
            pe.wait_ge(sem("toep_full"), 16)
            pe.wait_ge(sem("mirror_ready"), 1)
            for g in range(len(ph.groups)):
                products(pe, ph, 0, g, h_hi, h_lo, transposed=g < 4 or g in (6, 7),
                         ready={0: "norm2", 13: "att1"}.get(g))
                if 8 <= g < 12:
                    values_pe(pe, 1, g - 8, pt2, va)
                if 7 <= g < 11:
                    turn_pe(pe, 1, g - 7, sm2)
                if g == 6:
                    for n in range(6):
                        pe.wait_ge(psum_free[ph.pair[n]], ph.freed(0, n))
                if 6 <= g < 10:
                    scores_pe(pe, 1, g - 6, q2_t, k2_t, lambda h: h // 2)
                if g == 9:
                    pe.wait_ge(psum_free[ph.pair[8]], ph.freed(0, 8))
                    pe.wait_ge(bank_free[0], fill("low_rank", 0))
                    for t in range(TT):
                        mm = pe.matmul(bank[0:RANK, 0, t * P:(t + 1) * P], lr_tok[:, t, :], ident[:],
                                       start=(t == 0), stop=(t == 1), skip_group_check=True)
                    mm.then_inc(bank_full[0], 1)
                if g == 10:
                    pe.wait_ge(bank_free[0], emptied("low_rank", 0))
                    pe.wait_ge(sem("w_up_g_full"), 16)
                    for f in range(GLA_H):
                        if f % 2 == 0:
                            pe.wait_ge(bank_free[f // 2], fill("gate", f // 2))
                        mm = pe.matmul(bank[:, f // 2, (f % 2) * TOK:(f % 2 + 1) * TOK],
                                       w_up_g[:, f * P:(f + 1) * P], gate_lr[:], start=(f % 2 == 0),
                                       stop=(f % 2 == 1), skip_group_check=True)
                        if f % 2:
                            mm.then_inc(bank_full[f // 2], 1)
                if g == 12:
                    pe.wait_ge(bank_free[0], emptied("attn1_v3", 0))
                    transpose_pe(pe, "att1", tokbuf, A2 // P)
                    pe.wait_ge(sem("gla_fac"), 3)
                    gram("gla", ebuf[1], qg, 2)
                    recurrence_keys_pe(pe, 1, 1)
                if g == 13:
                    for n in (11, 12):
                        pe.wait_ge(psum_free[ph.pair[n]], ph.freed(0, n))
                    recurrence_updates_pe(pe, 1)
                if g == 14:
                    recurrence_outputs_pe(pe, 1)
                if g == 15:
                    pe.wait_ge(sem("heads1_ready"), 1)
                    transpose_pe(pe, "heads1", tokbuf, GLA_W // P, first=A2 // P)
            ph = plan.mix_out2
            with turns(pe, ph.iters) as i:
                for g in range(2):
                    products(pe, ph, i, g, h_hi[:, A2 // P:, :], h_lo[:, A2 // P:, :],
                             ready="heads1" if g == 0 else None)
            pe.wait_ge(sem("normed"), 8)
            transpose_pe(pe, "norm3", x, KD, 5)
            for part, (g0, n) in enumerate(FFN_PARTS):
                ph = plan.up2[part]
                with turns(pe, ph.iters) as i:
                    for g in range(2):
                        products(pe, ph, i, g, h_hi, h_lo, transposed=True,
                                 ready="norm3" if g == 0 and part == 0 else None)
                ph = plan.down2[part]
                with turns(pe, ph.iters) as i:
                    for g in range(2):
                        products(pe, ph, i, g, hid_hi, hid_lo, hidden=(sem("hid2_lo"), g0 + 2, g))
            pe.wait_ge(sem("p_full"), 16)
            transpose_pe(pe, "ple", p_tok, 2)
            tile_ready(pe, "ple", 0)
            pe.wait_ge(sem("normed"), 10)
            transpose_pe(pe, "norm4", x, KD, 6)
            for g in range(0, len(plan.ple.groups), 2):
                products(pe, plan.ple, 0, g, h_hi, h_lo, ready="norm4" if g == 0 else None)
                products(pe, plan.ple, 0, g + 1, p_hi, p_lo)


_INS = ["x", "c", "positions", "w_ada", "b_ada", "g_pre_mix", "g_post_mix", "g_pre_ffn",
        "g_post_ffn", "w_in", "attn_sinks", "w_attn_proj", "hg_lower_bounds", "hg_norm",
        "w_hgrn_proj", "w_out", "w_ffn_in", "w_ffn_out", "p_2", "norm_mix_w_2", "w_in_2",
        "att_rel_bias_2", "w_gla_gate_up_2", "b_gla_gate_2", "gla_norm_w_2", "w_out_2",
        "norm_ffn_w_2", "w_ffn_up_2", "w_ffn_conv_2", "b_ffn_conv_2", "w_ffn_down_2",
        "norm_ple_w_2", "w_ple_gate_2", "w_ple_proj_2", "final_norm_w_2"]


def kernel(**inputs):
    import numpy as _np
    import concourse.bacc as _bacc
    from concourse import mybir as _mybir
    from concourse.bass_utils import run_bass_kernel_spmd as _run

    nc = _bacc.Bacc("TRN2", target_bir_lowering=False, num_devices=1, dynamic_dma_scratch_size=1024)
    arrays, args = {}, {}
    for name in _INS:
        a = _np.ascontiguousarray(inputs[name])
        arrays[f"in_{name}_dram"] = a
        args[name] = nc.dram_tensor(f"in_{name}_dram", a.shape, _mybir.dt.from_np(a.dtype),
                                    kind="ExternalInput").ap()
    out = nc.dram_tensor("out_0_dram", (1, TOK, D), F32, kind="ExternalOutput").ap()
    build_program(nc, args, out)
    r = _run(nc, [arrays], core_ids=[0])
    return r.results[0]["out_0_dram"]
```
